# Optimizing a Trainium2 kernel written in Bass

```python
import jax, jax.numpy as jnp
from jax import lax
import numpy as np

D_MODEL = 1024
BATCH = 1
SEQ = 256
DEPTH = 1

D_MIX = D_MODEL
N_MIXERS = 4
GROUP_W = D_MIX // N_MIXERS
HEAD_DIM = 64
N_HEADS_GROUP = GROUP_W // HEAD_DIM
QK_SCALE = HEAD_DIM ** -0.5
POOL_WINDOWS = (2, 4, 8, 16)
POOL_CH = GROUP_W // len(POOL_WINDOWS)
MAX_WINDOW = 16
RWKV_DECAY_LORA = 64
RWKV_A_LORA = 64
RWKV_GATE_LORA = 128
RWKV_COLS = 3 * GROUP_W + RWKV_DECAY_LORA + RWKV_A_LORA + RWKV_GATE_LORA
RWKV_GN_EPS = 64e-5
GLA_GATE_LORA = 16
GLA_GATE_TAU = 16.0
GLA_COLS = 4 * GROUP_W + GLA_GATE_LORA
CHUNK = 64
D_IN = GROUP_W + 4 * GROUP_W + RWKV_COLS + GLA_COLS
D_FF = 2816
NORM_EPS = 1e-6
GATE_FLOOR = 1e-30


def rms_norm(x, g, eps=NORM_EPS):
    xf = x.astype(jnp.float32)
    y = xf * lax.rsqrt(jnp.mean(xf * xf, axis=-1, keepdims=True) + eps)
    return (y * g.astype(jnp.float32)).astype(x.dtype)

def swiglu_ffn(x, w_in, w_out):
    gate, up = jnp.split(x @ w_in, 2, axis=-1)
    return (jax.nn.silu(gate) * up) @ w_out

def split_heads(t):
    return t.reshape(t.shape[:-1] + (N_HEADS_GROUP, HEAD_DIM))

def causal_multiscale_pool(p, w_pool, b_pool, scale):
    B, T, _ = p.shape
    cs = jnp.pad(jnp.cumsum(p, axis=1), ((0, 0), (MAX_WINDOW, 0), (0, 0)))
    pos = jnp.arange(T)
    pooled = []
    for gi, w in enumerate(POOL_WINDOWS):
        lo, hi = gi * POOL_CH, (gi + 1) * POOL_CH
        win_sum = cs[:, MAX_WINDOW:, lo:hi] - cs[:, MAX_WINDOW - w:MAX_WINDOW - w + T, lo:hi]
        count = jnp.minimum(pos + 1, w).astype(jnp.float32)[None, :, None]
        pooled.append(win_sum / count)
    pooled = jnp.stack(pooled, axis=2) - p.reshape(B, T, len(POOL_WINDOWS), POOL_CH)
    y = jnp.einsum('btgc,gcd->btgd', pooled, w_pool).reshape(B, T, GROUP_W) + b_pool
    return y * scale

def chunked_gated_linear_attention(q, k, v, log_a):
    B, T, H, K = q.shape
    V = v.shape[-1]
    n = T // CHUNK

    def to_chunks(t):
        return t.reshape(B, n, CHUNK, H, t.shape[-1]).transpose(1, 0, 3, 2, 4)

    causal = jnp.tril(jnp.ones((CHUNK, CHUNK), dtype=bool))[:, :, None]

    def step(S, inp):
        qc, kc, vc, gc = inp
        b = jnp.cumsum(gc, axis=-2)
        diff = b[:, :, :, None, :] - b[:, :, None, :, :]
        decay = jnp.where(causal, jnp.exp(jnp.where(causal, diff, 0.0)), 0.0)
        scores = jnp.einsum('bhtk,bhsk,bhtsk->bhts', qc, kc, decay)
        o = jnp.einsum('bhts,bhsv->bhtv', scores, vc) + jnp.einsum('bhtk,bhkv->bhtv', qc * jnp.exp(b), S)
        b_last = b[:, :, -1:, :]
        S_new = jnp.exp(b_last[:, :, 0, :])[..., None] * S + jnp.einsum('bhsk,bhsv->bhkv', kc * jnp.exp(b_last - b), vc)
        return S_new, o

    S0 = jnp.zeros((B, H, K, V), jnp.float32)
    _, o = lax.scan(step, S0, (to_chunks(q), to_chunks(k), to_chunks(v), to_chunks(log_a)))
    return o.transpose(1, 0, 3, 2, 4).reshape(B, T, H, V)

def rwkv7_scan(r, w, k, v, kk, a):
    B, T, H, N = r.shape

    def step(S, inp):
        r_t, w_t, k_t, v_t, kk_t, a_t = inp
        s_kk = jnp.einsum('bhvk,bhk->bhv', S, kk_t)
        S = (S * w_t[:, :, None, :] - s_kk[..., None] * (kk_t * a_t)[:, :, None, :]
             + v_t[..., :, None] * k_t[:, :, None, :])
        return S, jnp.einsum('bhvk,bhk->bhv', S, r_t)

    xs = tuple(jnp.moveaxis(t, 1, 0) for t in (r, w, k, v, kk, a))
    S0 = jnp.zeros((B, H, N, N), jnp.float32)
    _, out = lax.scan(step, S0, xs)
    return jnp.moveaxis(out, 0, 1)

def token_mixer(u, w_in, w_out, pool_w, pool_b, pool_scale, lb, hgrn_norm,
                rwkv_mu, rwkv_w0, rwkv_w2, rwkv_a0, rwkv_a2, rwkv_g2, rwkv_k_k, rwkv_k_a,
                rwkv_r_k, rwkv_ln_w, rwkv_ln_b, gla_w2, gla_b, gla_norm):
    B, T, _ = u.shape
    G = GROUP_W
    p = (u @ w_in).astype(jnp.float32)
    p_pool, p_hg, p_rw, p_gla = jnp.split(p, [G, 5 * G, 5 * G + RWKV_COLS], axis=-1)

    y_pool = causal_multiscale_pool(p_pool, pool_w, pool_b, pool_scale)

    hq, hf, hi, hg = jnp.split(p_hg, 4, axis=-1)
    f = lb + (1.0 - lb) * jax.nn.sigmoid(hf)
    log_f = jnp.log(jnp.maximum(f, GATE_FLOOR))
    o_h = chunked_gated_linear_attention(split_heads(jax.nn.silu(hq) * QK_SCALE),
                                         split_heads(1.0 - f),
                                         split_heads(hi), split_heads(log_f)).reshape(B, T, G)
    y_hgrn = rms_norm(o_h, hgrn_norm) * jax.nn.sigmoid(hg)

    prev = jnp.pad(p_rw, ((0, 0), (1, 0), (0, 0)))[:, :T]
    p_rw = p_rw + (prev - p_rw) * rwkv_mu
    rr, rk, rv, xw, xa, xg = jnp.split(
        p_rw, [G, 2 * G, 3 * G, 3 * G + RWKV_DECAY_LORA, 3 * G + RWKV_DECAY_LORA + RWKV_A_LORA], axis=-1)
    w_log = -jax.nn.softplus(-(rwkv_w0 + jnp.tanh(xw) @ rwkv_w2)) - 0.5
    decay = jnp.exp(-jnp.exp(w_log))
    a = jax.nn.sigmoid(rwkv_a0 + xa @ rwkv_a2)
    g_r = jax.nn.sigmoid(xg) @ rwkv_g2
    kk = split_heads(rk * rwkv_k_k)
    kk = kk / jnp.maximum(jnp.sqrt(jnp.sum(kk * kk, axis=-1, keepdims=True)), 1e-12)
    rk = rk * (1.0 + (a - 1.0) * rwkv_k_a)
    r_h, k_h, v_h = split_heads(rr), split_heads(rk), split_heads(rv)
    o_r = rwkv7_scan(r_h, split_heads(decay), k_h, v_h, kk, split_heads(a))
    mu = jnp.mean(o_r, axis=-1, keepdims=True)
    var = jnp.mean(jnp.square(o_r - mu), axis=-1, keepdims=True)
    gn = ((o_r - mu) * lax.rsqrt(var + RWKV_GN_EPS)).reshape(B, T, G) * rwkv_ln_w + rwkv_ln_b
    bonus = (jnp.sum(r_h * k_h * split_heads(rwkv_r_k), axis=-1, keepdims=True) * v_h).reshape(B, T, G)
    y_rwkv = (gn + bonus) * g_r

    gq, gk, gv, gg, ga = jnp.split(p_gla, [G, 2 * G, 3 * G, 4 * G], axis=-1)
    log_a = jax.nn.log_sigmoid(ga @ gla_w2 + gla_b) / GLA_GATE_TAU
    o_g = chunked_gated_linear_attention(split_heads(gq * QK_SCALE), split_heads(gk),
                                         split_heads(gv), split_heads(log_a))
    o_g = (o_g * lax.rsqrt(jnp.mean(o_g * o_g, axis=-1, keepdims=True) + NORM_EPS)).reshape(B, T, G)
    y_gla = o_g * gla_norm * jax.nn.silu(gg)

    y = jnp.concatenate([y_pool, y_hgrn, y_rwkv, y_gla], axis=-1).astype(u.dtype)
    return y @ w_out

def first_inputs(seed: int = 0) -> dict:
    key = jax.random.key(seed)
    ks = jax.random.split(key, 32)
    f32 = jnp.float32
    L, D, G = DEPTH, D_MODEL, GROUP_W

    def dense(k, shape, fan_in):
        return jax.random.normal(k, shape, f32) * fan_in ** -0.5

    def gain(k, shape):
        return 1.0 + 0.1 * jax.random.normal(k, shape, f32)

    def small(k, shape, s):
        return s * jax.random.normal(k, shape, f32)

    return {
        'x': jax.random.normal(ks[0], (BATCH, SEQ, D), f32),
        'norm_ffn1': gain(ks[1], (L, D)),
        'ffn1_w_in': dense(ks[2], (L, D, 2 * D_FF), D),
        'ffn1_w_out': dense(ks[3], (L, D_FF, D), D_FF),
        'norm_mix': gain(ks[4], (L, D)),
        'w_in': dense(ks[5], (L, D, D_IN), D),
        'w_out': dense(ks[6], (L, D_MIX, D), D_MIX),
        'pool_w': dense(ks[7], (L, len(POOL_WINDOWS), POOL_CH, POOL_CH), POOL_CH),
        'pool_b': small(ks[8], (L, G), 0.01),
        'pool_scale': gain(ks[9], (L, G)),
        'hgrn_lb_logits': small(ks[10], (L, G), 0.5),
        'hgrn_norm': gain(ks[11], (L, G)),
        'rwkv_mu': jax.random.uniform(ks[12], (L, RWKV_COLS), f32),
        'rwkv_w0': jax.random.uniform(ks[13], (L, G), f32, -4.0, 0.0),
        'rwkv_w2': dense(ks[14], (L, RWKV_DECAY_LORA, G), RWKV_DECAY_LORA),
        'rwkv_a0': small(ks[15], (L, G), 0.5),
        'rwkv_a2': dense(ks[16], (L, RWKV_A_LORA, G), RWKV_A_LORA),
        'rwkv_g2': dense(ks[17], (L, RWKV_GATE_LORA, G), RWKV_GATE_LORA),
        'rwkv_k_k': 0.85 + small(ks[18], (L, G), 0.1),
        'rwkv_k_a': gain(ks[19], (L, G)),
        'rwkv_r_k': small(ks[20], (L, G), 0.1),
        'rwkv_ln_w': gain(ks[21], (L, G)),
        'rwkv_ln_b': small(ks[22], (L, G), 0.01),
        'gla_w2': dense(ks[23], (L, GLA_GATE_LORA, G), GLA_GATE_LORA),
        'gla_b': small(ks[24], (L, G), 0.5),
        'gla_norm': gain(ks[25], (L, G)),
        'norm_ffn2': gain(ks[26], (L, D)),
        'ffn2_w_in': dense(ks[27], (L, D, 2 * D_FF), D),
        'ffn2_w_out': dense(ks[28], (L, D_FF, D), D_FF),
        'norm_final': gain(ks[29], (D,)),
    }

def first_block(x, norm_ffn1, ffn1_w_in, ffn1_w_out, norm_mix, w_in, w_out, pool_w, pool_b,
              pool_scale, hgrn_lb_logits, hgrn_norm, rwkv_mu, rwkv_w0, rwkv_w2, rwkv_a0, rwkv_a2,
              rwkv_g2, rwkv_k_k, rwkv_k_a, rwkv_r_k, rwkv_ln_w, rwkv_ln_b, gla_w2, gla_b, gla_norm,
              norm_ffn2, ffn2_w_in, ffn2_w_out, norm_final):
    sm = jax.nn.softmax(hgrn_lb_logits.astype(jnp.float32), axis=0)
    lower_bounds = jnp.cumsum(sm, axis=0) - sm[0]
    for l in range(DEPTH):
        x = x + 0.5 * swiglu_ffn(rms_norm(x, norm_ffn1[l]), ffn1_w_in[l], ffn1_w_out[l])
        x = x + token_mixer(rms_norm(x, norm_mix[l]), w_in[l], w_out[l], pool_w[l], pool_b[l],
                            pool_scale[l], lower_bounds[l], hgrn_norm[l], rwkv_mu[l], rwkv_w0[l],
                            rwkv_w2[l], rwkv_a0[l], rwkv_a2[l], rwkv_g2[l], rwkv_k_k[l], rwkv_k_a[l],
                            rwkv_r_k[l], rwkv_ln_w[l], rwkv_ln_b[l], gla_w2[l], gla_b[l], gla_norm[l])
        x = x + 0.5 * swiglu_ffn(rms_norm(x, norm_ffn2[l]), ffn2_w_in[l], ffn2_w_out[l])
    return rms_norm(x, norm_final)


DEPTH_2 = 2

GRID_W = 64
NA_HEADS = 16
NA_HEAD_DIM = D_MODEL // NA_HEADS
NA_WIN_H = 8
NA_WIN_W = 16
MLA_HEADS = 16
MLA_Q_LORA = D_MODEL // 4
MLA_KV_LORA = D_MODEL // 8
MLA_NOPE = 64
MLA_ROPE = 32
MLA_V = 64
ROPE_THETA = 10000.0
Q_BLOCK = 128
FFN_DIM = 2816
N_EXPERTS = 8
TOP_K = 2
EXPERT_DIM = 1792


def _rmsnorm(x):
    xf = x.astype(jnp.float32)
    y = xf * lax.rsqrt(jnp.mean(xf * xf, axis=-1, keepdims=True) + NORM_EPS)
    return y.astype(x.dtype)

def _modulate(x, shift, scale):
    return _rmsnorm(x) * (1 + scale[:, None, :]) + shift[:, None, :]

def _swiglu(h, w_gu, w_down):
    gate, up = jnp.split(h @ w_gu, 2, axis=-1)
    return (jax.nn.silu(gate) * up) @ w_down

def _rope_2d_tables(seq_len):
    t = jnp.arange(seq_len)
    row = (t // GRID_W).astype(jnp.float32)
    col = (t % GRID_W).astype(jnp.float32)
    n = MLA_ROPE // 4
    inv = ROPE_THETA ** (-jnp.arange(n, dtype=jnp.float32) / n)
    ang = jnp.concatenate([row[:, None] * inv, col[:, None] * inv], axis=-1)
    return jnp.cos(ang), jnp.sin(ang)

def _apply_rope(x, cos, sin):
    x1 = x[..., 0::2].astype(jnp.float32)
    x2 = x[..., 1::2].astype(jnp.float32)
    out = jnp.stack([x1 * cos - x2 * sin, x1 * sin + x2 * cos], axis=-1)
    return out.reshape(x.shape).astype(x.dtype)

def _neighborhood_attention(h, w_qkv, rpb, w_o):
    B, S, D = h.shape
    rows = S // GRID_W
    kh = min(NA_WIN_H, rows)
    kw = min(NA_WIN_W, GRID_W)
    qkv = (h @ w_qkv).reshape(B, rows, GRID_W, 3, NA_HEADS, NA_HEAD_DIM)
    q = qkv[:, :, :, 0] * (NA_HEAD_DIM ** -0.5)
    k = qkv[:, :, :, 1]
    v = qkv[:, :, :, 2]
    cols = jnp.arange(GRID_W)
    col_idx = jnp.clip(cols - kw // 2, 0, GRID_W - kw)[:, None] + jnp.arange(kw)[None, :]
    dc_idx = col_idx - cols[:, None] + NA_WIN_W - 1

    def row_block(r):
        rs = jnp.clip(r - kh // 2, 0, rows - kh)
        q_r = lax.dynamic_index_in_dim(q, r, axis=1, keepdims=False)
        k_g = lax.dynamic_slice_in_dim(k, rs, kh, axis=1)[:, :, col_idx]
        v_g = lax.dynamic_slice_in_dim(v, rs, kh, axis=1)[:, :, col_idx]
        dr_idx = rs + jnp.arange(kh) - r + NA_WIN_H - 1
        bias = rpb[:, dr_idx[None, :, None], dc_idx[:, None, :]]
        s = jnp.einsum('bqhd,bkqjhd->bhqkj', q_r, k_g).astype(jnp.float32) + bias.astype(jnp.float32)
        p = jax.nn.softmax(s.reshape(B, NA_HEADS, GRID_W, kh * kw), axis=-1)
        p = p.reshape(s.shape).astype(v.dtype)
        return jnp.einsum('bhqkj,bkqjhd->bqhd', p, v_g)

    o = lax.map(row_block, jnp.arange(rows))
    o = jnp.moveaxis(o, 0, 1).reshape(B, S, D)
    return o @ w_o

def _mla(h, w_down, q_norm, w_uq, kv_norm, w_ukv, w_o):
    B, S, D = h.shape
    down = h @ w_down
    c_q = _rmsnorm(down[..., :MLA_Q_LORA]) * q_norm
    c_kv = _rmsnorm(down[..., MLA_Q_LORA:MLA_Q_LORA + MLA_KV_LORA]) * kv_norm
    k_rope = down[..., MLA_Q_LORA + MLA_KV_LORA:]
    q = (c_q @ w_uq).reshape(B, S, MLA_HEADS, MLA_NOPE + MLA_ROPE)
    kv = (c_kv @ w_ukv).reshape(B, S, MLA_HEADS, MLA_NOPE + MLA_V)
    k_nope, v = kv[..., :MLA_NOPE], kv[..., MLA_NOPE:]
    cos, sin = _rope_2d_tables(S)
    q_nope = q[..., :MLA_NOPE]
    q_rope = _apply_rope(q[..., MLA_NOPE:], cos[:, None, :], sin[:, None, :])
    k_rope = _apply_rope(k_rope, cos, sin)
    scale = (MLA_NOPE + MLA_ROPE) ** -0.5
    nb = S // Q_BLOCK

    def to_blocks(t):
        return jnp.moveaxis(t.reshape(B, nb, Q_BLOCK, *t.shape[2:]), 1, 0)

    def q_block(blk):
        qn, qr = blk
        s = (jnp.einsum('bqhd,bkhd->bhqk', qn, k_nope)
             + jnp.einsum('bqhr,bkr->bhqk', qr, k_rope)).astype(jnp.float32) * scale
        p = jax.nn.softmax(s, axis=-1).astype(v.dtype)
        return jnp.einsum('bhqk,bkhd->bqhd', p, v)

    o = lax.map(q_block, (to_blocks(q_nope), to_blocks(q_rope)))
    o = jnp.moveaxis(o, 0, 1).reshape(B, S, MLA_HEADS * MLA_V)
    return o @ w_o

def _moe(h, w_router, w_gu, w_down):
    B, S, D = h.shape
    hf = h.reshape(B * S, D)
    probs = jax.nn.softmax((hf @ w_router).astype(jnp.float32), axis=-1)
    vals, idx = lax.top_k(probs, TOP_K)
    wts = vals / jnp.sum(vals, axis=-1, keepdims=True)
    combine = jnp.sum(jax.nn.one_hot(idx, N_EXPERTS, dtype=jnp.float32) * wts[..., None], axis=1)
    combine = combine.astype(h.dtype)
    y = jnp.zeros_like(hf)
    for e in range(N_EXPERTS):
        y = y + combine[:, e:e + 1] * _swiglu(hf, w_gu[e], w_down[e])
    return y.reshape(B, S, D)

def second_inputs(seed: int = 0) -> dict:
    key = jax.random.key(seed)
    ks = iter(jax.random.split(key, 32))
    n_even = (DEPTH_2 + 1) // 2
    n_odd = DEPTH_2 // 2
    D = D_MODEL

    def nrm(shape, fan_in, mult=1.0):
        return jax.random.normal(next(ks), shape, jnp.float32) * (mult * fan_in ** -0.5)

    return {
        "x": jax.random.normal(next(ks), (BATCH, SEQ, D), jnp.float32),
        "c": jax.random.normal(next(ks), (BATCH, D), jnp.float32),
        "w_ada": nrm((DEPTH_2, D, 6 * D), D, 0.5),
        "b_ada": 0.02 * jax.random.normal(next(ks), (DEPTH_2, 6 * D), jnp.float32),
        "na_w_qkv": nrm((n_even, D, 3 * D), D),
        "na_rpb": 0.1 * jax.random.normal(next(ks), (n_even, NA_HEADS, 2 * NA_WIN_H - 1, 2 * NA_WIN_W - 1), jnp.float32),
        "na_w_o": nrm((n_even, D, D), D),
        "ffn_w_gu": nrm((n_even, D, 2 * FFN_DIM), D),
        "ffn_w_down": nrm((n_even, FFN_DIM, D), FFN_DIM),
        "mla_w_down": nrm((n_odd, D, MLA_Q_LORA + MLA_KV_LORA + MLA_ROPE), D),
        "mla_q_norm": 1.0 + 0.01 * jax.random.normal(next(ks), (n_odd, MLA_Q_LORA), jnp.float32),
        "mla_w_uq": nrm((n_odd, MLA_Q_LORA, MLA_HEADS * (MLA_NOPE + MLA_ROPE)), MLA_Q_LORA),
        "mla_kv_norm": 1.0 + 0.01 * jax.random.normal(next(ks), (n_odd, MLA_KV_LORA), jnp.float32),
        "mla_w_ukv": nrm((n_odd, MLA_KV_LORA, MLA_HEADS * (MLA_NOPE + MLA_V)), MLA_KV_LORA),
        "mla_w_o": nrm((n_odd, MLA_HEADS * MLA_V, D), MLA_HEADS * MLA_V),
        "moe_w_router": nrm((n_odd, D, N_EXPERTS), D),
        "moe_w_gu": nrm((n_odd, N_EXPERTS, D, 2 * EXPERT_DIM), D),
        "moe_w_down": nrm((n_odd, N_EXPERTS, EXPERT_DIM, D), EXPERT_DIM),
        "final_norm": 1.0 + 0.01 * jax.random.normal(next(ks), (D,), jnp.float32),
    }

def second_block(x, c, w_ada, b_ada, na_w_qkv, na_rpb, na_w_o, ffn_w_gu, ffn_w_down,
              mla_w_down, mla_q_norm, mla_w_uq, mla_kv_norm, mla_w_ukv, mla_w_o,
              moe_w_router, moe_w_gu, moe_w_down, final_norm):
    c_act = jax.nn.silu(c)
    for i in range(DEPTH_2):
        j = i // 2
        mod = c_act @ w_ada[i] + b_ada[i]
        sh_a, sc_a, g_a, sh_f, sc_f, g_f = jnp.split(mod, 6, axis=-1)
        h = _modulate(x, sh_a, sc_a)
        if i % 2 == 0:
            m = _neighborhood_attention(h, na_w_qkv[j], na_rpb[j], na_w_o[j])
        else:
            m = _mla(h, mla_w_down[j], mla_q_norm[j], mla_w_uq[j], mla_kv_norm[j], mla_w_ukv[j], mla_w_o[j])
        x = x + g_a[:, None, :] * m
        h = _modulate(x, sh_f, sc_f)
        if i % 2 == 0:
            f = _swiglu(h, ffn_w_gu[j], ffn_w_down[j])
        else:
            f = _moe(h, moe_w_router[j], moe_w_gu[j], moe_w_down[j])
        x = x + g_f[:, None, :] * f
    return _rmsnorm(x) * final_norm


def setup_inputs(seed=0):
    out = dict(first_inputs(seed))
    for name, value in second_inputs(seed + 1).items():
        if name != "x":
            out[name + "_2"] = value
    return out


def reference(
    x, norm_ffn1, ffn1_w_in, ffn1_w_out, norm_mix, w_in, w_out, pool_w, pool_b, pool_scale,
    hgrn_lb_logits, hgrn_norm, rwkv_mu, rwkv_w0, rwkv_w2, rwkv_a0, rwkv_a2, rwkv_g2, rwkv_k_k,
    rwkv_k_a, rwkv_r_k, rwkv_ln_w, rwkv_ln_b, gla_w2, gla_b, gla_norm, norm_ffn2, ffn2_w_in,
    ffn2_w_out, norm_final, c_2, w_ada_2, b_ada_2, na_w_qkv_2, na_rpb_2, na_w_o_2, ffn_w_gu_2,
    ffn_w_down_2, mla_w_down_2, mla_q_norm_2, mla_w_uq_2, mla_kv_norm_2, mla_w_ukv_2, mla_w_o_2,
    moe_w_router_2, moe_w_gu_2, moe_w_down_2, final_norm_2,
):
    x = first_block(
        x, norm_ffn1, ffn1_w_in, ffn1_w_out, norm_mix, w_in, w_out, pool_w, pool_b, pool_scale,
        hgrn_lb_logits, hgrn_norm, rwkv_mu, rwkv_w0, rwkv_w2, rwkv_a0, rwkv_a2, rwkv_g2,
        rwkv_k_k, rwkv_k_a, rwkv_r_k, rwkv_ln_w, rwkv_ln_b, gla_w2, gla_b, gla_norm, norm_ffn2,
        ffn2_w_in, ffn2_w_out, norm_final,
    )
    return second_block(
        x, c_2, w_ada_2, b_ada_2, na_w_qkv_2, na_rpb_2, na_w_o_2, ffn_w_gu_2, ffn_w_down_2,
        mla_w_down_2, mla_q_norm_2, mla_w_uq_2, mla_kv_norm_2, mla_w_ukv_2, mla_w_o_2,
        moe_w_router_2, moe_w_gu_2, moe_w_down_2, final_norm_2,
    )


_drawn_inputs = setup_inputs


def setup_inputs(seed=0):
    import zlib

    import numpy as np

    out = dict(_drawn_inputs(seed))
    spreads = {}
    factors = {'pool_b': 6.183,
     'rwkv_k_k': 3.78,
     'rwkv_ln_b': 8.0,
     'na_rpb_2': 4.934,
     'mla_q_norm_2': 8.0,
     'mla_kv_norm_2': 8.0,
     'final_norm_2': 5.563}
    for name, (base, spread) in spreads.items():
        noise = np.random.default_rng([zlib.crc32(name.encode()), seed]).standard_normal(out[name].shape)
        drawn = base * np.exp(spread * noise) if base else spread * noise
        out[name] = __import__('jax').numpy.asarray(drawn.astype(out[name].dtype))
    for name, factor in factors.items():
        out[name] = (out[name] * factor).astype(out[name].dtype)
    return out
```

```python
from contextlib import ExitStack

import numpy as np
import concourse.bass as bass
from concourse import mybir

F32 = mybir.dt.float32
F32R = mybir.dt.float32r
BF16 = mybir.dt.bfloat16
U32 = mybir.dt.uint32
ALU = mybir.AluOpType
ACT = mybir.ActivationFunctionType
AX_X = mybir.AxisListType.X

P = 128
T = 256
D = 1024
KT = D // P
NB = T // P
CW = 256
CHUNK = KT * CW
FFN_UNITS = 2816 // CW
EXPERTS = 8
EXPERT_UNITS = 1792 // CW
G = 256
GT = G // P
HD = 64
MH = G // HD
RCHUNK = 64
NCH = T // RCHUNK
MIX_TILES = 26
GLA_LORA = 16
ADA_W = 384
ADA_UNITS = 2 * 6 * D // ADA_W
MODS = 6 * KT
AH = 16
GRID = 64
ROWS = T // GRID
WIN_H, WIN_W = 8, 16
QL, ROPE, QH = 256, 32, 96
EPS = 1e-6
QK_SCALE = HD ** -0.5
NEG = -1e30

VECTORS = [
    ("norm_ffn1", KT), ("norm_mix", KT), ("norm_ffn2", KT), ("norm_final", KT), ("pool_b", GT),
    ("pool_scale", GT), ("hgrn_lb_logits", GT), ("hgrn_norm", GT), ("rwkv_mu", 8), ("rwkv_w0", GT),
    ("rwkv_a0", GT), ("rwkv_k_k", GT), ("rwkv_k_a", GT), ("rwkv_r_k", GT), ("rwkv_ln_w", GT),
    ("rwkv_ln_b", GT), ("gla_b", GT), ("gla_norm", GT), ("c_2", KT), ("b_ada_2", 2 * MODS),
    ("mla_q_norm_2", GT), ("mla_kv_norm_2", 1), ("final_norm_2", KT),
]
NVEC = sum(n for _, n in VECTORS)
VEC = {}
for _name, _n in VECTORS:
    VEC[_name] = sum(VECTORS[i][1] for i in range(len(VEC)))


def shape_constants():
    s, t = np.arange(P)[:, None], np.arange(P)[None, :]
    main = {"ident": s == t, "ones": np.ones((P, P)), "headsum": s // HD == t // HD}
    same = s // RCHUNK == t // RCHUNK
    main["before"] = same & (s < t)
    main["upto"] = same & (s <= t)
    main["after"] = same & (s > t)
    for m in (1, 2, 4, 8, 16, 32, 64):
        pair = (s // (2 * m) == t // (2 * m)) & (s // m % 2 == 0) & (t // m % 2 == 1)
        main[f"level{m}"] = pair
        if m < RCHUNK:
            main[f"levelT{m}"] = pair.T
    w = np.array([2, 4, 8, 16])[(np.arange(GT)[None, :] * 2 + np.arange(P)[:, None] // 64)]
    count = np.minimum(np.arange(T)[None, None, :] + 1, w[:, :, None])
    main["invcount"] = (np.float32(1) / count.astype(np.float32)).reshape(P, GT * T)
    e = np.arange(EXPERTS)
    main["earlier"] = np.broadcast_to((e[None, :] < e[:, None]).reshape(1, -1), (P, EXPERTS * EXPERTS))
    main["chunkkeep"] = np.broadcast_to((np.arange(T) % RCHUNK != 0)[None, :], (P, T))
    q, k = GRID - 1 - np.arange(P)[:, None] % GRID, np.arange(GRID)[None, :]
    first = np.clip(q - WIN_W // 2, 0, GRID - WIN_W)
    attn = {"window": np.where((k >= first) & (k < first + WIN_W), 0.0, NEG)}
    n = ROPE // 4
    inv = (np.float32(10000.0) ** (-np.arange(n, dtype=np.float32) / np.float32(n))).astype(np.float32)
    pos = np.arange(T)
    ang = np.concatenate([(pos // GRID).astype(np.float32)[:, None] * inv,
                          (pos % GRID).astype(np.float32)[:, None] * inv], axis=-1).astype(np.float32)
    cos, sin = np.ones((P, T)), np.zeros((P, T))
    cos[HD:QH] = np.repeat(np.cos(ang), 2, axis=1).T
    sin[HD:QH] = np.repeat(np.sin(ang), 2, axis=1).T
    turn = np.zeros((P, P))
    for i in range(ROPE // 2):
        a, b = HD + 2 * i, HD + 2 * i + 1
        turn[b, a], turn[a, b] = -1.0, 1.0
    place, placeturn = np.zeros((P, P)), np.zeros((P, P))
    for i in range(ROPE):
        place[i, HD + i] = 1.0
        placeturn[i] = turn[HD + i]
    attn |= {"cos": cos, "sin": sin, "turn": turn, "place": place, "placeturn": placeturn}

    def pack(parts):
        at, where = 0, {}
        for name, a in parts.items():
            where[name] = (at, a.shape[1])
            at += a.shape[1]
        return np.ascontiguousarray(np.concatenate([a.astype(np.float32) for a in parts.values()], 1)), where

    return pack(main), pack(attn)


class Lane:

    def __init__(self, sem):
        self.sem, self.n, self.queue, self.seen = sem, 0, [], {}

    def mark(self):
        return (self.sem, self.n)

    def wait(self, *marks):
        for m in marks:
            if m is None:
                continue
            sem, value = m
            if value > 0 and self.seen.get(sem.name, 0) < value:
                self.seen[sem.name] = value
                self.queue.append(lambda e, s=sem, v=value: e.wait_ge(s, v))

    def step(self, make, *after):
        self.wait(*after)
        self.n += 1
        self.queue.append(lambda e: make(e).then_inc(self.sem, 1))
        return self.mark()

    def plain(self, make):
        self.queue.append(make)

    def loop(self, first, end, body):
        def run(e):
            with e.Fori(first, end) as i:
                body(e, i)
        if end - first > 1:
            self.queue.append(run)
        elif end > first:
            self.queue.append(lambda e: body(e, first))


def build_program(nc, a, out):
    (_, MAIN), (_, ATT) = shape_constants()
    stack = ExitStack()
    with stack:
        def sb(name, shape, dt=F32, ctx=stack):
            return ctx.enter_context(nc.sbuf_tensor("sb_" + name, shape, dt))

        def sem(name):
            return stack.enter_context(nc.semaphore(name))

        bank = [stack.enter_context(nc.psum_tensor(f"bank{i}", [P, 512], F32)) for i in range(8)]
        pe, act, dve, pool, sp = (Lane(sem("done_" + n)) for n in ("pe", "act", "dve", "pool", "sp"))

        raw = [sb(f"raw{s}", [P, CHUNK]) for s in range(3)]
        whi = [sb(f"whi{s}", [P, CHUNK], F32R) for s in range(3)]
        wlo = [sb(f"wlo{s}", [P, CHUNK], F32R) for s in range(3)]
        x = sb("x", [P, KT, T])
        xn = sb("xn", [P, KT, T])
        xhi = sb("xhi", [P, KT, T], F32R)
        xlo = sb("xlo", [P, KT, T], F32R)
        h = sb("h", [P, 2, T])
        hhi = sb("hhi", [P, 2, T], F32R)
        hlo = sb("hlo", [P, 2, T], F32R)
        sil = sb("sil", [P, 2, T])
        ada_raw = sb("ada_raw", [P, KT, ADA_W])
        ada_acc = sb("ada_acc", [P, ADA_W])
        cact = sb("cact", [P, KT])
        mod = sb("mod", [P, 2, MODS])
        cst = sb("cst", [P, sum(n for _, n in MAIN.values())])
        vec = sb("vec", [P, NVEC])
        rstd = sb("rstd", [P, 2, T])
        zero = sb("zero", [P, 512], BF16)

        def C(name, p0=0, p1=P):
            at, n = MAIN[name]
            return cst[p0:p1, at:at + n]

        def V(name, i=0, p0=0, p1=P):
            return vec[p0:p1, VEC[name] + i:VEC[name] + i + 1]

        ident, ones = C("ident"), C("ones")

        def dma(lane, dst, src, name, *after):
            s = sem("in_" + name)
            lane.wait(*after)
            lane.queue.append(lambda e: e.dma_start(dst, src).then_inc(s, 16))
            return (s, 16)

        def meet():
            marks = [l.mark() for l in (pe, act, dve, pool)]
            for l in (pe, act, dve, pool):
                l.wait(*marks)
            return marks

        got_x = dma(act, x[:, :, :], a["x"], "x")
        got_vec = dma(act, vec[:, :], a["vec"], "vec")
        got_cst = dma(act, cst[:, :], a["cst"], "cst")
        for l in (pe, act, dve, pool):
            l.wait(got_vec, got_cst)
        m_zero = pool.step(lambda e: e.memset(zero[:, :], 0.0))
        m_cact = act.step(lambda e: e.activation(cact[:, :], vec[:, VEC["c_2"]:VEC["c_2"] + KT], ACT.Silu), got_vec)
        dve.wait(m_cact)
        pe.wait(m_zero)

        s_raw = [sem(f"raw_landed{s}") for s in range(3)]
        s_hi = [sem(f"high_ready{s}") for s in range(3)]
        s_lo = [sem(f"low_ready{s}") for s in range(3)]
        s_used = [sem(f"weights_used{s}") for s in range(3)]
        uses = [0, 0, 0]
        for s in range(3):
            pe.plain(lambda e, s=s: e.sem_inc(s_used[s], 1))
            act.plain(lambda e, s=s: e.sem_inc(s_hi[s], 1))
            dve.plain(lambda e, s=s: e.sem_inc(s_lo[s], 1))

        def load(e, s, n, src):
            e.wait_ge(s_lo[s], n + 1)
            e.dma_start(raw[s][:, :], src).then_inc(s_raw[s], 16)

        def high(e, s, n):
            e.wait_ge(s_raw[s], 16 * n + 16)
            e.wait_ge(s_used[s], n + 1)
            e.activation(whi[s][:, :], raw[s][:, :], ACT.Copy).then_inc(s_hi[s], 1)

        def low(e, s, n):
            e.wait_ge(s_hi[s], n + 2)
            e.tensor_tensor(wlo[s][:, :], raw[s][:, :], whi[s][:, :], ALU.subtract).then_inc(s_lo[s], 1)

        def product(e, dst, w, x_parts, first, last, skip=False):
            (wh, wl), (xh, xl) = w, x_parts
            e.matmul(dst, wh, xh, start=first, stop=False, skip_group_check=skip)
            e.matmul(dst, wh, xl, start=False, stop=False, skip_group_check=skip)
            return e.matmul(dst, wl, xh, start=False, stop=last, skip_group_check=skip)

        def wtile(s, at):
            return whi[s][:, at:at + P], wlo[s][:, at:at + P]

        def square_sum(src, tiles, dst, *after):
            last = None
            for k in range(tiles):
                m = act.step(lambda e, k=k: e.activation(sil[:, k % 2, :], src(k), ACT.Square),
                             *after, pe.mark() if k < 2 else marks[k - 2])
                if k == 0:
                    marks = []
                marks.append(pe.step(lambda e, k=k: e.matmul(dst, ones, sil[:, k % 2, :],
                                                             start=k == 0, stop=k == tiles - 1), m))
            return marks[-1]

        def inv_root(dst, src, scale, eps, *after):
            m = dve.step(lambda e: e.tensor_scalar(dst, src, scale, eps, ALU.mult, ALU.add), *after)
            m = act.step(lambda e: e.activation(dst, dst, ACT.Sqrt), m)
            return dve.step(lambda e: e.reciprocal(dst, dst), m)

        def norm(gain, shift, *after):
            m = square_sum(lambda k: x[:, k, :], KT, bank[6][:, 0:T], *after)
            m_r = inv_root(rstd[:, 0, :], bank[6][:, 0:T], 1.0 / D, EPS, m)
            for k in range(KT):
                m = dve.step(lambda e, k=k: e.scalar_tensor_tensor(
                    xn[:, k, :], x[:, k, :], gain(k), rstd[:, 0, :], ALU.mult, ALU.mult), m_r)
                if shift is not None:
                    m = dve.step(lambda e, k=k: e.tensor_scalar_add(xn[:, k, :], xn[:, k, :], shift(k)), m)
                m = act.step(lambda e, k=k: e.activation(xhi[:, k, :], xn[:, k, :], ACT.Copy), m)
                m = dve.step(lambda e, k=k: e.tensor_tensor(xlo[:, k, :], xn[:, k, :], xhi[:, k, :],
                                                            ALU.subtract), m)
            return m

        def split_xn(m):
            for k in range(0, KT, 4):
                mh = act.step(lambda e, k=k: e.activation(xhi[:, k:k + 4, :], xn[:, k:k + 4, :], ACT.Copy), m)
                ml = dve.step(lambda e, k=k: e.tensor_tensor(xlo[:, k:k + 4, :], xn[:, k:k + 4, :],
                                                             xhi[:, k:k + 4, :], ALU.subtract), mh)
            return ml

        s_silu, s_mult, s_hhi, s_hlo = sem("silu_done"), sem("mult_done"), sem("h_high"), sem("h_low")
        s_ada_raw, s_ada, s_chain, s_adr = sem("ada_landed"), sem("ada_partial"), sem("ada_chain"), sem("ada_summed")
        s_ctmp = sem("h_before_weighting")
        for l, s in ((pe, s_adr), (dve, s_ada), (act, s_silu), (dve, s_mult), (dve, s_hlo)):
            l.plain(lambda e, s=s: e.sem_inc(s, 1))
        units_before = [0]
        GATE, UP, MODP = bank[4], bank[5], bank[7]
        A_, B_, C_ = 0, 1, 2

        def ffn(w, n, ada_first, ada_n, weight, ready, ada_after=None):
            u0 = units_before[0]
            units_before[0] += n
            b0 = list(uses)
            for s in range(3):
                uses[s] += n
            has_ada = lambda j: ada_n > 0 and (not isinstance(j, int) or j < ada_n)

            def sp_unit(e, j):
                load(e, A_, b0[A_] + j, w[j, 0])
                load(e, B_, b0[B_] + j, w[j, 1])
                if has_ada(j):
                    e.wait_ge(s_ada, ada_first + j + 1)
                    e.dma_start(ada_raw[:, :, :], a["ada"][ada_first + j]).then_inc(s_ada_raw, 16)
                load(e, C_, b0[C_] + j, w[j, 2])

            def a_hhi(e, j):
                e.wait_ge(s_mult, u0 + j + 2)
                e.wait_ge(s_used[C_], b0[C_] + j + 1)
                e.activation(hhi[:, :, :], h[:, :, :], ACT.Copy).then_inc(s_hhi, 1)

            def a_silu(e, j):
                e.wait_ge(s_used[A_], b0[A_] + j + 2)
                e.wait_ge(s_mult, u0 + j + 1)
                e.activation(sil[:, :, :], GATE[:, :], ACT.Silu).then_inc(s_silu, 1)

            def v_hlo(e, j):
                e.wait_ge(s_hhi, u0 + j + 1)
                e.tensor_tensor(hlo[:, :, :], h[:, :, :], hhi[:, :, :], ALU.subtract).then_inc(s_hlo, 1)

            def v_mult(e, j):
                e.wait_ge(s_used[B_], b0[B_] + j + 2)
                e.wait_ge(s_hlo, u0 + j + 1)
                e.wait_ge(s_silu, u0 + j + 2)
                if weight is None:
                    e.tensor_tensor(h[:, :, :], sil[:, :, :], UP[:, :], ALU.mult).then_inc(s_mult, 1)
                else:
                    e.tensor_tensor(h[:, :, :], sil[:, :, :], UP[:, :], ALU.mult).then_inc(s_ctmp, 1)
                    e.wait_ge(s_ctmp, j + 1)
                    e.tensor_tensor(h[:, :, :], h[:, :, :], weight(j), ALU.mult).then_inc(s_mult, 1)

            def v_ada(e, j):
                e.wait_ge(s_ada_raw, 16 * (ada_first + j) + 16)
                e.wait_ge(s_adr, ada_first + j + 1)
                c0 = (ada_first + j) * (KT - 1)
                e.tensor_scalar(ada_acc[:, :], ada_raw[:, 0, :], cact[:, 0:1], None, ALU.mult).then_inc(s_chain, 1)
                for k in range(1, KT):
                    e.wait_ge(s_chain, c0 + k)
                    e.scalar_tensor_tensor(ada_acc[:, :], ada_raw[:, k, :], cact[:, k:k + 1], ada_acc[:, :],
                                           ALU.mult, ALU.add).then_inc(s_ada if k == KT - 1 else s_chain, 1)

            def p_ada(e, j):
                e.wait_ge(s_ada, ada_first + j + 2)
                for i in range(ADA_W // P):
                    l = e.matmul(MODP[:, bass.ds((ada_first + j) * (ADA_W // P) + i, 1)],
                                 ada_acc[:, i * P:(i + 1) * P], ones[:, 0:1], start=True, stop=True)
                l.then_inc(s_adr, 1)

            def p_gate(e, j, s, dst, free_sem):
                e.wait_ge(s_lo[s], b0[s] + j + 2)
                e.wait_ge(free_sem, u0 + j + 1)
                for m in range(CW // P):
                    for k in range(KT):
                        l = product(e, dst[:, m * T:(m + 1) * T], wtile(s, k * CW + m * P),
                                    (xhi[:, k, :], xlo[:, k, :]), k == 0, k == KT - 1)
                l.then_inc(s_used[s], 1)

            def p_down(e, j):
                e.wait_ge(s_lo[C_], b0[C_] + j + 2)
                e.wait_ge(s_hlo, u0 + j + 2)
                for m in range(KT):
                    for k in range(2):
                        l = product(e, bank[m // 2][:, (m % 2) * T:(m % 2 + 1) * T],
                                    wtile(C_, k * D + m * P), (hhi[:, k, :], hlo[:, k, :]),
                                    False, False, skip=True)
                l.then_inc(s_used[C_], 1)

            def sp_body(e, j):
                sp_unit(e, j)

            def act_body(e, j, more=True):
                a_hhi(e, j - 1)
                high(e, C_, b0[C_] + j - 1)
                a_silu(e, j)
                if more:
                    high(e, A_, b0[A_] + j + 1)
                    high(e, B_, b0[B_] + j + 1)

            def dve_body(e, j, more=True):
                v_hlo(e, j - 1)
                low(e, C_, b0[C_] + j - 1)
                if has_ada(j):
                    v_ada(e, j)
                if more:
                    low(e, A_, b0[A_] + j + 1)
                v_mult(e, j)
                if more:
                    low(e, B_, b0[B_] + j + 1)

            def pe_body(e, j):
                p_gate(e, j, A_, GATE, s_silu)
                p_gate(e, j, B_, UP, s_mult)
                p_down(e, j - 1)
                if has_ada(j):
                    p_ada(e, j)

            sp.wait(ada_after)
            sp.plain(lambda e: sp_unit(e, 0))
            sp.loop(1, n - 1, sp_body)
            sp.plain(lambda e: sp_unit(e, n - 1))

            for j in (0, 1):
                act.plain(lambda e, j=j: high(e, A_, b0[A_] + j))
                act.plain(lambda e, j=j: high(e, B_, b0[B_] + j))
                if j == 0:
                    act.plain(lambda e: a_silu(e, 0))
            act.loop(1, n - 1, act_body)
            act.plain(lambda e: act_body(e, n - 1, False))
            act.plain(lambda e: a_hhi(e, n - 1))
            act.plain(lambda e: high(e, C_, b0[C_] + n - 1))

            dve.plain(lambda e: low(e, A_, b0[A_]))
            dve.plain(lambda e: low(e, B_, b0[B_]))
            if has_ada(0):
                dve.plain(lambda e: v_ada(e, 0))
            dve.plain(lambda e: low(e, A_, b0[A_] + 1))
            dve.plain(lambda e: v_mult(e, 0))
            dve.plain(lambda e: low(e, B_, b0[B_] + 1))
            dve.loop(1, n - 1, dve_body)
            dve.plain(lambda e: dve_body(e, n - 1, False))
            dve.plain(lambda e: v_hlo(e, n - 1))
            dve.plain(lambda e: low(e, C_, b0[C_] + n - 1))

            pe.wait(*ready)
            for b in range(4):
                pe.plain(lambda e, b=b: e.matmul(bank[b][:, :], zero[:, 0:P], zero[:, :], start=True, stop=False,
                                                 skip_group_check=True))
            pe.plain(lambda e: p_gate(e, 0, A_, GATE, s_silu))
            pe.plain(lambda e: p_gate(e, 0, B_, UP, s_mult))
            if has_ada(0):
                pe.plain(lambda e: p_ada(e, 0))
            pe.loop(1, n - 1, pe_body)
            pe.plain(lambda e: pe_body(e, n - 1))
            pe.plain(lambda e: p_down(e, n - 1))
            for b in range(4):
                m = pe.step(lambda e, b=b: e.matmul(bank[b][:, :], zero[:, 0:P], zero[:, :], start=False,
                                                    stop=True, skip_group_check=True))
            return m

        def linear(w, n, operand, evac, ready, form="channels"):
            marks, done = [], []
            for c in range(n):
                s = c % 3
                nth = uses[s]
                uses[s] += 1
                sp.plain(lambda e, s=s, nth=nth, c=c: load(e, s, nth, w[c]))
                act.plain(lambda e, s=s, nth=nth: high(e, s, nth))
                dve.plain(lambda e, s=s, nth=nth: low(e, s, nth))
                dst = bank[4 + s]
                pe.wait(*ready, (s_lo[s], nth + 2), marks[c - 3] if c >= 3 else None)

                def run(e, s=s, dst=dst):
                    for m in range(2):
                        for k in range(KT):
                            if form == "channels":
                                o = dst[:, m * T:(m + 1) * T]
                                l = product(e, o, wtile(s, k * CW + m * P), (xhi[:, k, :], xlo[:, k, :]),
                                            k == 0, k == KT - 1)
                            else:
                                o = dst[:, m * CW:(m + 1) * CW]
                                wh, wl = (z[s][:, k * CW:(k + 1) * CW] for z in (whi, wlo))
                                xh, xl = (z[:, k, m * P:(m + 1) * P] for z in (xhi, xlo))
                                l = product(e, o, (xh, xl), (wh, wl), k == 0, k == KT - 1)
                    l.then_inc(s_used[s], 1)

                pe.plain(run)
                done.append((s_used[s], nth + 2))
                if c >= 2:
                    marks.append(evac(c - 2, bank[4 + (c - 2) % 3], done[c - 2]))
            for c in range(max(n - 2, 0), n):
                marks.append(evac(c, bank[4 + c % 3], done[c]))
            return marks

        def add_half(m):
            for b in range(4):
                r = dve.step(lambda e, b=b: e.scalar_tensor_tensor(
                    x[:, 2 * b:2 * b + 2, :], bank[b][:, :].rearrange("p (k t) -> p k t", k=2), 0.5,
                    x[:, 2 * b:2 * b + 2, :], ALU.mult, ALU.add), m)
            return r

        def add_gated(gate, m):
            for k in range(KT):
                r = dve.step(lambda e, k=k: e.scalar_tensor_tensor(
                    x[:, k, :], bank[k // 2][:, (k % 2) * T:(k % 2 + 1) * T], gate(k), x[:, k, :],
                    ALU.mult, ALU.add), m)
            return r

        def add_chunks(gate):
            def evac(c, b, m):
                for i in range(2):
                    k = 2 * c + i
                    src = b[:, i * T:(i + 1) * T]
                    if gate is None:
                        r = dve.step(lambda e, k=k, src=src: e.tensor_tensor(x[:, k, :], src, x[:, k, :], ALU.add), m)
                    else:
                        r = dve.step(lambda e, k=k, src=src: e.scalar_tensor_tensor(
                            x[:, k, :], src, gate(k), x[:, k, :], ALU.mult, ALU.add), m)
                return r
            return evac

        env = dict(locals())
        m = norm(lambda k: V("norm_ffn1", k), None, got_x)
        m = ffn(a["ffn1"], FFN_UNITS, 0, FFN_UNITS, None, [m])
        m = add_half(m)
        m = norm(lambda k: V("norm_mix", k), None, m)
        m = token_mixer(env, m)
        m = norm(lambda k: V("norm_ffn2", k), None, m)
        m = ffn(a["ffn2"], FFN_UNITS, FFN_UNITS, FFN_UNITS, None, [m], m)
        m = add_half(m)
        mm = square_sum(lambda k: x[:, k, :], KT, bank[6][:, 0:T], m)
        mm = inv_root(rstd[:, 0, :], bank[6][:, 0:T], 1.0 / D, EPS, mm)
        for k in range(KT):
            m = dve.step(lambda e, k=k: e.scalar_tensor_tensor(x[:, k, :], x[:, k, :], V("norm_final", k),
                                                               rstd[:, 0, :], ALU.mult, ALU.mult), mm)

        def take_mod(layer, pieces):
            mt = dve.step(lambda e: e.tensor_tensor(mod[:, layer, :], MODP[:, layer * MODS:(layer + 1) * MODS],
                                                    vec[:, VEC["b_ada_2"] + layer * MODS:VEC["b_ada_2"] + (layer + 1) * MODS],
                                                    ALU.add), (s_adr, pieces + 1))
            for part in (1, 4):
                sl = mod[:, layer, part * KT:(part + 1) * KT]
                mt = dve.step(lambda e, sl=sl: e.tensor_scalar_add(sl, sl, 1.0), mt)
            return mt

        def M(layer, part):
            return lambda k: mod[:, layer, part * KT + k:part * KT + k + 1]

        mt = take_mod(0, 2 * FFN_UNITS)
        m = norm(M(0, 1), M(0, 0), m, mt)
        m = neighbourhood(env, M(0, 2), m)
        m = norm(M(0, 4), M(0, 3), m)
        m = ffn(a["ffn3"], FFN_UNITS, 2 * FFN_UNITS, ADA_UNITS - 2 * FFN_UNITS, None, [m])
        m = add_gated(M(0, 5), m)
        mt = take_mod(1, ADA_UNITS)
        m = norm(M(1, 1), M(1, 0), m, mt)
        m = latent(env, M(1, 2), m)
        m = norm(M(1, 4), M(1, 3), m)
        with ExitStack() as ctx:
            comb, m = router(env, ctx, m)
            m = ffn(a["moe"], EXPERTS * EXPERT_UNITS, 0, 0,
                    lambda j: comb[:, bass.ds(j // EXPERT_UNITS, 1), :].broadcast_to([P, 2, T])
                    if not isinstance(j, int) else
                    comb[:, j // EXPERT_UNITS:j // EXPERT_UNITS + 1, :].broadcast_to([P, 2, T]), [m])
        m = add_gated(M(1, 5), m)
        mm = square_sum(lambda k: x[:, k, :], KT, bank[6][:, 0:T], m)
        mm = inv_root(rstd[:, 0, :], bank[6][:, 0:T], 1.0 / D, EPS, mm)
        for k in range(KT):
            m = dve.step(lambda e, k=k: e.scalar_tensor_tensor(xn[:, k, :], x[:, k, :], V("final_norm_2", k),
                                                               rstd[:, 0, :], ALU.mult, ALU.mult), mm)
        stored = dma(sp, out, xn[:, :, :], "stored", m)
        sp.wait(stored)

        with nc.Block() as block:
            for lane, attach in ((sp, block.sync), (act, block.scalar), (dve, block.vector),
                                 (pe, block.tensor), (pool, block.gpsimd)):
                def run(e, lane=lane):
                    for item in lane.queue:
                        item(e)
                attach(run)


def token_mixer(env, m_in):
    a, sb, bank, pe, act, dve, pool = (env[n] for n in ("a", "sb", "bank", "pe", "act", "dve", "pool"))
    C, V, ident, ones, dma, meet = (env[n] for n in ("C", "V", "ident", "ones", "dma", "meet"))
    linear, square_sum, inv_root, rstd, y = (env[n] for n in ("linear", "square_sum", "inv_root", "rstd", "xn"))
    with ExitStack() as outer:
        meet()
        p = sb("p", [P, MIX_TILES, T], ctx=outer)
        tok = sb("tok", [P, NB, T], ctx=outer)
        lora = sb("lora", [P, 2, G], ctx=outer)
        g2 = sb("g2", [P, G], ctx=outer)
        gw2 = sb("gw2", [GLA_LORA, G], ctx=outer)
        wga = sb("wga", [P, KT, GLA_LORA], ctx=outer)
        ga = sb("ga", [GLA_LORA, T], ctx=outer)
        wp = sb("wp", [P, GT, P], ctx=outer)
        m_z = pool.step(lambda e: e.memset(lora[:, :, :], 0.0))
        m_zp = pool.step(lambda e: e.memset(wp[:, :, :], 0.0))
        w_lora = [dma(act, lora[0:64, 0, :], a["rwkv_w2"], "rwkv_w2", m_z),
                  dma(act, lora[64:128, 1, :], a["rwkv_a2"], "rwkv_a2", m_z),
                  dma(act, g2[:, :], a["rwkv_g2"], "rwkv_g2"),
                  dma(act, gw2[:, :], a["gla_w2"], "gla_w2"),
                  dma(act, wga[:, :, :], a["w_in_ga"], "w_in_ga")]
        w_pool = [dma(act, wp[i % 2 * 64:i % 2 * 64 + 64, i // 2, i % 2 * 64:i % 2 * 64 + 64],
                      a["pool_w"][i], f"pool_w{i}", m_zp) for i in range(4)]

        def evac(c, b, m):
            dst = p[:, 2 * c:2 * c + 2, :]
            src = b[:, :].rearrange("p (k t) -> p k t", k=2)
            if c % 2:
                return act.step(lambda e: e.activation(dst, src, ACT.Copy), m)
            return dve.step(lambda e: e.tensor_copy(dst, src), m)

        em = linear(a["w_in"], MIX_TILES // 2, None, evac, [m_in])
        for k in range(KT):
            mga = pe.step(lambda e, k=k: e.matmul(bank[3][0:GLA_LORA, 0:T], wga[:, k, :], y[:, k, :],
                                                  start=k == 0, stop=k == KT - 1), w_lora[4], m_in)
        mga = act.step(lambda e: e.activation(ga[:, :], bank[3][0:GLA_LORA, 0:T], ACT.Copy), mga)
        meet()
        ready = list(em) + [mga]
        for l in (pe, act, dve, pool):
            l.wait(*ready, *w_lora, *w_pool)

        def TT(lane, o, i0, i1, op, *after):
            return lane.step(lambda e: e.tensor_tensor(o, i0, i1, op), *after)

        def TS(lane, o, i0, s1, s2, op0, op1, *after):
            if op1 is None:
                return lane.step(lambda e: e.tensor_scalar(o, i0, s1, None, op0), *after)
            return lane.step(lambda e: e.tensor_scalar(o, i0, s1, s2, op0, op1), *after)

        def STT(o, i0, s, i1, op0, op1, *after):
            return dve.step(lambda e: e.scalar_tensor_tensor(o, i0, s, i1, op0, op1), *after)

        def AC(o, i, f, *after, bias=None, scale=None):
            kw = {}
            if bias is not None:
                kw["bias"] = bias
            if scale is not None:
                kw["scale"] = scale
            return act.step(lambda e: e.activation(o, i, f, **kw), *after)

        def MM(o, l, r, start, stop, *after):
            return pe.step(lambda e: e.matmul(o, l, r, start=start, stop=stop), *after)

        def to_tokens(src, dst, b, *after):
            for i in range(GT):
                for blk in range(NB):
                    o = bank[b][:, blk * T + i * P:blk * T + (i + 1) * P]
                    m = pe.step(lambda e, o=o, i=i, blk=blk: e.transpose(o, src[:, i, blk * P:(blk + 1) * P], ident),
                                *after)
            return dve.step(lambda e: e.tensor_copy(dst, bank[b][:, :].rearrange("p (b c) -> p b c", b=NB)), m)

        with ExitStack() as c1:
            pad = 16
            wb = [sb(f"win{i}", [P, GT, pad + T], ctx=c1) for i in range(3)]
            m = pool.step(lambda e: e.memset(wb[0][:, :, 0:pad], 0.0))
            m1 = pool.step(lambda e: e.memset(wb[1][:, :, 0:pad], 0.0))
            m2 = pool.step(lambda e: e.memset(wb[2][:, :, 0:pad], 0.0))
            m = pool.step(lambda e: e.tensor_copy(wb[0][:, :, pad:], p[:, 0:2, :]), m)
            icn = C("invcount").rearrange("p (k t) -> p k t", k=GT)
            pooled = p[:, 0:2, :]
            cur, takes = 0, []
            for i, w in enumerate((1, 2, 4, 8)):
                nxt = 1 + i % 2 if i < 2 else (1 if i == 2 else 2)
                src, dst = wb[cur], wb[nxt]
                m = TT(pool, dst[:, :, pad:], src[:, :, pad:], src[:, :, pad - w:pad - w + T], ALU.add, m, m1, m2, *takes)
                tile, half = i // 2, i % 2 * 64
                takes.append(TT(pool, pooled[half:half + 64, tile, :], dst[half:half + 64, tile, pad:],
                                icn[half:half + 64, tile, :], ALU.mult, m))
                cur = nxt
            m = TT(pool, pooled, pooled, wb[0][:, :, pad:], ALU.subtract, *takes)
            for i in range(GT):
                m = MM(bank[7 - 1][:, i * T:(i + 1) * T], wp[:, i, :], p[:, i, :], True, True, m)
            for i in range(GT):
                m = TS(dve, p[:, i, :], bank[6][:, i * T:(i + 1) * T], V("pool_b", i), V("pool_scale", i),
                       ALU.add, ALU.mult, m)
            m_pool = m
            meet()

        def gated_attention(q, k, g, vt, dst, *after):
            with ExitStack() as c2:
                b = sb(f"cum{len(names)}", [P, GT, T], ctx=c2)
                ex = [sb(f"ex{i}{len(names)}", [P, GT * T], ctx=c2) for i in range(2)]
                sc = sb(f"sc{len(names)}", [P, MH, 3, P], ctx=c2)
                names.append(0)
                m_sc = pool.step(lambda e: e.memset(sc[:, :, :, :], 0.0))
                for i in range(GT):
                    mb = dve.step(lambda e, i=i: e.tensor_tensor_scan(
                        b[:, i, :], unit[:, :], g[:, i, :], 0.0, ALU.mult, ALU.add), *after)
                mv = to_tokens(vt, tok[:, :, :], 5, *after)
                bf = b[:, :, :].rearrange("p k t -> p (k t)")
                qf, kf = (z.rearrange("p k t -> p (k t)") for z in (q, k))
                m_pe = {0: None, 1: None}
                m_cp = {0: None, 1: None}
                levels = [0, 1, 2, 4, 8, 16, 32, 64, 128]
                for n, w in enumerate(levels):
                    e_, pair = ex[n % 2], n % 2
                    if w:
                        v3 = lambda z, w=w: z.rearrange("p (n j) -> p n j", j=2 * w)
                        mid = v3(bf)[:, :, w - 1:w].broadcast_to([P, GT * T // (2 * w), w])
                        lo, hi = (lambda z, w=w: v3(z, w)[:, :, 0:w]), (lambda z, w=w: v3(z, w)[:, :, w:2 * w])
                        m1 = TT(dve, hi(e_[:, :]), hi(bf), mid, ALU.subtract, mb, m_pe[pair])
                        m2 = TT(dve, lo(e_[:, :]), mid, lo(bf), ALU.subtract, mb, m_pe[pair])
                        m3 = AC(e_[:, :], e_[:, :], ACT.Exp, m1, m2)
                        m4 = TT(pool, hi(e_[:, :]), hi(e_[:, :]), hi(qf), ALU.mult, m3, *after)
                        m5 = TT(dve, lo(e_[:, :]), lo(e_[:, :]), lo(kf), ALU.mult, m3, *after)
                        kk_, qq_ = e_[:, :], e_[:, :]
                        wait = (m4, m5)
                    else:
                        kk_, qq_, wait = kf, qf, tuple(after)
                    for hh in range(MH):
                        hp, ti = hh % 2 * HD, hh // 2 * T
                        bk = bank[2 * pair + hh % 2]
                        if w < P:
                            for blk in range(NB):
                                o = bk[:, (hh // 2) * T + blk * P:(hh // 2) * T + (blk + 1) * P]
                                mm = MM(o, kk_[hp:hp + HD, ti + blk * P:ti + (blk + 1) * P],
                                        qq_[hp:hp + HD, ti + blk * P:ti + (blk + 1) * P], True, True,
                                        *wait, m_cp[pair])
                        else:
                            o = bk[:, (hh // 2) * P:(hh // 2 + 1) * P]
                            mm = MM(o, kk_[hp:hp + HD, ti:ti + P], qq_[hp:hp + HD, ti + P:ti + 2 * P],
                                    True, True, *wait, m_cp[pair])
                    m_pe[pair] = mm
                    for hb in range(2):
                        bk = bank[2 * pair + hb]
                        if w < P:
                            mask = (C(f"level{w}") if w else ident).bitcast(U32)
                            for hh in range(2):
                                src = bk[:, hh * T:(hh + 1) * T].rearrange("p (b t) -> p b t", b=NB)
                                ms = dve.step(lambda e, hb=hb, hh=hh, src=src, mask=mask: e.copy_predicated(
                                    sc[:, 2 * hh + hb, 0:3:2, :],
                                    mask.rearrange("p (b t) -> p b t", b=1).broadcast_to([P, NB, P]), src), mm, m_sc)
                        else:
                            src = bk[:, 0:2 * P].rearrange("p (h t) -> p h t", h=2)
                            ms = dve.step(lambda e, hb=hb, src=src: e.tensor_copy(
                                sc[:, hb:MH:2, 1, :], src), mm, m_sc)
                    m_cp[pair] = ms
                for hh in range(MH):
                    hp, ti = hh % 2 * HD, hh // 2
                    lh = lambda blk, hh=hh: tok[:, blk, hh * HD:(hh + 1) * HD]
                    MM(bank[5][hp:hp + HD, ti * T:(ti + 1) * T], lh(0),
                       sc[:, hh, 0:2, :].rearrange("p b t -> p (b t)"), True, False, ms, mv)
                    mo = MM(bank[5][hp:hp + HD, ti * T + P:(ti + 1) * T], lh(1), sc[:, hh, 2, :], False, True, ms)
                md = AC(dst, bank[5][:, :].rearrange("p (k t) -> p k t", k=2), ACT.Copy, mo)
                meet()
            return md

        names = []
        unit = outer.enter_context(env["nc"].sbuf_tensor("sb_unit", [P, T], F32))
        dve.wait(pool.step(lambda e: e.memset(unit[:, :], 1.0)))
        gate = sb("gate", [P, GT, T], ctx=outer)
        tmp = sb("tmp", [P, GT, T], ctx=outer)

        def ln_floor(dst, src, *after):
            big = float(2 ** 64)
            m1 = TS(dve, tmp[:, :, :], src, float(2.0 ** -50), big, ALU.is_lt, ALU.mult, *after)
            m2 = STT(src, tmp[:, :, :], 1.0, src, ALU.max, ALU.mult, m1)
            m3 = AC(dst, src, ACT.Ln, m2)
            return STT(dst, tmp[:, :, :], float(-64 * np.log(2.0) / big), dst, ALU.mult, ALU.add, m3)

        lbs = sb("lbs", [P, 6], ctx=outer)
        lg = env["vec"][:, VEC["hgrn_lb_logits"]:VEC["hgrn_lb_logits"] + GT]
        m0 = TT(dve, lbs[:, 0:2], lg, lg, ALU.subtract)
        m0 = AC(lbs[:, 0:2], lbs[:, 0:2], ACT.Exp, m0)
        m1 = dve.step(lambda e: e.reciprocal(lbs[:, 2:4], lbs[:, 0:2]), m0)
        m1 = TT(dve, lbs[:, 0:2], lbs[:, 0:2], lbs[:, 2:4], ALU.mult, m1)
        m1 = TT(dve, lbs[:, 4:6], lbs[:, 0:2], lbs[:, 0:2], ALU.subtract, m1)
        mlb = TS(dve, lbs[:, 2:4], lbs[:, 4:6], -1.0, 1.0, ALU.mult, ALU.add, m1)
        hq, hf, hi_, hg = (p[:, 2 * i:2 * i + 2, :] for i in (1, 2, 3, 4))
        mq = AC(hq, hq, ACT.Silu)
        mq = TS(dve, hq, hq, QK_SCALE, None, ALU.mult, None, mq)
        mf = AC(hf, hf, ACT.Sigmoid)
        for i in range(GT):
            mf = TS(dve, hf[:, i, :], hf[:, i, :], lbs[:, 2 + i:3 + i], lbs[:, 4 + i:5 + i], ALU.mult, ALU.add, mf, mlb)
        m1 = TS(dve, gate[:, :, :], hf, 1e-30, None, ALU.max, None, mf)
        mk = TS(dve, hf, hf, -1.0, 1.0, ALU.mult, ALU.add, m1)
        mg = ln_floor(gate[:, :, :], gate[:, :, :], m1)
        mhg = AC(hg, hg, ACT.Sigmoid)
        mo = gated_attention(hq, hf, gate[:, :, :], hi_, hq, mq, mk, mg)
        ms = square_sum(lambda k: hq[:, k, :], GT, bank[6][:, 0:T], mo)
        mr = inv_root(rstd[:, 0, :], bank[6][:, 0:T], 1.0 / G, EPS, ms)
        for i in range(GT):
            m1 = STT(hq[:, i, :], hq[:, i, :], V("hgrn_norm", i), rstd[:, 0, :], ALU.mult, ALU.mult, mr)
            m_hgrn = TT(dve, hq[:, i, :], hq[:, i, :], hg[:, i, :], ALU.mult, m1, mhg)

        def head_rstd(dst, src, scale, eps, *after):
            m = AC(tmp[:, :, :], src, ACT.Square, *after)
            for i in range(GT):
                m2 = MM(bank[6][:, i * T:(i + 1) * T], C("headsum"), tmp[:, i, :], True, True, m)
            return inv_root(dst, bank[6][:, :].rearrange("p (k t) -> p k t", k=2), scale, eps, m2)

        meet()
        gq, gk, gv, gg = (p[:, 18 + 2 * i:20 + 2 * i, :] for i in range(4))
        for i in range(GT):
            m1 = MM(bank[4][:, i * T:(i + 1) * T], gw2[:, i * P:(i + 1) * P], ga[:, :], True, True)
        for i in range(GT):
            m2 = TS(dve, gate[:, i, :], bank[4][:, i * T:(i + 1) * T], V("gla_b", i), None, ALU.add, None, m1)
        m3 = STT(tmp[:, :, :], gate[:, :, :], -1.0, gate[:, :, :], ALU.mult, ALU.min, m2)
        m4 = AC(tmp[:, :, :], tmp[:, :, :], ACT.Exp, m3)
        m4 = AC(tmp[:, :, :], tmp[:, :, :], ACT.Ln, m4, bias=1.0)
        m5 = STT(gate[:, :, :], gate[:, :, :], 0.0, tmp[:, :, :], ALU.min, ALU.subtract, m4)
        mg = TS(dve, gate[:, :, :], gate[:, :, :], 1.0 / 16.0, None, ALU.mult, None, m5)
        mq = TS(dve, gq, gq, QK_SCALE, None, ALU.mult, None)
        mgg = AC(gg, gg, ACT.Silu)
        mo = gated_attention(gq, gk, gate[:, :, :], gv, gq, mq, mg)
        mr = head_rstd(rstd[:, :, :], gq, 1.0 / HD, EPS, mo)
        for i in range(GT):
            m1 = STT(gq[:, i, :], gq[:, i, :], V("gla_norm", i), rstd[:, i, :], ALU.mult, ALU.mult, mr)
            m_gla = TT(dve, gq[:, i, :], gq[:, i, :], gg[:, i, :], ALU.mult, m1, mgg)
        meet()

        with ExitStack() as c3:
            rw = p[:, 10:18, :]
            cum = sb("rcum", [P, GT, T], ctx=c3)
            av = sb("rwkv_a", [P, GT, T], ctx=c3)
            bb = sb("rwkv_b", [P, GT, T], ctx=c3)
            qr = sb("qr", [P, GT, 2, T], ctx=c3)
            kp, bp, wi = (p[:, i:i + 2, :] for i in (20, 22, 24))
            sh = y[:, :, :]
            m1 = TT(dve, sh[:, :, 1:], rw[:, :, 0:T - 1], rw[:, :, 1:], ALU.subtract)
            m2 = TS(dve, sh[:, :, 0:1], rw[:, :, 0:1], -1.0, None, ALU.mult, None)
            for i in range(8):
                m3 = STT(rw[:, i, :], sh[:, i, :], V("rwkv_mu", i), rw[:, i, :], ALU.mult, ALU.add, m1, m2)
            r, k, v = (rw[:, 2 * i:2 * i + 2, :] for i in range(3))
            lo_in = rw[:, 6, :]
            m4 = AC(lo_in[0:64, :], lo_in[0:64, :], ACT.Tanh, m3)
            m5 = AC(rw[:, 7, :], rw[:, 7, :], ACT.Sigmoid, m3)
            for i in range(GT):
                m6 = MM(bank[0][:, i * T:(i + 1) * T], lora[:, 0, i * P:(i + 1) * P], lo_in, True, True, m4)
                m7 = MM(bank[1][:, i * T:(i + 1) * T], lora[:, 1, i * P:(i + 1) * P], lo_in, True, True, m4)
                m8 = MM(bank[2][:, i * T:(i + 1) * T], g2[:, i * P:(i + 1) * P], rw[:, 7, :], True, True, m5)
            for i in range(GT):
                m6 = AC(cum[:, i, :], bank[0][:, i * T:(i + 1) * T], ACT.Sigmoid, m6, bias=V("rwkv_w0", i))
                m7 = AC(av[:, i, :], bank[1][:, i * T:(i + 1) * T], ACT.Sigmoid, m7, bias=V("rwkv_a0", i))
            md = TS(dve, gate[:, :, :], cum[:, :, :], -float(np.exp(-0.5)), None, ALU.mult, None, m6)
            for i in range(GT):
                mc = dve.step(lambda e, i=i: e.tensor_tensor_scan(cum[:, i, :], C("chunkkeep"), gate[:, i, :], 0.0,
                                                                  ALU.mult, ALU.add), md)
            m_g = AC(y[:, 4:6, :], bank[2][:, :].rearrange("p (k t) -> p k t", k=2), ACT.Copy, m8, m3)
            for i in range(GT):
                m1 = TS(dve, bb[:, i, :], k[:, i, :], V("rwkv_k_k", i), None, ALU.mult, None, m3)
            m1 = AC(tmp[:, :, :], bb[:, :, :], ACT.Square, m1)
            for i in range(GT):
                m2 = MM(bank[6][:, i * T:(i + 1) * T], C("headsum"), tmp[:, i, :], True, True, m1)
            m2 = AC(rstd[:, :, :], bank[6][:, :].rearrange("p (k t) -> p k t", k=2), ACT.Sqrt, m2)
            m2 = TS(dve, rstd[:, :, :], rstd[:, :, :], 1e-12, None, ALU.max, None, m2)
            m2 = dve.step(lambda e: e.reciprocal(rstd[:, :, :], rstd[:, :, :]), m2)
            mkk = TT(dve, bb[:, :, :], bb[:, :, :], rstd[:, :, :], ALU.mult, m2)
            m1 = TS(dve, tmp[:, :, :], av[:, :, :], -1.0, None, ALU.add, None, m7, m2)
            for i in range(GT):
                m2 = TS(dve, tmp[:, i, :], tmp[:, i, :], V("rwkv_k_a", i), 1.0, ALU.mult, ALU.add, m1)
            mk = TT(dve, k, k, tmp[:, :, :], ALU.mult, m2)
            m1 = TT(dve, wi[:, :, :], cum[:, :, :], gate[:, :, :], ALU.subtract, mc)
            m1 = AC(wi[:, :, :], wi[:, :, :], ACT.Exp, m1)
            mq1 = TT(dve, qr[:, :, 0, :], bb[:, :, :], wi[:, :, :], ALU.mult, m1, mkk)
            mb = TT(dve, bb[:, :, :], bb[:, :, :], av[:, :, :], ALU.mult, mq1)
            m2 = AC(wi[:, :, :], cum[:, :, :], ACT.Exp, mq1)
            mq2 = TT(dve, qr[:, :, 1, :], r, wi[:, :, :], ALU.mult, m2)
            m3_ = AC(av[:, :, :], cum[:, :, :], ACT.Exp, mb, mc, scale=-1.0)
            mkp = TT(dve, kp[:, :, :], k, av[:, :, :], ALU.mult, m3_, mk)
            mbp = TT(dve, bp[:, :, :], bb[:, :, :], av[:, :, :], ALU.mult, m3_)
            c4 = cum[:, :, :].rearrange("p k (c t) -> p (k c) t", t=RCHUNK)
            g4 = gate[:, :, :].rearrange("p k (c t) -> p (k c) t", t=RCHUNK)
            end = c4[:, :, RCHUNK - 1:RCHUNK].broadcast_to([P, GT * NCH, RCHUNK])
            m1 = TT(dve, g4, end, c4, ALU.subtract, mc, mq1)
            m1 = AC(gate[:, :, :], gate[:, :, :], ACT.Exp, m1)
            kc, bc = y[:, 0:2, :], y[:, 2:4, :]
            mkc = TT(dve, kc, k, gate[:, :, :], ALU.mult, m1, mk)
            mbc = TT(dve, bc, bb[:, :, :], gate[:, :, :], ALU.mult, m1, mb)
            m1 = TT(dve, tmp[:, :, :], r, k, ALU.mult, mk)
            for i in range(GT):
                m2 = TS(dve, tmp[:, i, :], tmp[:, i, :], V("rwkv_r_k", i), None, ALU.mult, None, m1)
            for i in range(GT):
                m3_ = MM(bank[6][:, i * T:(i + 1) * T], C("headsum"), tmp[:, i, :], True, True, m2)
            m_bonus = TT(dve, r, bank[6][:, :].rearrange("p (k t) -> p k t", k=2), v, ALU.mult, m3_, mq2)

            kkt, kct, bct = (p[:, i:i + 2, :] for i in (4, 6, 8))
            mt = [to_tokens(qr[:, :, 0, :], kkt[:, :, :], 3, mq1),
                  to_tokens(kc, kct[:, :, :], 4, mkc),
                  to_tokens(bc, bct[:, :, :], 5, mbc),
                  to_tokens(v, tok[:, :, :], 6, m3, m_bonus)]
            meet()
            names4 = ("akt", "art", "abt", "arbt", "ab", "inv", "invt", "xx")
            spare = env["ada_raw"][:, :, :].rearrange("p k n -> p (k n)").rearrange("p (i n t) -> p i n t", n=4, t=P)
            akt, art, abt, arbt, ab, inv = (spare[:, i] for i in range(6))
            invt, xx = (sb("r_" + n, [P, 4, P], ctx=c3)[:, :, :] for n in names4[6:])
            yy = sb("yy", [P, 4, P], ctx=c3)
            st = sb("st", [P, NCH, HD], ctx=c3)
            mc_ = sb("mc", [P, NCH, HD], ctx=c3)
            qq = sb("qq", [P, T], ctx=c3)
            oo = sb("oo", [P, GT, T], ctx=c3)

            def bc4(z):
                return z.rearrange("p (n t) -> p n t", n=1).broadcast_to([P, 4, P])

            def b3(i):
                return bank[i][:, :].rearrange("p (n t) -> p n t", n=4)

            probs = [(hh, blk) for hh in range(2) for blk in range(NB)]
            for ti in range(GT):
                def hs(hh):
                    return slice(hh * HD, (hh + 1) * HD)
                m = [None]
                for n, (hh, blk) in enumerate(probs):
                    if n == 2:
                        pe.wait(m[-1])
                    ts = slice(blk * P, (blk + 1) * P)
                    s_ = slice(n * P, (n + 1) * P)
                    kk_c, r_c = qr[hs(hh), ti, 0, ts], qr[hs(hh), ti, 1, ts]
                    kp_c, bp_c = kp[hs(hh), ti, ts], bp[hs(hh), ti, ts]
                    m = [MM(bank[0][:, s_], bp_c, kk_c, True, True),
                         MM(bank[1][:, s_], kk_c, bp_c, True, True),
                         MM(bank[2][:, s_], kp_c, kk_c, True, True),
                         MM(bank[3][:, s_], kp_c, r_c, True, True),
                         MM(bank[4][:, s_], bp_c, r_c, True, True)]
                m_abt = TT(dve, abt[:, :, :], b3(0), bc4(C("before")), ALU.mult, m[-1])
                m_ab = TT(dve, ab[:, :, :], b3(1), bc4(C("after")), ALU.mult, m[-1])
                m_akt = TT(dve, akt[:, :, :], b3(2), bc4(C("before")), ALU.mult, m[-1])
                m_art = TT(dve, art[:, :, :], b3(3), bc4(C("upto")), ALU.mult, m[-1])
                m_arb = TT(dve, arbt[:, :, :], b3(4), bc4(C("upto")), ALU.mult, m[-1])
                for n, (hh, blk) in enumerate(probs):
                    mz = MM(bank[5][:, n * HD:(n + 1) * HD], akt[:, n, :],
                            tok[:, blk, ti * P + hh * HD:ti * P + (hh + 1) * HD], True, True, m_akt)
                m1 = TT(pool, xx[:, :, :], ab[:, :, :], bc4(C("levelT1")), ALU.mult, m_ab)
                m1 = TT(pool, inv[:, :, :], bc4(ident), xx[:, :, :], ALU.subtract, m1)
                m2 = TT(pool, xx[:, :, :], abt[:, :, :], bc4(C("level1")), ALU.mult, m_abt, m1)
                m2 = TT(pool, invt[:, :, :], bc4(ident), xx[:, :, :], ALU.subtract, m2)
                m_i, m_it, m_free = m1, m2, m2
                lev = {}
                for w in (2, 4, 8, 16, 32):
                    if w == 2:
                        ml = TT(pool, akt[:, :, :], abt[:, :, :], bc4(C("level2")), ALU.mult, m_abt, mz)
                    for n in range(4):
                        mx = MM(bank[0][:, n * P:(n + 1) * P], akt[:, n, :], inv[:, n, :], True, True, ml, m_i, m_abt)
                    if w < 32:
                        ml = TT(pool, akt[:, :, :], abt[:, :, :], bc4(C(f"level{2 * w}")), ALU.mult, mx)
                    mx = AC(xx[:, :, :], b3(0), ACT.Copy, mx, m_it)
                    for n in range(4):
                        ma = MM(bank[1][:, n * P:(n + 1) * P], invt[:, n, :], xx[:, n, :], True, True, mx, m_it, m_ab)
                    for n in range(4):
                        mb_ = MM(bank[2][:, n * P:(n + 1) * P], xx[:, n, :], invt[:, n, :], True, True, mx, m_it, m_akt)
                    m_i = TT(dve, inv[:, :, :], inv[:, :, :], b3(1), ALU.subtract, ma)
                    m_it = TT(dve, invt[:, :, :], invt[:, :, :], b3(2), ALU.subtract, mb_)
                for n, (hh, blk) in enumerate(probs):
                    cs = slice(ti * P + hh * HD, ti * P + (hh + 1) * HD)
                    m1 = dve.step(lambda e, n=n, blk=blk, cs=cs: e.tensor_copy(xx[:, n, 0:HD], kkt[:, blk, cs]), mb_)
                    m2 = dve.step(lambda e, n=n: e.tensor_copy(xx[:, n, HD:P], bank[5][:, n * HD:(n + 1) * HD]), mz, mb_)
                for n in range(4):
                    m3_ = MM(bank[0][:, n * P:(n + 1) * P], invt[:, n, :], xx[:, n, :], True, True, m2, m_it)
                my = TS(dve, yy[:, :, :], b3(0), -1.0, None, ALU.mult, None, m3_)
                for n, (hh, blk) in enumerate(probs):
                    ts = slice(blk * P, (blk + 1) * P)
                    vs = tok[:, blk, ti * P + hh * HD:ti * P + (hh + 1) * HD]
                    mq_ = MM(bank[1][hs(hh), ts], yy[:, n, 0:HD], arbt[:, n, :], True, True, my, m_i)
                    MM(bank[2][hs(hh), ts], yy[:, n, HD:P], arbt[:, n, :], True, False, my, m_it)
                    mo_ = MM(bank[2][hs(hh), ts], vs, art[:, n, :], False, True)
                mqq = TT(dve, qq[:, :], bank[1][:, 0:T], qr[:, ti, 1, :], ALU.add, mq_)
                for c in (0, 2, 1):
                    if c == 1:
                        pe.wait(m2)
                    for hh in range(2):
                        blk, rs = c // 2, slice(c % 2 * 64, c % 2 * 64 + 64)
                        n = hh * NB + blk
                        cs = slice(ti * P + hh * HD, ti * P + (hh + 1) * HD)
                        o1 = bank[3][hs(hh), c * HD:(c + 1) * HD]
                        o2 = bank[4][hs(hh), c * HD:(c + 1) * HD]
                        m1 = MM(o1, yy[rs, n, 0:HD], bct[rs, blk, cs], True, True, my)
                        MM(o2, kct[rs, blk, cs], tok[rs, blk, cs], True, False)
                        m2 = MM(o2, bct[rs, blk, cs], yy[rs, n, HD:P], False, True)
                for c in range(NCH - 1):
                    for hh in range(2):
                        e0 = c * RCHUNK + RCHUNK - 1
                        m3_ = STT(mc_[hs(hh), c, :], C("ident")[hs(hh), hh * HD:(hh + 1) * HD],
                                  wi[hs(hh), ti, e0:e0 + 1], bank[3][hs(hh), c * HD:(c + 1) * HD],
                                  ALU.mult, ALU.add, m1)
                ms_ = dve.step(lambda e: e.tensor_copy(
                    st[:, 1:, :], bank[4][:, 0:(NCH - 1) * HD].rearrange("p (c v) -> p c v", v=HD)), m2)
                for c in (1, 2):
                    for hh in range(2):
                        mm_ = MM(bank[0][hs(hh), c * HD:(c + 1) * HD], mc_[hs(hh), c, :], st[hs(hh), c, :],
                                 True, True, ms_, m3_, my)
                    ms_ = TT(dve, st[:, c + 1, :], bank[0][:, c * HD:(c + 1) * HD], st[:, c + 1, :], ALU.add, mm_)
                for c in range(1, NCH):
                    for hh in range(2):
                        mm_ = MM(bank[6][hs(hh), c * RCHUNK:(c + 1) * RCHUNK], st[hs(hh), c, :],
                                 qq[hs(hh), c * RCHUNK:(c + 1) * RCHUNK], True, True, ms_, mqq)
                m1 = AC(oo[:, ti, :], bank[2][:, 0:T], ACT.Copy, mo_)
                m2 = TT(dve, oo[:, ti, RCHUNK:], bank[6][:, RCHUNK:T], oo[:, ti, RCHUNK:], ALU.add, m1, mm_)
                meet()

            for i in range(GT):
                m1 = MM(bank[0][:, i * T:(i + 1) * T], C("headsum"), oo[:, i, :], True, True, m2)
            m1 = STT(oo[:, :, :], bank[0][:, :].rearrange("p (k t) -> p k t", k=2), -1.0 / HD, oo[:, :, :],
                     ALU.mult, ALU.add, m1)
            mr = head_rstd(rstd[:, :, :], oo[:, :, :], 1.0 / HD, 64e-5, m1)
            for i in range(GT):
                m1 = STT(oo[:, i, :], oo[:, i, :], V("rwkv_ln_w", i), rstd[:, i, :], ALU.mult, ALU.mult, mr)
                m1 = STT(oo[:, i, :], oo[:, i, :], V("rwkv_ln_b", i), r[:, i, :], ALU.add, ALU.add, m1)
                m_rwkv = TT(dve, r[:, i, :], oo[:, i, :], y[:, 4 + i, :], ALU.mult, m1)
            meet()

        for j, t0 in enumerate((0, 2, 10, 18)):
            m = dve.step(lambda e, j=j, t0=t0: e.tensor_copy(y[:, 2 * j:2 * j + 2, :], p[:, t0:t0 + 2, :]))
        m = env["split_xn"](m)
        m = linear(a["w_out"], 4, None, env["add_chunks"](None), [m])
        meet()
    return m[-1]


def backwards(ap):
    step, n = ap.ap[-1]
    return bass.AP(tensor=ap.tensor, offset=ap.offset + step * (n - 1), ap=[*ap.ap[:-1], [-step, n]])


def attend(env, ctx, tag, scores, values, scale, bias, m_ready, order=None):
    sb, bank, pe, act, dve, pool = (env[n] for n in ("sb", "bank", "pe", "act", "dve", "pool"))
    ident, y = env["ident"], env["xn"]
    s = [env["h"], env["sil"], sb(f"s2_{tag}", [P, NB, T], ctx=ctx)]
    pt = [env["rstd"], sb(f"pt_{tag}", [P, NB, T], ctx=ctx)]
    mx = sb(f"mx_{tag}", [P, AH, 4], ctx=ctx)
    m_exp, m_nrm, m_pv, m_tr, m_out = {}, {}, {}, {}, {}
    m_sread, m_tread = {}, {}

    def softmax(i):
        sb_, bk = s[i % 3], bank[i % 2]
        for q in range(NB):
            m = pe.step(lambda e, q=q: e.matmul(bk[:, q * T:(q + 1) * T], *scores(i, q), start=True, stop=True),
                        *m_ready, m_sread.get(i - 2))
        if bias is not None:
            for q in range(NB):
                m1 = dve.step(lambda e, q=q: e.tensor_tensor_reduce(
                    sb_[:, q, :], bk[:, q * T:(q + 1) * T], bias[:, q, i, :], 1.0, -3e38, ALU.add, ALU.max,
                    mx[:, i, q:q + 1]), m, m_tr.get(i - 3))
            src = sb_[:, :, :]
        else:
            src = bk[:, :].rearrange("p (q t) -> p q t", q=NB)
            m1 = dve.step(lambda e: e.reduce_max(mx[:, i, 0:2], src, AX_X), m)
        m1 = dve.step(lambda e: e.tensor_scalar(mx[:, i, 0:2], mx[:, i, 0:2], -scale, None, ALU.mult), m1)
        m_sread[i] = m1
        for q in range(NB):
            m2 = act.step(lambda e, q=q: e.activation(sb_[:, q, :], src[:, q, :], ACT.Exp, bias=mx[:, i, q:q + 1],
                                                      scale=scale, accum_out=mx[:, i, 2 + q:3 + q]),
                          m1, m_tr.get(i - 3))
        if bias is None:
            m_sread[i] = m2
        m3 = dve.step(lambda e: e.reciprocal(mx[:, i, 2:4], mx[:, i, 2:4]), m2)
        for q in range(NB):
            m3 = pool.step(lambda e, q=q: e.tensor_scalar(sb_[:, q, :], sb_[:, q, :], mx[:, i, 2 + q:3 + q], None,
                                                          ALU.mult), m3)
        m_nrm[i] = m3

    def transposed(i):
        bk = bank[2 + i % 2]
        for kb in range(NB):
            for q in range(NB):
                m = pe.step(lambda e, kb=kb, q=q: e.transpose(bk[:, kb * T + q * P:kb * T + (q + 1) * P],
                                                              s[i % 3][:, q, kb * P:(kb + 1) * P], ident),
                            m_nrm[i], m_tread.get(i - 2))
        m_tr[i] = m
        m_tread[i] = dve.step(lambda e: e.tensor_copy(pt[i % 2][:, :, :], bk[:, :].rearrange("p (k q) -> p k q", k=NB)),
                              m, m_pv.get(i - 2))

    def weigh(i):
        hp, bk = i % 2 * HD, bank[4 + i // 2 % 2]
        for kb in range(NB):
            m = pe.step(lambda e, kb=kb: e.matmul(bk[hp:hp + HD, 0:T], values(i, kb), pt[i % 2][:, kb, :],
                                                  start=kb == 0, stop=kb == NB - 1), m_tread[i], m_out.get(i // 2 - 2))
        m_pv[i] = m
        if i % 2:
            dst, src = y[:, i // 2, :], bk[:, 0:T]
            if order is not None:
                dst, src = order(dst), src.rearrange("p (r c) -> p r c", c=GRID)
            m_out[i // 2] = act.step(lambda e: e.activation(dst, src, ACT.Copy), m)

    for i in range(AH + 2):
        if i < AH:
            softmax(i)
        if 0 <= i - 1 < AH:
            transposed(i - 1)
        if 0 <= i - 2 < AH:
            weigh(i - 2)
    return m_out[AH // 2 - 1]


def neighbourhood(env, gate, m_in):
    a, sb, bank, act, dve, pool = (env[n] for n in ("a", "sb", "bank", "act", "dve", "pool"))
    dma, meet, linear = (env[n] for n in ("dma", "meet", "linear"))
    assert ROWS <= WIN_H
    (_, _), (_, att) = shape_constants()
    with ExitStack() as ctx:
        marks = meet()
        q = sb("na_q", [P, 8, T], ctx=ctx)
        k = sb("na_k", [P, 8, T], ctx=ctx)
        v = sb("na_v", [P, NB, D], ctx=ctx)
        bias = sb("na_bias", [P, NB, AH, ROWS, GRID], ctx=ctx)
        win = sb("na_win", [P, GRID], ctx=ctx)
        rpb = a["rpb"]
        width = 2 * GRID - 1
        got = []
        for qr in range(ROWS):
            for kr in range(ROWS):
                src = bass.AP(tensor=rpb.tensor, offset=rpb.offset + (WIN_H - 1 + kr - qr) * width,
                              ap=[[1, GRID], [(2 * WIN_H - 1) * width, AH], [1, GRID]])
                got.append(dma(act, bias[qr % 2 * GRID:(qr % 2 + 1) * GRID, qr // 2, :, kr, :], src,
                               f"bias{qr}{kr}", *marks))
        at = att["window"][0]
        got.append(dma(act, win[:, :], a["att"][:, at:at + GRID], "window", *marks))
        for b in range(NB):
            for j in range(AH):
                m_b = pool.step(lambda e, b=b, j=j: e.tensor_tensor(
                    bias[:, b, j], bias[:, b, j],
                    win[:, :].rearrange("p (r c) -> p r c", r=1).broadcast_to([P, ROWS, GRID]), ALU.add), *got)

        def evac_qk(c, b, m):
            dst = (q if c < 4 else k)[:, 2 * (c % 4):2 * (c % 4) + 2, :]
            src = b[:, :].rearrange("p (k t) -> p k t", k=2)
            if c < 4:
                dst, src = backwards(dst.rearrange("p k (r c) -> p (k r) c", c=GRID)), \
                    src.rearrange("p k (r c) -> p (k r) c", c=GRID)
            return dve.step(lambda e: e.tensor_scalar(dst, src, QK_SCALE if c < 4 else 1.0, None, ALU.mult), m)

        def evac_v(c, b, m):
            dst = v[:, :, c * CW:(c + 1) * CW]
            return act.step(lambda e: e.activation(dst, b[:, :].rearrange("p (b n) -> p b n", b=NB), ACT.Copy), m)

        m1 = linear(a["na_qk"], 8, None, evac_qk, [m_in])
        m2 = linear(a["na_v"], 4, None, evac_v, [m_in] + m1, form="tokens")
        meet()

        def scores(i, qb):
            hp = i % 2 * HD
            return q[hp:hp + HD, i // 2, qb * P:(qb + 1) * P], k[hp:hp + HD, i // 2, :]

        m = attend(env, ctx, "na", scores, lambda i, kb: v[:, kb, i * HD:(i + 1) * HD], 1.0,
                   bias[:, :, :, :, :].rearrange("p b h r c -> p b h (r c)"), [*m1, *m2, m_b],
                   lambda z: backwards(z.rearrange("p (r c) -> p r c", c=GRID)))
        m = env["split_xn"](m)
        m = linear(a["na_o"], 4, None, env["add_chunks"](gate), [m])
        meet()
    return m[-1]


def latent(env, gate, m_in):
    a, sb, bank, pe, act, dve, pool = (env[n] for n in ("a", "sb", "bank", "pe", "act", "dve", "pool"))
    dma, meet, linear, V, y = (env[n] for n in ("dma", "meet", "linear", "V", "xn"))
    square_sum, inv_root, rstd = (env[n] for n in ("square_sum", "inv_root", "rstd"))
    (_, _), (_, att) = shape_constants()
    with ExitStack() as ctx:
        marks = meet()
        tab = sb("tab", [P, sum(n for _, n in att.values())], ctx=ctx)
        wukv = sb("wukv", [P, AH * 2 * HD], ctx=ctx)
        v = sb("mla_v", [P, NB, D], ctx=ctx)
        lat = sb("lat", [P, 3, T], ctx=ctx)
        kr = sb("kr", [P, T], ctx=ctx)
        wuq = env["ada_raw"][:, :, :].rearrange("p k n -> p (k n)").rearrange("p (k n) -> p k n", k=2)
        got = [dma(act, tab[:, :], a["att"], "tab", *marks), dma(act, wuq, a["mla_uq"], "uq", *marks),
               dma(act, wukv[:, :], a["mla_ukv"], "ukv", *marks)]

        def A(name, n=None, p0=0, p1=P):
            at, w = att[name]
            return tab[p0:p1, at:at + (n or w)]

        rp = slice(HD, QH)
        with ExitStack() as c1:
            wd = sb("wd", [P, KT, QL + P + ROPE], ctx=c1)
            gd = dma(act, wd[:, :, :], a["mla_down"], "down", *marks)
            outs = [(bank[0][:, 0:T], 0, P), (bank[0][:, T:2 * T], P, P), (bank[1][:, 0:T], 2 * P, P),
                    (bank[2][0:ROPE, 0:T], 3 * P, ROPE)]
            for o, at, n in outs:
                for k_ in range(KT):
                    m = pe.step(lambda e, o=o, at=at, n=n, k_=k_: e.matmul(
                        o, wd[:, k_, at:at + n], y[:, k_, :], start=k_ == 0, stop=k_ == KT - 1), gd, m_in)
            m1 = act.step(lambda e: e.activation(lat[:, 0:2, :], bank[0][:, :].rearrange("p (k t) -> p k t", k=2),
                                                 ACT.Copy), m)
            m2 = act.step(lambda e: e.activation(lat[:, 2, :], bank[1][:, 0:T], ACT.Copy), m)
            m3 = dve.step(lambda e: e.tensor_copy(kr[0:ROPE, :], bank[2][0:ROPE, 0:T]), m)
            meet()
        for l in (pe, dve, act, pool):
            l.wait(*got)
        ms = square_sum(lambda k_: lat[:, k_, :], 2, bank[3][:, 0:T], m1)
        mr = inv_root(rstd[:, 0, :], bank[3][:, 0:T], 1.0 / QL, EPS, ms)
        for i in range(2):
            m_cq = dve.step(lambda e, i=i: e.scalar_tensor_tensor(lat[:, i, :], lat[:, i, :], V("mla_q_norm_2", i),
                                                                  rstd[:, 0, :], ALU.mult, ALU.mult), mr)
        ms = square_sum(lambda k_: lat[:, 2, :], 1, bank[3][:, T:2 * T], m2, mr)
        mr = inv_root(rstd[:, 1, :], bank[3][:, T:2 * T], 1.0 / P, EPS, ms)
        m_ckv = dve.step(lambda e: e.scalar_tensor_tensor(lat[:, 2, :], lat[:, 2, :], V("mla_kv_norm_2"),
                                                          rstd[:, 1, :], ALU.mult, ALU.mult), mr)
        q = sb("mla_q", [P, AH, T], ctx=ctx)
        k = sb("mla_k", [P, AH, T], ctx=ctx)
        pe.step(lambda e: e.matmul(bank[2][0:QH, 0:T], A("place", QH, 0, ROPE), kr[0:ROPE, :], start=True, stop=True), m3)
        m = pe.step(lambda e: e.matmul(bank[2][0:QH, T:2 * T], A("placeturn", QH, 0, ROPE), kr[0:ROPE, :],
                                       start=True, stop=True))
        m1 = dve.step(lambda e: e.tensor_tensor(kr[rp, :], bank[2][rp, 0:T], A("cos", None, HD, QH), ALU.mult), m)
        m2 = dve.step(lambda e: e.tensor_tensor(k[rp, 0, :], bank[2][rp, T:2 * T], A("sin", None, HD, QH), ALU.mult), m)
        m1 = dve.step(lambda e: e.tensor_tensor(kr[rp, :], kr[rp, :], k[rp, 0, :], ALU.add), m1, m2)
        m_kr = pool.step(lambda e: e.tensor_copy(k[rp, :, :], kr[rp, :].rearrange("p (n t) -> p n t", n=1)
                                                 .broadcast_to([ROPE, AH, T])), m1)
        vcols = wukv[:, :].rearrange("p (h n) -> p h n", n=2 * HD)
        prev = []
        for b in range(NB):
            for hf in range(2):
                bk = bank[4 + hf]
                m = pe.step(lambda e, b=b, hf=hf, bk=bk: e.matmul(
                    bk[:, :], lat[:, 2, b * P:(b + 1) * P], vcols[:, 8 * hf:8 * hf + 8, HD:2 * HD],
                    start=True, stop=True), m_ckv, *prev)
                m_v = act.step(lambda e, b=b, hf=hf, bk=bk: e.activation(v[:, b, hf * 512:(hf + 1) * 512], bk[:, :],
                                                                         ACT.Copy), m)
                if hf:
                    prev = [m_v]
        mk_, mq_, mt_ = {}, {}, {}
        meet()
        for i in range(AH // 2):
            kb, qb, tb = bank[0 + i % 2], bank[2 + i % 2], bank[4 + i % 2]
            for j in range(2):
                hh = 2 * i + j
                m = pe.step(lambda e, hh=hh, j=j, kb=kb: e.matmul(
                    kb[0:HD, j * T:(j + 1) * T], vcols[:, hh, 0:HD], lat[:, 2, :], start=True, stop=True), mk_.get(i - 2))
            mk_[i] = act.step(lambda e, i=i, kb=kb: e.activation(
                k[0:HD, 2 * i:2 * i + 2, :], kb[0:HD, :].rearrange("p (h t) -> p h t", h=2), ACT.Copy), m)
            for j in range(2):
                hh = 2 * i + j
                for kt in range(2):
                    m = pe.step(lambda e, hh=hh, j=j, kt=kt, qb=qb: e.matmul(
                        qb[0:QH, j * T:(j + 1) * T], wuq[:, kt, hh * QH:(hh + 1) * QH], lat[:, kt, :],
                        start=kt == 0, stop=kt == 1), m_cq, mq_.get(i - 2))
            qs = q[:, 2 * i:2 * i + 2, :]
            mq_[i] = act.step(lambda e, qs=qs, qb=qb: e.activation(
                qs[0:QH], qb[0:QH, :].rearrange("p (h t) -> p h t", h=2), ACT.Copy), m)
            m = pe.step(lambda e, qs=qs, tb=tb: e.matmul(tb[0:QH, :], A("turn", QH, 0, QH), qs[0:QH],
                                                         start=True, stop=True), mq_[i], mt_.get(i - 2))
            two = lambda z: z.rearrange("p (n t) -> p n t", n=1).broadcast_to([ROPE, 2, T])
            m1 = pool.step(lambda e, qs=qs: e.tensor_tensor(qs[rp], qs[rp], two(A("cos", None, HD, QH)), ALU.mult), m)
            m2 = dve.step(lambda e, tb=tb, i=i: e.tensor_tensor(
                env["h"][rp, :, :], tb[rp, :].rearrange("p (h t) -> p h t", h=2), two(A("sin", None, HD, QH)),
                ALU.mult), m, mt_.get(i - 1))
            mt_[i] = dve.step(lambda e, qs=qs: e.tensor_tensor(qs[rp], qs[rp], env["h"][rp, :, :], ALU.add), m1, m2)
        meet()
        m = attend(env, ctx, "mla", lambda i, qb: (q[0:QH, i, qb * P:(qb + 1) * P], k[0:QH, i, :]),
                   lambda i, kb: v[:, kb, i * HD:(i + 1) * HD], float(QH) ** -0.5, None, [m_kr, m_v])
        m = env["split_xn"](m)
        m = linear(a["mla_o"], 4, None, env["add_chunks"](gate), [m])
        meet()
    return m[-1]


def router(env, ctx, m_in):
    a, sb, bank, pe, act, dve = (env[n] for n in ("a", "sb", "bank", "pe", "act", "dve"))
    dma, meet, C, ident, xn = (env[n] for n in ("dma", "meet", "C", "ident", "xn"))
    E = EXPERTS
    marks = meet()
    comb = sb("comb", [P, E, T], ctx=ctx)
    wr = sb("wr", [P, KT, E], ctx=ctx)
    pr = sb("pr", [P, NB, E], ctx=ctx)
    st = sb("rst", [P, NB], ctx=ctx)
    gt = sb("rgt", [P, NB, E, E], ctx=ctx)
    eq = sb("req", [P, NB, E, E], ctx=ctx)
    got = dma(act, wr[:, :, :], a["router"], "router", *marks)
    for b in range(NB):
        for k in range(KT):
            m = pe.step(lambda e, b=b, k=k: e.matmul(bank[0][:, b * E:(b + 1) * E], xn[:, k, b * P:(b + 1) * P],
                                                     wr[:, k, :], start=k == 0, stop=k == KT - 1), got, m_in)
    m = dve.step(lambda e: e.tensor_copy(pr[:, :, :], bank[0][:, 0:NB * E].rearrange("p (b e) -> p b e", b=NB)), m)
    wide = lambda z: z.rearrange("p (b n) -> p b n", n=1).broadcast_to([P, NB, E])

    def TT(o, i0, i1, op, *after):
        return dve.step(lambda e: e.tensor_tensor(o, i0, i1, op), *after)

    m = dve.step(lambda e: e.reduce_max(st[:, :], pr[:, :, :], AX_X), m)
    m = TT(pr[:, :, :], pr[:, :, :], wide(st[:, :]), ALU.subtract, m)
    m = act.step(lambda e: e.activation(pr[:, :, :], pr[:, :, :], ACT.Exp), m)

    def normalise(m):
        m = dve.step(lambda e: e.reduce_sum(st[:, :], pr[:, :, :], AX_X), m)
        m = dve.step(lambda e: e.reciprocal(st[:, :], st[:, :]), m)
        return TT(pr[:, :, :], pr[:, :, :], wide(st[:, :]), ALU.mult, m)

    m = normalise(m)
    for b in range(NB):
        other = pr[:, b, :].rearrange("p (n j) -> p n j", n=1).broadcast_to([P, E, E])
        own = pr[:, b, :].rearrange("p (j n) -> p j n", n=1).broadcast_to([P, E, E])
        m1 = TT(gt[:, b], other, own, ALU.is_gt, m)
        m2 = TT(eq[:, b], other, own, ALU.is_equal, m)
        m2 = TT(eq[:, b], eq[:, b], C("earlier").rearrange("p (e j) -> p e j", e=E), ALU.mult, m2)
        m3 = TT(gt[:, b], gt[:, b], eq[:, b], ALU.add, m1, m2)
        m4 = dve.step(lambda e, b=b: e.reduce_sum(eq[:, b, 0, :], gt[:, b], AX_X), m3)
        m5 = dve.step(lambda e, b=b: e.tensor_scalar(eq[:, b, 0, :], eq[:, b, 0, :], 1.5, None, ALU.is_lt), m4)
        ml = TT(pr[:, b, :], pr[:, b, :], eq[:, b, 0, :], ALU.mult, m5)
    m = normalise(ml)
    for i in range(E):
        bk = bank[1 + i // 2 % 4]
        for b in range(NB):
            mm = pe.step(lambda e, i=i, b=b, bk=bk: e.matmul(
                bk[:, (i % 2) * T + b * P:(i % 2) * T + (b + 1) * P],
                pr[:, b, i:i + 1].broadcast_to([P, P]), ident, start=True, stop=True), m)
        if i % 2:
            mc = dve.step(lambda e, i=i, bk=bk: e.tensor_copy(
                comb[:, i - 1:i + 1, :], bk[:, :].rearrange("p (k t) -> p k t", k=2)), mm)
    meet()
    return comb, mc


def column_chunks(w):
    return w.reshape(KT, P, -1, CW).transpose(2, 1, 0, 3).reshape(-1, P, CHUNK)


def ffn_chunks(w_in, w_out):
    f = w_out.shape[0]
    down = w_out.reshape(f // CW, 2, P, D).transpose(0, 2, 1, 3).reshape(-1, P, CHUNK)
    return np.stack([column_chunks(w_in[:, :f]), column_chunks(w_in[:, f:]), down], axis=1)


def layout(inp):
    g = {k: np.asarray(v) for k, v in inp.items()}
    (main, _), (att, _) = shape_constants()
    tiles = lambda w: w.reshape(-1, P, w.shape[-1]).transpose(1, 0, 2)
    vec = np.concatenate([g[n].reshape(-1, P).T for n, _ in VECTORS], axis=1)
    w_in = g["w_in"][0]
    qkv = g["na_w_qkv_2"][0]
    ada = g["w_ada_2"].reshape(2, KT, P, 6 * D // ADA_W, ADA_W).transpose(0, 3, 2, 1, 4)
    moe_in, moe_out = g["moe_w_gu_2"][0], g["moe_w_down_2"][0]
    return {
        "x": tiles(g["x"][0].T), "vec": vec, "cst": main, "att": att,
        "ffn1": ffn_chunks(g["ffn1_w_in"][0], g["ffn1_w_out"][0]),
        "ffn2": ffn_chunks(g["ffn2_w_in"][0], g["ffn2_w_out"][0]),
        "ffn3": ffn_chunks(g["ffn_w_gu_2"][0], g["ffn_w_down_2"][0]),
        "moe": np.concatenate([ffn_chunks(moe_in[e], moe_out[e]) for e in range(EXPERTS)]),
        "ada": ada.reshape(ADA_UNITS, P, KT, ADA_W),
        "w_in": column_chunks(w_in[:, :MIX_TILES * P]), "w_in_ga": tiles(w_in[:, MIX_TILES * P:]),
        "w_out": column_chunks(g["w_out"][0]),
        "rwkv_w2": g["rwkv_w2"][0], "rwkv_a2": g["rwkv_a2"][0], "rwkv_g2": g["rwkv_g2"][0],
        "gla_w2": g["gla_w2"][0], "pool_w": g["pool_w"][0],
        "na_qk": column_chunks(qkv[:, :2 * D]), "na_v": column_chunks(qkv[:, 2 * D:]),
        "na_o": column_chunks(g["na_w_o_2"][0]),
        "rpb": np.pad(g["na_rpb_2"][0], ((0, 0), (0, 0), (GRID - WIN_W, GRID - WIN_W))),
        "mla_down": tiles(g["mla_w_down_2"][0]), "mla_uq": tiles(g["mla_w_uq_2"][0]),
        "mla_ukv": g["mla_w_ukv_2"][0], "mla_o": column_chunks(g["mla_w_o_2"][0]),
        "router": tiles(g["moe_w_router_2"][0]),
    }


def kernel(**inputs):
    import concourse.bacc as bacc
    from concourse.bass_utils import run_bass_kernel_spmd

    nc = bacc.Bacc("TRN2", target_bir_lowering=False, num_devices=1)
    arrays = {"in_" + k: np.ascontiguousarray(v) for k, v in layout(inputs).items()}
    aps = {k[3:]: nc.dram_tensor(k, v.shape, mybir.dt.from_np(v.dtype), kind="ExternalInput").ap()
           for k, v in arrays.items()}
    out = nc.dram_tensor("out", (P, KT, T), F32, kind="ExternalOutput").ap()
    build_program(nc, aps, out)
    r = run_bass_kernel_spmd(nc, [arrays], core_ids=[0])
    got = r.results[0]["out"]
    return np.ascontiguousarray(got.transpose(2, 1, 0).reshape(1, T, D))
```

```python
from contextlib import ExitStack

import numpy as np
import concourse.bass as bass
from concourse import mybir

F32 = mybir.dt.float32
F32R = mybir.dt.float32r
BF16 = mybir.dt.bfloat16
U32 = mybir.dt.uint32
ALU = mybir.AluOpType
ACT = mybir.ActivationFunctionType
AX_X = mybir.AxisListType.X

P = 128
T = 256
D = 1024
KT = D // P
NB = T // P
CW = 256
CHUNK = KT * CW
FFN_UNITS = 2816 // CW
EXPERTS = 8
EXPERT_UNITS = 1792 // CW
G = 256
GT = G // P
HD = 64
MH = G // HD
RCHUNK = 64
NCH = T // RCHUNK
MIX_TILES = 26
GLA_LORA = 16
ADA_W = 384
ADA_UNITS = 2 * 6 * D // ADA_W
MODS = 6 * KT
AH = 16
GRID = 64
ROWS = T // GRID
WIN_H, WIN_W = 8, 16
QL, ROPE, QH = 256, 32, 96
EPS = 1e-6
GN_EPS = 64e-5
QK_SCALE = HD ** -0.5
NEG = -1e30

VECTORS = [
    ("norm_ffn1", KT), ("norm_mix", KT), ("norm_ffn2", KT), ("norm_final", KT), ("pool_b", GT),
    ("pool_scale", GT), ("hgrn_lb_logits", GT), ("hgrn_norm", GT), ("rwkv_mu", 8), ("rwkv_w0", GT),
    ("rwkv_a0", GT), ("rwkv_k_k", GT), ("rwkv_k_a", GT), ("rwkv_r_k", GT), ("rwkv_ln_w", GT),
    ("rwkv_ln_b", GT), ("gla_b", GT), ("gla_norm", GT), ("c_2", KT), ("b_ada_2", 2 * MODS),
    ("mla_q_norm_2", GT), ("mla_kv_norm_2", 1), ("final_norm_2", KT),
]
NVEC = sum(n for _, n in VECTORS)
VEC = {}
for _name, _n in VECTORS:
    VEC[_name] = sum(VECTORS[i][1] for i in range(len(VEC)))


def shape_constants():
    s, t = np.arange(P)[:, None], np.arange(P)[None, :]
    main = {"ident": s == t, "ones": np.ones((P, P)), "headsum": s // HD == t // HD}
    same = s // RCHUNK == t // RCHUNK
    main["before"] = same & (s < t)
    main["upto"] = same & (s <= t)
    main["after"] = same & (s > t)
    for m in (1, 2, 4, 8, 16, 32, 64):
        pair = (s // (2 * m) == t // (2 * m)) & (s // m % 2 == 0) & (t // m % 2 == 1)
        main[f"level{m}"] = pair
        if m < RCHUNK:
            main[f"levelT{m}"] = pair.T
    w = np.array([2, 4, 8, 16])[(np.arange(GT)[None, :] * 2 + np.arange(P)[:, None] // 64)]
    count = np.minimum(np.arange(T)[None, None, :] + 1, w[:, :, None])
    main["invcount"] = (np.float32(1) / count.astype(np.float32)).reshape(P, GT * T)
    e = np.arange(EXPERTS)
    main["earlier"] = np.broadcast_to((e[None, :] < e[:, None]).reshape(1, -1), (P, EXPERTS * EXPERTS))
    main["chunkkeep"] = np.broadcast_to((np.arange(T) % RCHUNK != 0)[None, :], (P, T))
    q, k = GRID - 1 - np.arange(P)[:, None] % GRID, np.arange(GRID)[None, :]
    first = np.clip(q - WIN_W // 2, 0, GRID - WIN_W)
    attn = {"window": np.where((k >= first) & (k < first + WIN_W), 0.0, NEG)}
    n = ROPE // 4
    inv = (np.float32(10000.0) ** (-np.arange(n, dtype=np.float32) / np.float32(n))).astype(np.float32)
    pos = np.arange(T)
    ang = np.concatenate([(pos // GRID).astype(np.float32)[:, None] * inv,
                          (pos % GRID).astype(np.float32)[:, None] * inv], axis=-1).astype(np.float32)
    cos, sin = np.ones((P, T)), np.zeros((P, T))
    cos[HD:QH] = np.repeat(np.cos(ang), 2, axis=1).T
    sin[HD:QH] = np.repeat(np.sin(ang), 2, axis=1).T
    turn = np.zeros((P, P))
    for i in range(ROPE // 2):
        a, b = HD + 2 * i, HD + 2 * i + 1
        turn[b, a], turn[a, b] = -1.0, 1.0
    place, placeturn = np.zeros((P, P)), np.zeros((P, P))
    for i in range(ROPE):
        place[i, HD + i] = 1.0
        placeturn[i] = turn[HD + i]
    attn |= {"cos": cos, "sin": sin, "turn": turn, "place": place, "placeturn": placeturn}

    def pack(parts):
        at, where = 0, {}
        for name, a in parts.items():
            where[name] = (at, a.shape[1])
            at += a.shape[1]
        return np.ascontiguousarray(np.concatenate([a.astype(np.float32) for a in parts.values()], 1)), where

    return pack(main), pack(attn)


class Lane:

    def __init__(self, sem):
        self.sem, self.n, self.queue, self.seen = sem, 0, [], {}

    def mark(self):
        return (self.sem, self.n)

    def wait(self, *marks):
        for m in marks:
            if m is None:
                continue
            sem, value = m
            if value > 0 and self.seen.get(sem.name, 0) < value:
                self.seen[sem.name] = value
                self.queue.append(lambda e, s=sem, v=value: e.wait_ge(s, v))

    def step(self, make, *after):
        self.wait(*after)
        self.n += 1
        self.queue.append(lambda e: make(e).then_inc(self.sem, 1))
        return self.mark()

    def plain(self, make):
        self.queue.append(make)

    def loop(self, first, end, body):
        def run(e):
            with e.Fori(first, end) as i:
                body(e, i)
        if end - first > 1:
            self.queue.append(run)
        elif end > first:
            self.queue.append(lambda e: body(e, first))


def build_program(nc, a, out):
    (_, MAIN), (_, ATT) = shape_constants()
    stack = ExitStack()
    with stack:
        def sb(name, shape, dt=F32, ctx=stack):
            return ctx.enter_context(nc.sbuf_tensor("sb_" + name, shape, dt))

        def sem(name):
            return stack.enter_context(nc.semaphore(name))

        bank = [stack.enter_context(nc.psum_tensor(f"bank{i}", [P, 512], F32)) for i in range(8)]
        pe, act, dve, pool, sp = (Lane(sem("done_" + n)) for n in ("pe", "act", "dve", "pool", "sp"))

        raw = [sb(f"raw{s}", [P, CHUNK]) for s in range(3)]
        whi = [sb(f"whi{s}", [P, CHUNK], F32R) for s in range(3)]
        wlo = [sb(f"wlo{s}", [P, CHUNK], F32R) for s in range(3)]
        x = sb("x", [P, KT, T])
        xn = sb("xn", [P, KT, T])
        xhi = sb("xhi", [P, KT, T], F32R)
        xlo = sb("xlo", [P, KT, T], F32R)
        h = sb("h", [P, 2, T])
        hhi = sb("hhi", [P, 2, T], F32R)
        hlo = sb("hlo", [P, 2, T], F32R)
        sil = sb("sil", [P, 2, T])
        ada_raw = sb("ada_raw", [P, KT, ADA_W])
        ada_acc = sb("ada_acc", [P, ADA_W])
        cact = sb("cact", [P, KT])
        mod = sb("mod", [P, 2, MODS])
        cst = sb("cst", [P, sum(n for _, n in MAIN.values())])
        vec = sb("vec", [P, NVEC])
        rstd = sb("rstd", [P, 2, T])
        epss = sb("epss", [P, 2])
        sq = sb("sq", [P, 2, T])
        zero = sb("zero", [P, 512], BF16)

        def C(name, p0=0, p1=P):
            at, n = MAIN[name]
            return cst[p0:p1, at:at + n]

        def V(name, i=0, p0=0, p1=P):
            return vec[p0:p1, VEC[name] + i:VEC[name] + i + 1]

        ident, ones = C("ident"), C("ones")

        def dma(lane, dst, src, name, *after):
            s = sem("in_" + name)
            lane.wait(*after)
            lane.queue.append(lambda e: e.dma_start(dst, src).then_inc(s, 16))
            return (s, 16)

        scratch_free = [[]]

        def meet():
            marks = [l.mark() for l in (pe, act, dve, pool)]
            scratch_free[0] = marks
            for l in (pe, act, dve, pool):
                l.wait(*marks)
            return marks

        got_x = dma(act, x[:, :, :], a["x"], "x")
        got_vec = dma(act, vec[:, :], a["vec"], "vec")
        got_cst = dma(act, cst[:, :], a["cst"], "cst")
        for l in (pe, act, dve, pool):
            l.wait(got_vec, got_cst)
        m_zero = pool.step(lambda e: e.memset(zero[:, :], 0.0))
        m_cact = act.step(lambda e: e.activation(cact[:, :], vec[:, VEC["c_2"]:VEC["c_2"] + KT], ACT.Silu), got_vec)
        dve.wait(m_cact)
        pe.wait(m_zero)
        m_eps = pool.step(lambda e: e.memset(epss[:, 0:1], EPS))
        act.wait(pool.step(lambda e: e.memset(epss[:, 1:2], GN_EPS)), m_eps)

        s_raw = [sem(f"raw_landed{s}") for s in range(3)]
        s_hi = [sem(f"high_ready{s}") for s in range(3)]
        s_lo = [sem(f"low_ready{s}") for s in range(3)]
        s_used = [sem(f"weights_used{s}") for s in range(3)]
        uses = [0, 0, 0]
        turn = [0]
        split_ahead = []
        for s in range(3):
            pe.plain(lambda e, s=s: e.sem_inc(s_used[s], 1))
            act.plain(lambda e, s=s: e.sem_inc(s_hi[s], 1))
            dve.plain(lambda e, s=s: e.sem_inc(s_lo[s], 1))

        def load(e, s, n, src):
            e.wait_ge(s_lo[s], n + 1)
            e.dma_start(raw[s][:, :], src).then_inc(s_raw[s], 16)

        def high(e, s, n):
            e.wait_ge(s_raw[s], 16 * n + 16)
            e.wait_ge(s_used[s], n + 1)
            e.activation(whi[s][:, :], raw[s][:, :], ACT.Copy).then_inc(s_hi[s], 1)

        def low(e, s, n):
            e.wait_ge(s_hi[s], n + 2)
            e.tensor_tensor(wlo[s][:, :], raw[s][:, :], whi[s][:, :], ALU.subtract).then_inc(s_lo[s], 1)

        def fetch(src):
            if split_ahead and src is not None and split_ahead[0][2] is src:
                s, nth, _ = split_ahead.pop(0)
                return s, nth
            assert not split_ahead
            return fetch_now(src)

        def fetch_now(src):
            s = turn[0]
            nth = uses[s]
            turn[0] = (s + 1) % 3
            uses[s] += 1
            sp.plain(lambda e: load(e, s, nth, src))
            act.plain(lambda e: high(e, s, nth))
            dve.plain(lambda e: low(e, s, nth))
            return s, nth

        def ahead(*srcs):
            for src in srcs:
                split_ahead.append((*fetch_now(src), src))

        def product(e, dst, w, x_parts, first, last, skip=False):
            (wh, wl), (xh, xl) = w, x_parts
            e.matmul(dst, wh, xh, start=first, stop=False, skip_group_check=skip)
            e.matmul(dst, wh, xl, start=False, stop=False, skip_group_check=skip)
            return e.matmul(dst, wl, xh, start=False, stop=last, skip_group_check=skip)

        def wtile(s, at):
            return whi[s][:, at:at + P], wlo[s][:, at:at + P]

        def square_sum(src, tiles, dst, *after):
            marks = []
            buf = lambda k: (sil if k % 4 < 2 else sq)[:, k % 2, :]
            for k in range(tiles):
                mine = (after[k],) if len(after) == tiles else after
                m = act.step(lambda e, k=k: e.activation(buf(k), src(k), ACT.Square),
                             *mine, marks[k - 4] if k >= 4 else None)
                marks.append(pe.step(lambda e, k=k: e.matmul(dst, ones, buf(k),
                                                             start=k == 0, stop=k == tiles - 1), m))
            return marks[-1]

        def inv_root(dst, src, scale, eps, *after):
            bias = epss[:, 0:1] if eps == EPS else epss[:, 1:2]
            m = act.step(lambda e: e.activation(dst, src, ACT.Sqrt, bias=bias, scale=scale), *after)
            return dve.step(lambda e: e.reciprocal(dst, dst), m)

        def norm(gain, shift, after, *also):
            act.wait(*also)
            dve.wait(*also)
            m = square_sum(lambda k: x[:, k, :], KT, bank[6][:, 0:T], *after)
            m_r = inv_root(rstd[:, 0, :], bank[6][:, 0:T], 1.0 / D, EPS, m)
            parts, mh = [], []

            def lows(k):
                parts.append(dve.step(lambda e: e.tensor_tensor(
                    xlo[:, k, :], xn[:, k, :], xhi[:, k, :], ALU.subtract), mh[k]))

            for k in range(KT):
                m = dve.step(lambda e, k=k: e.scalar_tensor_tensor(
                    xn[:, k, :], x[:, k, :], gain(k), rstd[:, 0, :], ALU.mult, ALU.mult), m_r)
                if shift is not None:
                    m = act.step(lambda e, k=k: e.activation(xn[:, k, :], xn[:, k, :], ACT.Identity,
                                                             bias=shift(k)), m)
                mh.append(act.step(lambda e, k=k: e.activation(xhi[:, k, :], xn[:, k, :], ACT.Copy), m))
                if k >= 2:
                    lows(k - 2)
            lows(KT - 2)
            lows(KT - 1)
            return parts

        def split_xn(m):
            parts = []
            for k in range(0, KT, 2):
                mh = act.step(lambda e, k=k: e.activation(xhi[:, k:k + 2, :], xn[:, k:k + 2, :], ACT.Copy),
                              *(m[k:k + 2] if isinstance(m, list) else (m,)))
                ml = dve.step(lambda e, k=k: e.tensor_tensor(xlo[:, k:k + 2, :], xn[:, k:k + 2, :],
                                                             xhi[:, k:k + 2, :], ALU.subtract), mh)
                parts += [ml, ml]
            return parts

        s_silu, s_mult, s_hhi, s_hlo = sem("silu_done"), sem("mult_done"), sem("h_high"), sem("h_low")
        s_ada_raw, s_ada, s_chain, s_adr = sem("ada_landed"), sem("ada_partial"), sem("ada_chain"), sem("ada_summed")
        s_ctmp = sem("h_before_weighting")
        for l, s in ((pe, s_adr), (dve, s_ada), (act, s_silu), (dve, s_mult), (dve, s_hlo)):
            l.plain(lambda e, s=s: e.sem_inc(s, 1))
        units_before = [0]
        GATE, UP, MODP = bank[4], bank[5], bank[7]

        def ffn(w, n, ada_first, ada_n, weight, parts, free, following, ada_after=None):
            u0 = units_before[0]
            units_before[0] += n
            (A_, na, _), (B_, nb, _) = split_ahead
            split_ahead.clear()
            C_ = turn[0]
            b0 = {A_: na, B_: nb, C_: uses[C_]}
            for s in range(3):
                uses[s] = b0[s] + n
            turn[0] = A_
            has_ada = lambda j: ada_n > 0 and (not isinstance(j, int) or j < ada_n)

            def sp_in(e, j):
                load(e, A_, b0[A_] + j, w[j, 0])
                load(e, B_, b0[B_] + j, w[j, 1])

            def sp_ada(e, j):
                e.wait_ge(s_ada, ada_first + j + 1)
                e.dma_start(ada_raw[:, :, :], a["ada"][ada_first + j]).then_inc(s_ada_raw, 16)

            def sp_down(e, j):
                load(e, C_, b0[C_] + j, w[j, 2])

            def a_hhi(e, j):
                e.wait_ge(s_mult, u0 + j + 2)
                e.wait_ge(s_used[C_], b0[C_] + j + 1)
                e.activation(hhi[:, :, :], h[:, :, :], ACT.Copy).then_inc(s_hhi, 1)

            def a_silu(e, j):
                e.wait_ge(s_used[A_], b0[A_] + j + 2)
                e.wait_ge(s_mult, u0 + j + 1)
                e.activation(sil[:, :, :], GATE[:, :], ACT.Silu).then_inc(s_silu, 1)

            def v_hlo(e, j):
                e.wait_ge(s_hhi, u0 + j + 1)
                e.tensor_tensor(hlo[:, :, :], h[:, :, :], hhi[:, :, :], ALU.subtract).then_inc(s_hlo, 1)

            def v_mult(e, j):
                e.wait_ge(s_used[B_], b0[B_] + j + 2)
                e.wait_ge(s_hlo, u0 + j + 1)
                e.wait_ge(s_silu, u0 + j + 2)
                if weight is None:
                    e.tensor_tensor(h[:, :, :], sil[:, :, :], UP[:, :], ALU.mult).then_inc(s_mult, 1)
                else:
                    e.tensor_tensor(h[:, :, :], sil[:, :, :], UP[:, :], ALU.mult).then_inc(s_ctmp, 1)
                    e.wait_ge(s_ctmp, j + 1)
                    e.tensor_tensor(h[:, :, :], h[:, :, :], weight(j), ALU.mult).then_inc(s_mult, 1)

            def v_ada(e, j):
                e.wait_ge(s_ada_raw, 16 * (ada_first + j) + 16)
                e.wait_ge(s_adr, ada_first + j + 1)
                c0 = (ada_first + j) * (KT - 1)
                e.tensor_scalar(ada_acc[:, :], ada_raw[:, 0, :], cact[:, 0:1], None, ALU.mult).then_inc(s_chain, 1)
                for k in range(1, KT):
                    e.wait_ge(s_chain, c0 + k)
                    e.scalar_tensor_tensor(ada_acc[:, :], ada_raw[:, k, :], cact[:, k:k + 1], ada_acc[:, :],
                                           ALU.mult, ALU.add).then_inc(s_ada if k == KT - 1 else s_chain, 1)

            def p_ada(e, j):
                e.wait_ge(s_ada, ada_first + j + 2)
                for i in range(ADA_W // P):
                    l = e.matmul(MODP[:, bass.ds((ada_first + j) * (ADA_W // P) + i, 1)],
                                 ada_acc[:, i * P:(i + 1) * P], ones[:, 0:1], start=True, stop=True)
                l.then_inc(s_adr, 1)

            def p_gate(e, j, s, dst, free_sem, parts=None):
                e.wait_ge(s_lo[s], b0[s] + j + 2)
                e.wait_ge(free_sem, u0 + j + 1)
                for m in range(CW // P):
                    for k in range(KT):
                        if parts is not None and m == 0:
                            e.wait_ge(*parts[k])
                        l = product(e, dst[:, m * T:(m + 1) * T], wtile(s, k * CW + m * P),
                                    (xhi[:, k, :], xlo[:, k, :]), k == 0, k == KT - 1)
                l.then_inc(s_used[s], 1)

            def p_down(e, j):
                e.wait_ge(s_lo[C_], b0[C_] + j + 2)
                e.wait_ge(s_hlo, u0 + j + 2)
                for m in range(KT):
                    for k in range(2):
                        l = product(e, bank[m // 2][:, (m % 2) * T:(m % 2 + 1) * T],
                                    wtile(C_, k * D + m * P), (hhi[:, k, :], hlo[:, k, :]),
                                    False, False, skip=True)
                l.then_inc(s_used[C_], 1)

            def sp_body(e, j):
                sp_in(e, j + 1)
                if has_ada(j):
                    sp_ada(e, j)
                sp_down(e, j)

            def act_body(e, j, more=True):
                a_hhi(e, j - 1)
                high(e, C_, b0[C_] + j - 1)
                a_silu(e, j)
                if more:
                    high(e, A_, b0[A_] + j + 1)
                    high(e, B_, b0[B_] + j + 1)

            def dve_body(e, j, more=True):
                v_hlo(e, j - 1)
                low(e, C_, b0[C_] + j - 1)
                if more:
                    low(e, A_, b0[A_] + j + 1)
                v_mult(e, j)
                if more:
                    low(e, B_, b0[B_] + j + 1)
                if has_ada(j):
                    v_ada(e, j)

            def pe_body(e, j):
                p_gate(e, j, A_, GATE, s_silu)
                if has_ada(j - 1):
                    p_ada(e, j - 1)
                p_gate(e, j, B_, UP, s_mult)
                p_down(e, j - 1)

            sp.plain(lambda e: sp_in(e, 1))
            sp.wait(ada_after)
            if has_ada(0):
                sp.plain(lambda e: sp_ada(e, 0))
            sp.plain(lambda e: sp_down(e, 0))
            sp.loop(1, n - 1, sp_body)
            if has_ada(n - 1):
                sp.plain(lambda e: sp_ada(e, n - 1))
            sp.plain(lambda e: sp_down(e, n - 1))

            act.plain(lambda e: a_silu(e, 0))
            act.plain(lambda e: high(e, A_, b0[A_] + 1))
            act.plain(lambda e: high(e, B_, b0[B_] + 1))
            act.loop(1, n - 1, act_body)
            act.plain(lambda e: act_body(e, n - 1, False))
            act.plain(lambda e: a_hhi(e, n - 1))
            act.plain(lambda e: high(e, C_, b0[C_] + n - 1))

            dve.plain(lambda e: low(e, A_, b0[A_] + 1))
            dve.plain(lambda e: v_mult(e, 0))
            dve.plain(lambda e: low(e, B_, b0[B_] + 1))
            if has_ada(0):
                dve.plain(lambda e: v_ada(e, 0))
            dve.loop(1, n - 1, dve_body)
            dve.plain(lambda e: dve_body(e, n - 1, False))
            dve.plain(lambda e: v_hlo(e, n - 1))
            dve.plain(lambda e: low(e, C_, b0[C_] + n - 1))
            ahead(*following)

            pe.wait(*free)
            for b in range(4):
                pe.plain(lambda e, b=b: e.matmul(bank[b][:, :], zero[:, 0:P], zero[:, :], start=True, stop=False,
                                                 skip_group_check=True))
            pe.plain(lambda e: p_gate(e, 0, A_, GATE, s_silu, parts))
            pe.plain(lambda e: p_gate(e, 0, B_, UP, s_mult))
            pe.loop(1, n - 1, pe_body)
            pe.plain(lambda e: pe_body(e, n - 1))
            pe.plain(lambda e: p_down(e, n - 1))
            if has_ada(n - 1):
                pe.plain(lambda e: p_ada(e, n - 1))
            for b in range(4):
                m = pe.step(lambda e, b=b: e.matmul(bank[b][:, :], zero[:, 0:P], zero[:, :], start=False,
                                                    stop=True, skip_group_check=True))
            return m

        def linear(chunks, evac, parts, following):
            marks, done, slots = [], [], []
            n = len(chunks)

            def run(e, s, form, dst, first):
                for m in range(2):
                    for k in range(KT):
                        if first and m == 0:
                            e.wait_ge(*parts[k])
                        if form == "channels":
                            o = dst[:, m * T:(m + 1) * T]
                            l = product(e, o, wtile(s, k * CW + m * P), (xhi[:, k, :], xlo[:, k, :]),
                                        k == 0, k == KT - 1)
                        else:
                            o = dst[:, m * CW:(m + 1) * CW]
                            wh, wl = (z[s][:, k * CW:(k + 1) * CW] for z in (whi, wlo))
                            xh, xl = (z[:, k, m * P:(m + 1) * P] for z in (xhi, xlo))
                            l = product(e, o, (xh, xl), (wh, wl), k == 0, k == KT - 1)
                l.then_inc(s_used[s], 1)

            for c, (src, form) in enumerate(chunks):
                s, nth = fetch(src)
                slots.append(s)
                pe.wait((s_lo[s], nth + 2), marks[c - 3] if c >= 3 else None)
                pe.plain(lambda e, s=s, form=form, c=c: run(e, s, form, bank[4 + s], c == 0))
                done.append((s_used[s], nth + 2))
                if c >= 2:
                    marks.append(evac(c - 2, bank[4 + slots[c - 2]], done[c - 2]))
            ahead(*following)
            for c in range(max(n - 2, 0), n):
                marks.append(evac(c, bank[4 + slots[c]], done[c]))
            return marks

        def add_half(m):
            r = []
            for b in range(4):
                r += 2 * [dve.step(lambda e, b=b: e.scalar_tensor_tensor(
                    x[:, 2 * b:2 * b + 2, :], bank[b][:, :].rearrange("p (k t) -> p k t", k=2), 0.5,
                    x[:, 2 * b:2 * b + 2, :], ALU.mult, ALU.add), m)]
            return r

        def add_gated(gate, m):
            return [dve.step(lambda e, k=k: e.scalar_tensor_tensor(
                x[:, k, :], bank[k // 2][:, (k % 2) * T:(k % 2 + 1) * T], gate(k), x[:, k, :],
                ALU.mult, ALU.add), m) for k in range(KT)]

        def add_chunks(gate):
            def evac(c, b, m):
                r = None
                for i in range(2):
                    k = 2 * c + i
                    src = b[:, i * T:(i + 1) * T]
                    if gate is None:
                        r = dve.step(lambda e, k=k, src=src: e.tensor_tensor(x[:, k, :], src, x[:, k, :], ALU.add), m)
                    else:
                        r = dve.step(lambda e, k=k, src=src: e.scalar_tensor_tensor(
                            x[:, k, :], src, gate(k), x[:, k, :], ALU.mult, ALU.add), m)
                return r
            return evac

        env = dict(locals())
        first = {n: (a[n][0, 0], a[n][0, 1]) for n in ("ffn1", "ffn2", "ffn3", "moe")}
        chunks = {n: [a[n][c] for c in range(a[n].shape[0])]
                  for n in ("w_in", "w_out", "na_qk", "na_v", "na_o", "mla_o")}
        env |= {"first": first, "chunks": chunks}
        ahead(*first["ffn1"])
        m = norm(lambda k: V("norm_ffn1", k), None, [got_x])
        m = ffn(a["ffn1"], FFN_UNITS, 0, FFN_UNITS, None, m, [], chunks["w_in"][:2])
        mx = add_half(m)
        m = norm(lambda k: V("norm_mix", k), None, mx)
        mx = token_mixer(env, m)
        m = norm(lambda k: V("norm_ffn2", k), None, mx)
        m = ffn(a["ffn2"], FFN_UNITS, FFN_UNITS, FFN_UNITS, None, m, [], chunks["na_qk"][:2], mx[-1])
        mx = add_half(m)
        mm = square_sum(lambda k: x[:, k, :], KT, bank[6][:, 0:T], *mx)
        mm = inv_root(rstd[:, 0, :], bank[6][:, 0:T], 1.0 / D, EPS, mm)
        mx = [dve.step(lambda e, k=k: e.scalar_tensor_tensor(x[:, k, :], x[:, k, :], V("norm_final", k),
                                                             rstd[:, 0, :], ALU.mult, ALU.mult), mm)
              for k in range(KT)]

        def take_mod(layer, pieces):
            b = VEC["b_ada_2"] + layer * MODS
            mt = dve.step(lambda e: e.tensor_tensor(mod[:, layer, :], MODP[:, layer * MODS:(layer + 1) * MODS],
                                                    vec[:, b:b + MODS], ALU.add), (s_adr, pieces + 1))
            for part in (1, 4):
                sl = mod[:, layer, part * KT:(part + 1) * KT]
                mt = dve.step(lambda e, sl=sl: e.tensor_scalar_add(sl, sl, 1.0), mt)
            return mt

        def M(layer, part):
            return lambda k: mod[:, layer, part * KT + k:part * KT + k + 1]

        mt = take_mod(0, 2 * FFN_UNITS)
        m = norm(M(0, 1), M(0, 0), mx, mt)
        mx = neighbourhood(env, M(0, 2), m)
        m = norm(M(0, 4), M(0, 3), mx)
        m = ffn(a["ffn3"], FFN_UNITS, 2 * FFN_UNITS, ADA_UNITS - 2 * FFN_UNITS, None, m, [], chunks["mla_o"][:2])
        mx = add_gated(M(0, 5), m)
        mt = take_mod(1, ADA_UNITS)
        m = norm(M(1, 1), M(1, 0), mx, mt)
        mx = latent(env, M(1, 2), m)
        m = norm(M(1, 4), M(1, 3), mx)
        with ExitStack() as ctx:
            comb, mc = router(env, ctx, m[-1])
            m = ffn(a["moe"], EXPERTS * EXPERT_UNITS, 0, 0,
                    lambda j: comb[:, bass.ds(j // EXPERT_UNITS, 1), :].broadcast_to([P, 2, T])
                    if not isinstance(j, int) else
                    comb[:, j // EXPERT_UNITS:j // EXPERT_UNITS + 1, :].broadcast_to([P, 2, T]), m, [mc], [])
        mx = add_gated(M(1, 5), m)
        mm = square_sum(lambda k: x[:, k, :], KT, bank[6][:, 0:T], *mx)
        mm = inv_root(rstd[:, 0, :], bank[6][:, 0:T], 1.0 / D, EPS, mm)
        stored = []
        for k in range(KT):
            m = dve.step(lambda e, k=k: e.scalar_tensor_tensor(xn[:, k, :], x[:, k, :], V("final_norm_2", k),
                                                               rstd[:, 0, :], ALU.mult, ALU.mult), mm)
            if k % 4 == 3:
                stored.append(dma(sp, out[:, k - 3:k + 1, :], xn[:, k - 3:k + 1, :], f"stored{k}", m))
        sp.wait(*stored)

        with nc.Block() as block:
            for lane, attach in ((sp, block.sync), (act, block.scalar), (dve, block.vector),
                                 (pe, block.tensor), (pool, block.gpsimd)):
                def run(e, lane=lane):
                    for item in lane.queue:
                        item(e)
                attach(run)


def token_mixer(env, m_in):
    a, sb, bank, pe, act, dve, pool = (env[n] for n in ("a", "sb", "bank", "pe", "act", "dve", "pool"))
    C, V, ident, ones, dma, meet = (env[n] for n in ("C", "V", "ident", "ones", "dma", "meet"))
    linear, square_sum, inv_root, rstd, y = (env[n] for n in ("linear", "square_sum", "inv_root", "rstd", "xn"))
    with ExitStack() as outer:
        p = sb("p", [P, MIX_TILES, T], ctx=outer)
        tok = sb("tok", [P, NB, T], ctx=outer)
        lora = sb("lora", [P, 2, G], ctx=outer)
        g2 = sb("g2", [P, G], ctx=outer)
        gw2 = sb("gw2", [GLA_LORA, G], ctx=outer)
        wga = sb("wga", [P, KT, GLA_LORA], ctx=outer)
        ga = sb("ga", [GLA_LORA, T], ctx=outer)
        wp = sb("wp", [P, GT, P], ctx=outer)
        m_z = pool.step(lambda e: e.memset(lora[:, :, :], 0.0))
        m_zp = pool.step(lambda e: e.memset(wp[:, :, :], 0.0))
        w_lora = [dma(pool, lora[0:64, 0, :], a["rwkv_w2"], "rwkv_w2", m_z),
                  dma(pool, lora[64:128, 1, :], a["rwkv_a2"], "rwkv_a2", m_z),
                  dma(pool, g2[:, :], a["rwkv_g2"], "rwkv_g2"),
                  dma(pool, gw2[:, :], a["gla_w2"], "gla_w2"),
                  dma(pool, wga[:, :, :], a["w_in_ga"], "w_in_ga")]
        w_pool = [dma(pool, wp[i % 2 * 64:i % 2 * 64 + 64, i // 2, i % 2 * 64:i % 2 * 64 + 64],
                      a["pool_w"][i], f"pool_w{i}", m_zp) for i in range(4)]

        def evac(c, b, m):
            dst = p[:, 2 * c:2 * c + 2, :]
            src = b[:, :].rearrange("p (k t) -> p k t", k=2)
            if c % 2:
                return act.step(lambda e: e.activation(dst, src, ACT.Copy), m)
            return dve.step(lambda e: e.tensor_copy(dst, src), m)

        em = linear([(w, "channels") for w in env["chunks"]["w_in"]], evac, m_in, env["chunks"]["w_out"][:2])
        for k in range(KT):
            mga = pe.step(lambda e, k=k: e.matmul(bank[3][0:GLA_LORA, 0:T], wga[:, k, :], y[:, k, :],
                                                  start=k == 0, stop=k == KT - 1), w_lora[4], m_in[-1])
        mga = act.step(lambda e: e.activation(ga[:, :], bank[3][0:GLA_LORA, 0:T], ACT.Copy), mga)
        meet()
        ready = list(em) + [mga]
        for l in (pe, act, dve, pool):
            l.wait(*ready, *w_lora, *w_pool)

        def TT(lane, o, i0, i1, op, *after):
            return lane.step(lambda e: e.tensor_tensor(o, i0, i1, op), *after)

        def TS(lane, o, i0, s1, s2, op0, op1, *after):
            if op1 is None:
                return lane.step(lambda e: e.tensor_scalar(o, i0, s1, None, op0), *after)
            return lane.step(lambda e: e.tensor_scalar(o, i0, s1, s2, op0, op1), *after)

        def STT(o, i0, s, i1, op0, op1, *after):
            return dve.step(lambda e: e.scalar_tensor_tensor(o, i0, s, i1, op0, op1), *after)

        def AC(o, i, f, *after, bias=None, scale=None):
            kw = {}
            if bias is not None:
                kw["bias"] = bias
            if scale is not None:
                kw["scale"] = scale
            return act.step(lambda e: e.activation(o, i, f, **kw), *after)

        def MM(o, l, r, start, stop, *after):
            return pe.step(lambda e: e.matmul(o, l, r, start=start, stop=stop), *after)

        def to_tokens(src, dst, b, *after):
            for i in range(GT):
                for blk in range(NB):
                    o = bank[b][:, blk * T + i * P:blk * T + (i + 1) * P]
                    m = pe.step(lambda e, o=o, i=i, blk=blk: e.transpose(o, src[:, i, blk * P:(blk + 1) * P], ident),
                                *after)
            return dve.step(lambda e: e.tensor_copy(dst, bank[b][:, :].rearrange("p (b c) -> p b c", b=NB)), m)

        with ExitStack() as c1:
            pad = 16
            wb = [sb(f"win{i}", [P, GT, pad + T], ctx=c1) for i in range(3)]
            m = pool.step(lambda e: e.memset(wb[0][:, :, 0:pad], 0.0))
            m1 = pool.step(lambda e: e.memset(wb[1][:, :, 0:pad], 0.0))
            m2 = pool.step(lambda e: e.memset(wb[2][:, :, 0:pad], 0.0))
            m = pool.step(lambda e: e.tensor_copy(wb[0][:, :, pad:], p[:, 0:2, :]), m)
            icn = C("invcount").rearrange("p (k t) -> p k t", k=GT)
            pooled = p[:, 0:2, :]
            cur, takes = 0, []
            for i, w in enumerate((1, 2, 4, 8)):
                nxt = 1 + i % 2 if i < 2 else (1 if i == 2 else 2)
                src, dst = wb[cur], wb[nxt]
                m = TT(pool, dst[:, :, pad:], src[:, :, pad:], src[:, :, pad - w:pad - w + T], ALU.add, m, m1, m2, *takes)
                tile, half = i // 2, i % 2 * 64
                takes.append(TT(pool, pooled[half:half + 64, tile, :], dst[half:half + 64, tile, pad:],
                                icn[half:half + 64, tile, :], ALU.mult, m))
                cur = nxt
            m = TT(pool, pooled, pooled, wb[0][:, :, pad:], ALU.subtract, *takes)
            for i in range(GT):
                m = MM(bank[7 - 1][:, i * T:(i + 1) * T], wp[:, i, :], p[:, i, :], True, True, m)
            for i in range(GT):
                m = TS(dve, p[:, i, :], bank[6][:, i * T:(i + 1) * T], V("pool_b", i), V("pool_scale", i),
                       ALU.add, ALU.mult, m)
            m_pool = m
            meet()

        def gated_attention(q, k, g, vt, dst, *after):
            with ExitStack() as c2:
                b = sb(f"cum{len(names)}", [P, GT, T], ctx=c2)
                ex = [sb(f"ex{i}{len(names)}", [P, GT * T], ctx=c2) for i in range(2)]
                sc = sb(f"sc{len(names)}", [P, MH, 3, P], ctx=c2)
                names.append(0)
                m_sc = pool.step(lambda e: e.memset(sc[:, :, :, :], 0.0))
                for i in range(GT):
                    mb = dve.step(lambda e, i=i: e.tensor_tensor_scan(
                        b[:, i, :], unit[:, :], g[:, i, :], 0.0, ALU.mult, ALU.add), *after)
                mv = to_tokens(vt, tok[:, :, :], 5, *after)
                bf = b[:, :, :].rearrange("p k t -> p (k t)")
                qf, kf = (z.rearrange("p k t -> p (k t)") for z in (q, k))
                m_pe = {0: None, 1: None}
                m_cp = {0: None, 1: None}
                levels = [0, 1, 2, 4, 8, 16, 32, 64, 128]
                for n, w in enumerate(levels):
                    e_, pair = ex[n % 2], n % 2
                    if w:
                        v3 = lambda z, w=w: z.rearrange("p (n j) -> p n j", j=2 * w)
                        mid = v3(bf)[:, :, w - 1:w].broadcast_to([P, GT * T // (2 * w), w])
                        lo, hi = (lambda z, w=w: v3(z, w)[:, :, 0:w]), (lambda z, w=w: v3(z, w)[:, :, w:2 * w])
                        m1 = TT(dve, hi(e_[:, :]), hi(bf), mid, ALU.subtract, mb, m_pe[pair])
                        m2 = TT(dve, lo(e_[:, :]), mid, lo(bf), ALU.subtract, mb, m_pe[pair])
                        m3 = AC(e_[:, :], e_[:, :], ACT.Exp, m1, m2)
                        m4 = TT(pool, hi(e_[:, :]), hi(e_[:, :]), hi(qf), ALU.mult, m3, *after)
                        m5 = TT(dve, lo(e_[:, :]), lo(e_[:, :]), lo(kf), ALU.mult, m3, *after)
                        kk_, qq_ = e_[:, :], e_[:, :]
                        wait = (m4, m5)
                    else:
                        kk_, qq_, wait = kf, qf, tuple(after)
                    for hh in range(MH):
                        hp, ti = hh % 2 * HD, hh // 2 * T
                        bk = bank[2 * pair + hh % 2]
                        if w < P:
                            for blk in range(NB):
                                o = bk[:, (hh // 2) * T + blk * P:(hh // 2) * T + (blk + 1) * P]
                                mm = MM(o, kk_[hp:hp + HD, ti + blk * P:ti + (blk + 1) * P],
                                        qq_[hp:hp + HD, ti + blk * P:ti + (blk + 1) * P], True, True,
                                        *wait, m_cp[pair])
                        else:
                            o = bk[:, (hh // 2) * P:(hh // 2 + 1) * P]
                            mm = MM(o, kk_[hp:hp + HD, ti:ti + P], qq_[hp:hp + HD, ti + P:ti + 2 * P],
                                    True, True, *wait, m_cp[pair])
                    m_pe[pair] = mm
                    for hb in range(2):
                        bk = bank[2 * pair + hb]
                        if w < P:
                            mask = (C(f"level{w}") if w else ident).bitcast(U32)
                            for hh in range(2):
                                src = bk[:, hh * T:(hh + 1) * T].rearrange("p (b t) -> p b t", b=NB)
                                ms = dve.step(lambda e, hb=hb, hh=hh, src=src, mask=mask: e.copy_predicated(
                                    sc[:, 2 * hh + hb, 0:3:2, :],
                                    mask.rearrange("p (b t) -> p b t", b=1).broadcast_to([P, NB, P]), src), mm, m_sc)
                        else:
                            src = bk[:, 0:2 * P].rearrange("p (h t) -> p h t", h=2)
                            ms = dve.step(lambda e, hb=hb, src=src: e.tensor_copy(
                                sc[:, hb:MH:2, 1, :], src), mm, m_sc)
                    m_cp[pair] = ms
                for hh in range(MH):
                    hp, ti = hh % 2 * HD, hh // 2
                    lh = lambda blk, hh=hh: tok[:, blk, hh * HD:(hh + 1) * HD]
                    MM(bank[5][hp:hp + HD, ti * T:(ti + 1) * T], lh(0),
                       sc[:, hh, 0:2, :].rearrange("p b t -> p (b t)"), True, False, ms, mv)
                    mo = MM(bank[5][hp:hp + HD, ti * T + P:(ti + 1) * T], lh(1), sc[:, hh, 2, :], False, True, ms)
                md = AC(dst, bank[5][:, :].rearrange("p (k t) -> p k t", k=2), ACT.Copy, mo)
                meet()
            return md

        names = []
        unit = outer.enter_context(env["nc"].sbuf_tensor("sb_unit", [P, T], F32))
        dve.wait(pool.step(lambda e: e.memset(unit[:, :], 1.0)))
        gate = sb("gate", [P, GT, T], ctx=outer)
        tmp = sb("tmp", [P, GT, T], ctx=outer)

        def ln_floor(dst, src, *after):
            big = float(2 ** 64)
            m1 = TS(dve, tmp[:, :, :], src, float(2.0 ** -50), big, ALU.is_lt, ALU.mult, *after)
            m2 = STT(src, tmp[:, :, :], 1.0, src, ALU.max, ALU.mult, m1)
            m3 = AC(dst, src, ACT.Ln, m2)
            return STT(dst, tmp[:, :, :], float(-64 * np.log(2.0) / big), dst, ALU.mult, ALU.add, m3)

        lbs = sb("lbs", [P, 6], ctx=outer)
        lg = env["vec"][:, VEC["hgrn_lb_logits"]:VEC["hgrn_lb_logits"] + GT]
        m0 = TT(dve, lbs[:, 0:2], lg, lg, ALU.subtract)
        m0 = AC(lbs[:, 0:2], lbs[:, 0:2], ACT.Exp, m0)
        m1 = dve.step(lambda e: e.reciprocal(lbs[:, 2:4], lbs[:, 0:2]), m0)
        m1 = TT(dve, lbs[:, 0:2], lbs[:, 0:2], lbs[:, 2:4], ALU.mult, m1)
        m1 = TT(dve, lbs[:, 4:6], lbs[:, 0:2], lbs[:, 0:2], ALU.subtract, m1)
        mlb = TS(dve, lbs[:, 2:4], lbs[:, 4:6], -1.0, 1.0, ALU.mult, ALU.add, m1)
        hq, hf, hi_, hg = (p[:, 2 * i:2 * i + 2, :] for i in (1, 2, 3, 4))
        mq = AC(hq, hq, ACT.Silu)
        mq = TS(dve, hq, hq, QK_SCALE, None, ALU.mult, None, mq)
        mf = AC(hf, hf, ACT.Sigmoid)
        for i in range(GT):
            mf = TS(dve, hf[:, i, :], hf[:, i, :], lbs[:, 2 + i:3 + i], lbs[:, 4 + i:5 + i], ALU.mult, ALU.add, mf, mlb)
        m1 = TS(dve, gate[:, :, :], hf, 1e-30, None, ALU.max, None, mf)
        mk = TS(dve, hf, hf, -1.0, 1.0, ALU.mult, ALU.add, m1)
        mg = ln_floor(gate[:, :, :], gate[:, :, :], m1)
        mhg = AC(hg, hg, ACT.Sigmoid)
        mo = gated_attention(hq, hf, gate[:, :, :], hi_, hq, mq, mk, mg)
        ms = square_sum(lambda k: hq[:, k, :], GT, bank[6][:, 0:T], mo)
        mr = inv_root(rstd[:, 0, :], bank[6][:, 0:T], 1.0 / G, EPS, ms)
        for i in range(GT):
            m1 = STT(hq[:, i, :], hq[:, i, :], V("hgrn_norm", i), rstd[:, 0, :], ALU.mult, ALU.mult, mr)
            m_hgrn = TT(dve, hq[:, i, :], hq[:, i, :], hg[:, i, :], ALU.mult, m1, mhg)

        def head_rstd(dst, src, scale, eps, *after):
            m = AC(tmp[:, :, :], src, ACT.Square, *after)
            for i in range(GT):
                m2 = MM(bank[6][:, i * T:(i + 1) * T], C("headsum"), tmp[:, i, :], True, True, m)
            return inv_root(dst, bank[6][:, :].rearrange("p (k t) -> p k t", k=2), scale, eps, m2)

        meet()
        gq, gk, gv, gg = (p[:, 18 + 2 * i:20 + 2 * i, :] for i in range(4))
        for i in range(GT):
            m1 = MM(bank[4][:, i * T:(i + 1) * T], gw2[:, i * P:(i + 1) * P], ga[:, :], True, True)
        for i in range(GT):
            m2 = TS(dve, gate[:, i, :], bank[4][:, i * T:(i + 1) * T], V("gla_b", i), None, ALU.add, None, m1)
        m3 = STT(tmp[:, :, :], gate[:, :, :], -1.0, gate[:, :, :], ALU.mult, ALU.min, m2)
        m4 = AC(tmp[:, :, :], tmp[:, :, :], ACT.Exp, m3)
        m4 = AC(tmp[:, :, :], tmp[:, :, :], ACT.Ln, m4, bias=1.0)
        m5 = STT(gate[:, :, :], gate[:, :, :], 0.0, tmp[:, :, :], ALU.min, ALU.subtract, m4)
        mg = TS(dve, gate[:, :, :], gate[:, :, :], 1.0 / 16.0, None, ALU.mult, None, m5)
        mq = TS(dve, gq, gq, QK_SCALE, None, ALU.mult, None)
        mgg = AC(gg, gg, ACT.Silu)
        mo = gated_attention(gq, gk, gate[:, :, :], gv, gq, mq, mg)
        mr = head_rstd(rstd[:, :, :], gq, 1.0 / HD, EPS, mo)
        for i in range(GT):
            m1 = STT(gq[:, i, :], gq[:, i, :], V("gla_norm", i), rstd[:, i, :], ALU.mult, ALU.mult, mr)
            m_gla = TT(dve, gq[:, i, :], gq[:, i, :], gg[:, i, :], ALU.mult, m1, mgg)
        meet()

        with ExitStack() as c3:
            rw = p[:, 10:18, :]
            cum = sb("rcum", [P, GT, T], ctx=c3)
            av = sb("rwkv_a", [P, GT, T], ctx=c3)
            bb = sb("rwkv_b", [P, GT, T], ctx=c3)
            qr = sb("qr", [P, GT, 2, T], ctx=c3)
            kp, bp, wi = (p[:, i:i + 2, :] for i in (20, 22, 24))
            sh = y[:, :, :]
            m1 = TT(dve, sh[:, :, 1:], rw[:, :, 0:T - 1], rw[:, :, 1:], ALU.subtract)
            m2 = TS(dve, sh[:, :, 0:1], rw[:, :, 0:1], -1.0, None, ALU.mult, None)
            for i in range(8):
                m3 = STT(rw[:, i, :], sh[:, i, :], V("rwkv_mu", i), rw[:, i, :], ALU.mult, ALU.add, m1, m2)
            r, k, v = (rw[:, 2 * i:2 * i + 2, :] for i in range(3))
            lo_in = rw[:, 6, :]
            m4 = AC(lo_in[0:64, :], lo_in[0:64, :], ACT.Tanh, m3)
            m5 = AC(rw[:, 7, :], rw[:, 7, :], ACT.Sigmoid, m3)
            for i in range(GT):
                m6 = MM(bank[0][:, i * T:(i + 1) * T], lora[:, 0, i * P:(i + 1) * P], lo_in, True, True, m4)
                m7 = MM(bank[1][:, i * T:(i + 1) * T], lora[:, 1, i * P:(i + 1) * P], lo_in, True, True, m4)
                m8 = MM(bank[2][:, i * T:(i + 1) * T], g2[:, i * P:(i + 1) * P], rw[:, 7, :], True, True, m5)
            for i in range(GT):
                m6 = AC(cum[:, i, :], bank[0][:, i * T:(i + 1) * T], ACT.Sigmoid, m6, bias=V("rwkv_w0", i))
                m7 = AC(av[:, i, :], bank[1][:, i * T:(i + 1) * T], ACT.Sigmoid, m7, bias=V("rwkv_a0", i))
            md = TS(dve, gate[:, :, :], cum[:, :, :], -float(np.exp(-0.5)), None, ALU.mult, None, m6)
            for i in range(GT):
                mc = dve.step(lambda e, i=i: e.tensor_tensor_scan(cum[:, i, :], C("chunkkeep"), gate[:, i, :], 0.0,
                                                                  ALU.mult, ALU.add), md)
            m_g = AC(y[:, 4:6, :], bank[2][:, :].rearrange("p (k t) -> p k t", k=2), ACT.Copy, m8, m3)
            for i in range(GT):
                m1 = TS(dve, bb[:, i, :], k[:, i, :], V("rwkv_k_k", i), None, ALU.mult, None, m3)
            m1 = AC(tmp[:, :, :], bb[:, :, :], ACT.Square, m1)
            for i in range(GT):
                m2 = MM(bank[6][:, i * T:(i + 1) * T], C("headsum"), tmp[:, i, :], True, True, m1)
            m2 = AC(rstd[:, :, :], bank[6][:, :].rearrange("p (k t) -> p k t", k=2), ACT.Sqrt, m2)
            m2 = TS(dve, rstd[:, :, :], rstd[:, :, :], 1e-12, None, ALU.max, None, m2)
            m2 = dve.step(lambda e: e.reciprocal(rstd[:, :, :], rstd[:, :, :]), m2)
            mkk = TT(dve, bb[:, :, :], bb[:, :, :], rstd[:, :, :], ALU.mult, m2)
            m1 = TS(dve, tmp[:, :, :], av[:, :, :], -1.0, None, ALU.add, None, m7, m2)
            for i in range(GT):
                m2 = TS(dve, tmp[:, i, :], tmp[:, i, :], V("rwkv_k_a", i), 1.0, ALU.mult, ALU.add, m1)
            mk = TT(dve, k, k, tmp[:, :, :], ALU.mult, m2)
            m1 = TT(dve, wi[:, :, :], cum[:, :, :], gate[:, :, :], ALU.subtract, mc)
            m1 = AC(wi[:, :, :], wi[:, :, :], ACT.Exp, m1)
            mq1 = TT(dve, qr[:, :, 0, :], bb[:, :, :], wi[:, :, :], ALU.mult, m1, mkk)
            mb = TT(dve, bb[:, :, :], bb[:, :, :], av[:, :, :], ALU.mult, mq1)
            m2 = AC(wi[:, :, :], cum[:, :, :], ACT.Exp, mq1)
            mq2 = TT(dve, qr[:, :, 1, :], r, wi[:, :, :], ALU.mult, m2)
            m3_ = AC(av[:, :, :], cum[:, :, :], ACT.Exp, mb, mc, scale=-1.0)
            mkp = TT(dve, kp[:, :, :], k, av[:, :, :], ALU.mult, m3_, mk)
            mbp = TT(dve, bp[:, :, :], bb[:, :, :], av[:, :, :], ALU.mult, m3_)
            c4 = cum[:, :, :].rearrange("p k (c t) -> p (k c) t", t=RCHUNK)
            g4 = gate[:, :, :].rearrange("p k (c t) -> p (k c) t", t=RCHUNK)
            end = c4[:, :, RCHUNK - 1:RCHUNK].broadcast_to([P, GT * NCH, RCHUNK])
            m1 = TT(dve, g4, end, c4, ALU.subtract, mc, mq1)
            m1 = AC(gate[:, :, :], gate[:, :, :], ACT.Exp, m1)
            kc, bc = y[:, 0:2, :], y[:, 2:4, :]
            mkc = TT(dve, kc, k, gate[:, :, :], ALU.mult, m1, mk)
            mbc = TT(dve, bc, bb[:, :, :], gate[:, :, :], ALU.mult, m1, mb)
            m1 = TT(dve, tmp[:, :, :], r, k, ALU.mult, mk)
            for i in range(GT):
                m2 = TS(dve, tmp[:, i, :], tmp[:, i, :], V("rwkv_r_k", i), None, ALU.mult, None, m1)
            for i in range(GT):
                m3_ = MM(bank[6][:, i * T:(i + 1) * T], C("headsum"), tmp[:, i, :], True, True, m2)
            m_bonus = TT(dve, r, bank[6][:, :].rearrange("p (k t) -> p k t", k=2), v, ALU.mult, m3_, mq2)

            kkt, kct, bct = (p[:, i:i + 2, :] for i in (4, 6, 8))
            mt = [to_tokens(qr[:, :, 0, :], kkt[:, :, :], 3, mq1),
                  to_tokens(kc, kct[:, :, :], 4, mkc),
                  to_tokens(bc, bct[:, :, :], 5, mbc),
                  to_tokens(v, tok[:, :, :], 6, m3, m_bonus)]
            meet()
            names4 = ("akt", "art", "abt", "arbt", "ab", "inv", "invt", "xx")
            spare = env["ada_raw"][:, :, :].rearrange("p k n -> p (k n)").rearrange("p (i n t) -> p i n t", n=4, t=P)
            akt, art, abt, arbt, ab, inv = (spare[:, i] for i in range(6))
            invt, xx = (sb("r_" + n, [P, 4, P], ctx=c3)[:, :, :] for n in names4[6:])
            yy = sb("yy", [P, 4, P], ctx=c3)
            st = sb("st", [P, NCH, HD], ctx=c3)
            mc_ = sb("mc", [P, NCH, HD], ctx=c3)
            qq = sb("qq", [P, T], ctx=c3)
            oo = sb("oo", [P, GT, T], ctx=c3)

            def bc4(z):
                return z.rearrange("p (n t) -> p n t", n=1).broadcast_to([P, 4, P])

            def b3(i):
                return bank[i][:, :].rearrange("p (n t) -> p n t", n=4)

            probs = [(hh, blk) for hh in range(2) for blk in range(NB)]
            for ti in range(GT):
                def hs(hh):
                    return slice(hh * HD, (hh + 1) * HD)
                m = [None]
                for n, (hh, blk) in enumerate(probs):
                    if n == 2:
                        pe.wait(m[-1])
                    ts = slice(blk * P, (blk + 1) * P)
                    s_ = slice(n * P, (n + 1) * P)
                    kk_c, r_c = qr[hs(hh), ti, 0, ts], qr[hs(hh), ti, 1, ts]
                    kp_c, bp_c = kp[hs(hh), ti, ts], bp[hs(hh), ti, ts]
                    m = [MM(bank[0][:, s_], bp_c, kk_c, True, True),
                         MM(bank[1][:, s_], kk_c, bp_c, True, True),
                         MM(bank[2][:, s_], kp_c, kk_c, True, True),
                         MM(bank[3][:, s_], kp_c, r_c, True, True),
                         MM(bank[4][:, s_], bp_c, r_c, True, True)]
                m_abt = TT(dve, abt[:, :, :], b3(0), bc4(C("before")), ALU.mult, m[-1])
                m_ab = TT(dve, ab[:, :, :], b3(1), bc4(C("after")), ALU.mult, m[-1])
                m_akt = TT(dve, akt[:, :, :], b3(2), bc4(C("before")), ALU.mult, m[-1])
                m_art = TT(dve, art[:, :, :], b3(3), bc4(C("upto")), ALU.mult, m[-1])
                m_arb = TT(dve, arbt[:, :, :], b3(4), bc4(C("upto")), ALU.mult, m[-1])
                for n, (hh, blk) in enumerate(probs):
                    mz = MM(bank[5][:, n * HD:(n + 1) * HD], akt[:, n, :],
                            tok[:, blk, ti * P + hh * HD:ti * P + (hh + 1) * HD], True, True, m_akt)
                m1 = TT(pool, xx[:, :, :], ab[:, :, :], bc4(C("levelT1")), ALU.mult, m_ab)
                m1 = TT(pool, inv[:, :, :], bc4(ident), xx[:, :, :], ALU.subtract, m1)
                m2 = TT(pool, xx[:, :, :], abt[:, :, :], bc4(C("level1")), ALU.mult, m_abt, m1)
                m2 = TT(pool, invt[:, :, :], bc4(ident), xx[:, :, :], ALU.subtract, m2)
                m_i, m_it, m_free = m1, m2, m2
                lev = {}
                for w in (2, 4, 8, 16, 32):
                    if w == 2:
                        ml = TT(pool, akt[:, :, :], abt[:, :, :], bc4(C("level2")), ALU.mult, m_abt, mz)
                    for n in range(4):
                        mx = MM(bank[0][:, n * P:(n + 1) * P], akt[:, n, :], inv[:, n, :], True, True, ml, m_i, m_abt)
                    if w < 32:
                        ml = TT(pool, akt[:, :, :], abt[:, :, :], bc4(C(f"level{2 * w}")), ALU.mult, mx)
                    mx = AC(xx[:, :, :], b3(0), ACT.Copy, mx, m_it)
                    for n in range(4):
                        ma = MM(bank[1][:, n * P:(n + 1) * P], invt[:, n, :], xx[:, n, :], True, True, mx, m_it, m_ab)
                    for n in range(4):
                        mb_ = MM(bank[2][:, n * P:(n + 1) * P], xx[:, n, :], invt[:, n, :], True, True, mx, m_it, m_akt)
                    m_i = TT(dve, inv[:, :, :], inv[:, :, :], b3(1), ALU.subtract, ma)
                    m_it = TT(dve, invt[:, :, :], invt[:, :, :], b3(2), ALU.subtract, mb_)
                for n, (hh, blk) in enumerate(probs):
                    cs = slice(ti * P + hh * HD, ti * P + (hh + 1) * HD)
                    m1 = dve.step(lambda e, n=n, blk=blk, cs=cs: e.tensor_copy(xx[:, n, 0:HD], kkt[:, blk, cs]), mb_)
                    m2 = dve.step(lambda e, n=n: e.tensor_copy(xx[:, n, HD:P], bank[5][:, n * HD:(n + 1) * HD]), mz, mb_)
                for n in range(4):
                    m3_ = MM(bank[0][:, n * P:(n + 1) * P], invt[:, n, :], xx[:, n, :], True, True, m2, m_it)
                my = TS(dve, yy[:, :, :], b3(0), -1.0, None, ALU.mult, None, m3_)
                for n, (hh, blk) in enumerate(probs):
                    ts = slice(blk * P, (blk + 1) * P)
                    vs = tok[:, blk, ti * P + hh * HD:ti * P + (hh + 1) * HD]
                    mq_ = MM(bank[1][hs(hh), ts], yy[:, n, 0:HD], arbt[:, n, :], True, True, my, m_i)
                    MM(bank[2][hs(hh), ts], yy[:, n, HD:P], arbt[:, n, :], True, False, my, m_it)
                    mo_ = MM(bank[2][hs(hh), ts], vs, art[:, n, :], False, True)
                mqq = TT(dve, qq[:, :], bank[1][:, 0:T], qr[:, ti, 1, :], ALU.add, mq_)
                for c in (0, 2, 1):
                    if c == 1:
                        pe.wait(m2)
                    for hh in range(2):
                        blk, rs = c // 2, slice(c % 2 * 64, c % 2 * 64 + 64)
                        n = hh * NB + blk
                        cs = slice(ti * P + hh * HD, ti * P + (hh + 1) * HD)
                        o1 = bank[3][hs(hh), c * HD:(c + 1) * HD]
                        o2 = bank[4][hs(hh), c * HD:(c + 1) * HD]
                        m1 = MM(o1, yy[rs, n, 0:HD], bct[rs, blk, cs], True, True, my)
                        MM(o2, kct[rs, blk, cs], tok[rs, blk, cs], True, False)
                        m2 = MM(o2, bct[rs, blk, cs], yy[rs, n, HD:P], False, True)
                for c in range(NCH - 1):
                    for hh in range(2):
                        e0 = c * RCHUNK + RCHUNK - 1
                        m3_ = STT(mc_[hs(hh), c, :], C("ident")[hs(hh), hh * HD:(hh + 1) * HD],
                                  wi[hs(hh), ti, e0:e0 + 1], bank[3][hs(hh), c * HD:(c + 1) * HD],
                                  ALU.mult, ALU.add, m1)
                ms_ = dve.step(lambda e: e.tensor_copy(
                    st[:, 1:, :], bank[4][:, 0:(NCH - 1) * HD].rearrange("p (c v) -> p c v", v=HD)), m2)
                for c in (1, 2):
                    for hh in range(2):
                        mm_ = MM(bank[0][hs(hh), c * HD:(c + 1) * HD], mc_[hs(hh), c, :], st[hs(hh), c, :],
                                 True, True, ms_, m3_, my)
                    ms_ = TT(dve, st[:, c + 1, :], bank[0][:, c * HD:(c + 1) * HD], st[:, c + 1, :], ALU.add, mm_)
                for c in range(1, NCH):
                    for hh in range(2):
                        mm_ = MM(bank[6][hs(hh), c * RCHUNK:(c + 1) * RCHUNK], st[hs(hh), c, :],
                                 qq[hs(hh), c * RCHUNK:(c + 1) * RCHUNK], True, True, ms_, mqq)
                m1 = AC(oo[:, ti, :], bank[2][:, 0:T], ACT.Copy, mo_)
                m2 = TT(dve, oo[:, ti, RCHUNK:], bank[6][:, RCHUNK:T], oo[:, ti, RCHUNK:], ALU.add, m1, mm_)
                meet()

            for i in range(GT):
                m1 = MM(bank[0][:, i * T:(i + 1) * T], C("headsum"), oo[:, i, :], True, True, m2)
            m1 = STT(oo[:, :, :], bank[0][:, :].rearrange("p (k t) -> p k t", k=2), -1.0 / HD, oo[:, :, :],
                     ALU.mult, ALU.add, m1)
            mr = head_rstd(rstd[:, :, :], oo[:, :, :], 1.0 / HD, GN_EPS, m1)
            for i in range(GT):
                m1 = STT(oo[:, i, :], oo[:, i, :], V("rwkv_ln_w", i), rstd[:, i, :], ALU.mult, ALU.mult, mr)
                m1 = STT(oo[:, i, :], oo[:, i, :], V("rwkv_ln_b", i), r[:, i, :], ALU.add, ALU.add, m1)
                m_rwkv = TT(dve, r[:, i, :], oo[:, i, :], y[:, 4 + i, :], ALU.mult, m1)
            meet()

        for j, t0 in enumerate((0, 2, 10, 18)):
            m = dve.step(lambda e, j=j, t0=t0: e.tensor_copy(y[:, 2 * j:2 * j + 2, :], p[:, t0:t0 + 2, :]))
        m = env["split_xn"](m)
        m = linear([(w, "channels") for w in env["chunks"]["w_out"]], env["add_chunks"](None), m, env["first"]["ffn2"])
        meet()
    return [z for z in m for _ in range(2)]


def backwards(ap):
    step, n = ap.ap[-1]
    return bass.AP(tensor=ap.tensor, offset=ap.offset + step * (n - 1), ap=[*ap.ap[:-1], [-step, n]])


def attend(env, ctx, tag, scores, values, scale, bias, m_ready, order=None):
    sb, bank, pe, act, dve, pool = (env[n] for n in ("sb", "bank", "pe", "act", "dve", "pool"))
    ident, y = env["ident"], env["xn"]
    s = [env["h"], env["sil"], sb(f"s2_{tag}", [P, NB, T], ctx=ctx)]
    pt = [env["rstd"], sb(f"pt_{tag}", [P, NB, T], ctx=ctx)]
    mx = sb(f"mx_{tag}", [P, AH, 4], ctx=ctx)
    m_exp, m_nrm, m_pv, m_tr, m_out = {}, {}, {}, {}, {}
    m_sread, m_tread = {}, {}

    def softmax(i):
        sb_, bk = s[i % 3], bank[i % 2]
        for q in range(NB):
            m = pe.step(lambda e, q=q: e.matmul(bk[:, q * T:(q + 1) * T], *scores(i, q), start=True, stop=True),
                        *m_ready, m_sread.get(i - 2))
        if bias is not None:
            for q in range(NB):
                m1 = dve.step(lambda e, q=q: e.tensor_tensor_reduce(
                    sb_[:, q, :], bk[:, q * T:(q + 1) * T], bias[:, q, i, :], 1.0, -3e38, ALU.add, ALU.max,
                    mx[:, i, q:q + 1]), m, m_tr.get(i - 3))
            src = sb_[:, :, :]
        else:
            src = bk[:, :].rearrange("p (q t) -> p q t", q=NB)
            m1 = dve.step(lambda e: e.reduce_max(mx[:, i, 0:2], src, AX_X), m)
        m1 = dve.step(lambda e: e.tensor_scalar(mx[:, i, 0:2], mx[:, i, 0:2], -scale, None, ALU.mult), m1)
        m_sread[i] = m1
        for q in range(NB):
            m2 = act.step(lambda e, q=q: e.activation(sb_[:, q, :], src[:, q, :], ACT.Exp, bias=mx[:, i, q:q + 1],
                                                      scale=scale, accum_out=mx[:, i, 2 + q:3 + q]),
                          m1, m_tr.get(i - 3))
        if bias is None:
            m_sread[i] = m2
        m3 = dve.step(lambda e: e.reciprocal(mx[:, i, 2:4], mx[:, i, 2:4]), m2)
        for q in range(NB):
            m3 = pool.step(lambda e, q=q: e.tensor_scalar(sb_[:, q, :], sb_[:, q, :], mx[:, i, 2 + q:3 + q], None,
                                                          ALU.mult), m3)
        m_nrm[i] = m3

    def transposed(i):
        bk = bank[2 + i % 2]
        for kb in range(NB):
            for q in range(NB):
                m = pe.step(lambda e, kb=kb, q=q: e.transpose(bk[:, kb * T + q * P:kb * T + (q + 1) * P],
                                                              s[i % 3][:, q, kb * P:(kb + 1) * P], ident),
                            m_nrm[i], m_tread.get(i - 2))
        m_tr[i] = m
        m_tread[i] = dve.step(lambda e: e.tensor_copy(pt[i % 2][:, :, :], bk[:, :].rearrange("p (k q) -> p k q", k=NB)),
                              m, m_pv.get(i - 2))

    def weigh(i):
        hp, bk = i % 2 * HD, bank[4 + i // 2 % 2]
        for kb in range(NB):
            m = pe.step(lambda e, kb=kb: e.matmul(bk[hp:hp + HD, 0:T], values(i, kb), pt[i % 2][:, kb, :],
                                                  start=kb == 0, stop=kb == NB - 1), m_tread[i], m_out.get(i // 2 - 2))
        m_pv[i] = m
        if i % 2:
            dst, src = y[:, i // 2, :], bk[:, 0:T]
            if order is not None:
                dst, src = order(dst), src.rearrange("p (r c) -> p r c", c=GRID)
            m_out[i // 2] = act.step(lambda e: e.activation(dst, src, ACT.Copy), m)

    for i in range(AH + 2):
        if i < AH:
            softmax(i)
        if 0 <= i - 1 < AH:
            transposed(i - 1)
        if 0 <= i - 2 < AH:
            weigh(i - 2)
    return [m_out[i] for i in range(AH // 2)]


def neighbourhood(env, gate, m_in):
    a, sb, bank, act, dve, pool = (env[n] for n in ("a", "sb", "bank", "act", "dve", "pool"))
    dma, meet, linear = (env[n] for n in ("dma", "meet", "linear"))
    assert ROWS <= WIN_H
    (_, _), (_, att) = shape_constants()
    with ExitStack() as ctx:
        marks = env["scratch_free"][0]
        q = sb("na_q", [P, 8, T], ctx=ctx)
        k = sb("na_k", [P, 8, T], ctx=ctx)
        v = sb("na_v", [P, NB, D], ctx=ctx)
        bias = sb("na_bias", [P, NB, AH, ROWS, GRID], ctx=ctx)
        win = sb("na_win", [P, GRID], ctx=ctx)
        rpb = a["rpb"]
        width = 2 * GRID - 1
        got = []
        for qr in range(ROWS):
            for kr in range(ROWS):
                src = bass.AP(tensor=rpb.tensor, offset=rpb.offset + (WIN_H - 1 + kr - qr) * width,
                              ap=[[1, GRID], [(2 * WIN_H - 1) * width, AH], [1, GRID]])
                got.append(dma(pool, bias[qr % 2 * GRID:(qr % 2 + 1) * GRID, qr // 2, :, kr, :], src,
                               f"bias{qr}{kr}", *marks))
        at = att["window"][0]
        got.append(dma(pool, win[:, :], a["att"][:, at:at + GRID], "window", *marks))
        for b in range(NB):
            for j in range(AH):
                m_b = pool.step(lambda e, b=b, j=j: e.tensor_tensor(
                    bias[:, b, j], bias[:, b, j],
                    win[:, :].rearrange("p (r c) -> p r c", r=1).broadcast_to([P, ROWS, GRID]), ALU.add), *got)

        def evac_qk(c, b, m):
            dst = (q if c < 4 else k)[:, 2 * (c % 4):2 * (c % 4) + 2, :]
            src = b[:, :].rearrange("p (k t) -> p k t", k=2)
            if c < 4:
                dst, src = backwards(dst.rearrange("p k (r c) -> p (k r) c", c=GRID)), \
                    src.rearrange("p k (r c) -> p (k r) c", c=GRID)
            return dve.step(lambda e: e.tensor_scalar(dst, src, QK_SCALE if c < 4 else 1.0, None, ALU.mult), m)

        def evac_v(c, b, m):
            dst = v[:, :, c * CW:(c + 1) * CW]
            return act.step(lambda e: e.activation(dst, b[:, :].rearrange("p (b n) -> p b n", b=NB), ACT.Copy), m)

        ch = env["chunks"]
        m1 = linear([(w, "channels") for w in ch["na_qk"]] + [(w, "tokens") for w in ch["na_v"]],
                    lambda c, b, m: evac_qk(c, b, m) if c < 8 else evac_v(c - 8, b, m), m_in, ch["na_o"][:2])
        meet()

        def scores(i, qb):
            hp = i % 2 * HD
            return q[hp:hp + HD, i // 2, qb * P:(qb + 1) * P], k[hp:hp + HD, i // 2, :]

        m = attend(env, ctx, "na", scores, lambda i, kb: v[:, kb, i * HD:(i + 1) * HD], 1.0,
                   bias[:, :, :, :, :].rearrange("p b h r c -> p b h (r c)"), [*m1, m_b],
                   lambda z: backwards(z.rearrange("p (r c) -> p r c", c=GRID)))
        m = env["split_xn"](m)
        m = linear([(w, "channels") for w in ch["na_o"]], env["add_chunks"](gate), m, env["first"]["ffn3"])
        meet()
    return [z for z in m for _ in range(2)]


def latent(env, gate, m_in):
    a, sb, bank, pe, act, dve, pool = (env[n] for n in ("a", "sb", "bank", "pe", "act", "dve", "pool"))
    dma, meet, linear, V, y = (env[n] for n in ("dma", "meet", "linear", "V", "xn"))
    square_sum, inv_root, rstd = (env[n] for n in ("square_sum", "inv_root", "rstd"))
    (_, _), (_, att) = shape_constants()
    with ExitStack() as ctx:
        marks = env["scratch_free"][0]
        tab = sb("tab", [P, sum(n for _, n in att.values())], ctx=ctx)
        wukv = sb("wukv", [P, AH * 2 * HD], ctx=ctx)
        v = sb("mla_v", [P, NB, D], ctx=ctx)
        lat = sb("lat", [P, 3, T], ctx=ctx)
        kr = sb("kr", [P, T], ctx=ctx)
        wuq = env["ada_raw"][:, :, :].rearrange("p k n -> p (k n)").rearrange("p (k n) -> p k n", k=2)

        def A(name, n=None, p0=0, p1=P):
            at, w = att[name]
            return tab[p0:p1, at:at + (n or w)]

        rp = slice(HD, QH)
        with ExitStack() as c1:
            wd = sb("wd", [P, KT, QL + P + ROPE], ctx=c1)
            gd = dma(pool, wd[:, :, :], a["mla_down"], "down", *marks)
            got = [dma(pool, tab[:, :], a["att"], "tab"), dma(pool, wukv[:, :], a["mla_ukv"], "ukv"),
                   dma(pool, wuq, a["mla_uq"], "uq", (env["s_ada"], ADA_UNITS + 1))]
            outs = [(bank[0][:, 0:T], 0, P), (bank[0][:, T:2 * T], P, P), (bank[1][:, 0:T], 2 * P, P),
                    (bank[2][0:ROPE, 0:T], 3 * P, ROPE)]
            for o, at, n in outs:
                for k_ in range(KT):
                    m = pe.step(lambda e, o=o, at=at, n=n, k_=k_: e.matmul(
                        o, wd[:, k_, at:at + n], y[:, k_, :], start=k_ == 0, stop=k_ == KT - 1), gd, m_in[-1])
            m1 = act.step(lambda e: e.activation(lat[:, 0:2, :], bank[0][:, :].rearrange("p (k t) -> p k t", k=2),
                                                 ACT.Copy), m)
            m2 = act.step(lambda e: e.activation(lat[:, 2, :], bank[1][:, 0:T], ACT.Copy), m)
            m3 = dve.step(lambda e: e.tensor_copy(kr[0:ROPE, :], bank[2][0:ROPE, 0:T]), m)
            meet()
        for l in (pe, dve, act, pool):
            l.wait(*got)
        ms = square_sum(lambda k_: lat[:, k_, :], 2, bank[3][:, 0:T], m1)
        mr = inv_root(rstd[:, 0, :], bank[3][:, 0:T], 1.0 / QL, EPS, ms)
        for i in range(2):
            m_cq = dve.step(lambda e, i=i: e.scalar_tensor_tensor(lat[:, i, :], lat[:, i, :], V("mla_q_norm_2", i),
                                                                  rstd[:, 0, :], ALU.mult, ALU.mult), mr)
        ms = square_sum(lambda k_: lat[:, 2, :], 1, bank[3][:, T:2 * T], m2, mr)
        mr = inv_root(rstd[:, 1, :], bank[3][:, T:2 * T], 1.0 / P, EPS, ms)
        m_ckv = dve.step(lambda e: e.scalar_tensor_tensor(lat[:, 2, :], lat[:, 2, :], V("mla_kv_norm_2"),
                                                          rstd[:, 1, :], ALU.mult, ALU.mult), mr)
        q = sb("mla_q", [P, AH, T], ctx=ctx)
        k = sb("mla_k", [P, AH, T], ctx=ctx)
        pe.step(lambda e: e.matmul(bank[2][0:QH, 0:T], A("place", QH, 0, ROPE), kr[0:ROPE, :], start=True, stop=True), m3)
        m = pe.step(lambda e: e.matmul(bank[2][0:QH, T:2 * T], A("placeturn", QH, 0, ROPE), kr[0:ROPE, :],
                                       start=True, stop=True))
        m1 = dve.step(lambda e: e.tensor_tensor(kr[rp, :], bank[2][rp, 0:T], A("cos", None, HD, QH), ALU.mult), m)
        m2 = dve.step(lambda e: e.tensor_tensor(k[rp, 0, :], bank[2][rp, T:2 * T], A("sin", None, HD, QH), ALU.mult), m)
        m1 = dve.step(lambda e: e.tensor_tensor(kr[rp, :], kr[rp, :], k[rp, 0, :], ALU.add), m1, m2)
        m_kr = pool.step(lambda e: e.tensor_copy(k[rp, :, :], kr[rp, :].rearrange("p (n t) -> p n t", n=1)
                                                 .broadcast_to([ROPE, AH, T])), m1)
        vcols = wukv[:, :].rearrange("p (h n) -> p h n", n=2 * HD)
        prev = []
        for b in range(NB):
            for hf in range(2):
                bk = bank[4 + hf]
                m = pe.step(lambda e, b=b, hf=hf, bk=bk: e.matmul(
                    bk[:, :], lat[:, 2, b * P:(b + 1) * P], vcols[:, 8 * hf:8 * hf + 8, HD:2 * HD],
                    start=True, stop=True), m_ckv, *prev)
                m_v = act.step(lambda e, b=b, hf=hf, bk=bk: e.activation(v[:, b, hf * 512:(hf + 1) * 512], bk[:, :],
                                                                         ACT.Copy), m)
                if hf:
                    prev = [m_v]
        mk_, mq_, mt_ = {}, {}, {}
        meet()
        for i in range(AH // 2):
            kb, qb, tb = bank[0 + i % 2], bank[2 + i % 2], bank[4 + i % 2]
            for j in range(2):
                hh = 2 * i + j
                m = pe.step(lambda e, hh=hh, j=j, kb=kb: e.matmul(
                    kb[0:HD, j * T:(j + 1) * T], vcols[:, hh, 0:HD], lat[:, 2, :], start=True, stop=True), mk_.get(i - 2))
            mk_[i] = act.step(lambda e, i=i, kb=kb: e.activation(
                k[0:HD, 2 * i:2 * i + 2, :], kb[0:HD, :].rearrange("p (h t) -> p h t", h=2), ACT.Copy), m)
            for j in range(2):
                hh = 2 * i + j
                for kt in range(2):
                    m = pe.step(lambda e, hh=hh, j=j, kt=kt, qb=qb: e.matmul(
                        qb[0:QH, j * T:(j + 1) * T], wuq[:, kt, hh * QH:(hh + 1) * QH], lat[:, kt, :],
                        start=kt == 0, stop=kt == 1), m_cq, mq_.get(i - 2))
            qs = q[:, 2 * i:2 * i + 2, :]
            mq_[i] = act.step(lambda e, qs=qs, qb=qb: e.activation(
                qs[0:QH], qb[0:QH, :].rearrange("p (h t) -> p h t", h=2), ACT.Copy), m)
            m = pe.step(lambda e, qs=qs, tb=tb: e.matmul(tb[0:QH, :], A("turn", QH, 0, QH), qs[0:QH],
                                                         start=True, stop=True), mq_[i], mt_.get(i - 2))
            two = lambda z: z.rearrange("p (n t) -> p n t", n=1).broadcast_to([ROPE, 2, T])
            m1 = pool.step(lambda e, qs=qs: e.tensor_tensor(qs[rp], qs[rp], two(A("cos", None, HD, QH)), ALU.mult), m)
            m2 = dve.step(lambda e, tb=tb, i=i: e.tensor_tensor(
                env["h"][rp, :, :], tb[rp, :].rearrange("p (h t) -> p h t", h=2), two(A("sin", None, HD, QH)),
                ALU.mult), m, mt_.get(i - 1))
            mt_[i] = dve.step(lambda e, qs=qs: e.tensor_tensor(qs[rp], qs[rp], env["h"][rp, :, :], ALU.add), m1, m2)
        meet()
        m = attend(env, ctx, "mla", lambda i, qb: (q[0:QH, i, qb * P:(qb + 1) * P], k[0:QH, i, :]),
                   lambda i, kb: v[:, kb, i * HD:(i + 1) * HD], float(QH) ** -0.5, None, [m_kr, m_v])
        m = env["split_xn"](m)
        m = linear([(w, "channels") for w in env["chunks"]["mla_o"]], env["add_chunks"](gate), m, env["first"]["moe"])
        meet()
    return [z for z in m for _ in range(2)]


def router(env, ctx, m_in):
    a, sb, bank, pe, act, dve, pool = (env[n] for n in ("a", "sb", "bank", "pe", "act", "dve", "pool"))
    dma, meet, C, ident, xn = (env[n] for n in ("dma", "meet", "C", "ident", "xn"))
    E = EXPERTS
    marks = env["scratch_free"][0]
    comb = sb("comb", [P, E, T], ctx=ctx)
    wr = sb("wr", [P, KT, E], ctx=ctx)
    pr = sb("pr", [P, NB, E], ctx=ctx)
    st = sb("rst", [P, NB], ctx=ctx)
    gt = sb("rgt", [P, NB, E, E], ctx=ctx)
    eq = sb("req", [P, NB, E, E], ctx=ctx)
    got = dma(pool, wr[:, :, :], a["router"], "router", *marks)
    for b in range(NB):
        for k in range(KT):
            m = pe.step(lambda e, b=b, k=k: e.matmul(bank[0][:, b * E:(b + 1) * E], xn[:, k, b * P:(b + 1) * P],
                                                     wr[:, k, :], start=k == 0, stop=k == KT - 1), got, m_in)
    m = dve.step(lambda e: e.tensor_copy(pr[:, :, :], bank[0][:, 0:NB * E].rearrange("p (b e) -> p b e", b=NB)), m)
    wide = lambda z: z.rearrange("p (b n) -> p b n", n=1).broadcast_to([P, NB, E])

    def TT(o, i0, i1, op, *after):
        return dve.step(lambda e: e.tensor_tensor(o, i0, i1, op), *after)

    m = dve.step(lambda e: e.reduce_max(st[:, :], pr[:, :, :], AX_X), m)
    m = TT(pr[:, :, :], pr[:, :, :], wide(st[:, :]), ALU.subtract, m)
    m = act.step(lambda e: e.activation(pr[:, :, :], pr[:, :, :], ACT.Exp), m)

    def normalise(m):
        m = dve.step(lambda e: e.reduce_sum(st[:, :], pr[:, :, :], AX_X), m)
        m = dve.step(lambda e: e.reciprocal(st[:, :], st[:, :]), m)
        return TT(pr[:, :, :], pr[:, :, :], wide(st[:, :]), ALU.mult, m)

    m = normalise(m)
    for b in range(NB):
        other = pr[:, b, :].rearrange("p (n j) -> p n j", n=1).broadcast_to([P, E, E])
        own = pr[:, b, :].rearrange("p (j n) -> p j n", n=1).broadcast_to([P, E, E])
        m1 = TT(gt[:, b], other, own, ALU.is_gt, m)
        m2 = TT(eq[:, b], other, own, ALU.is_equal, m)
        m2 = TT(eq[:, b], eq[:, b], C("earlier").rearrange("p (e j) -> p e j", e=E), ALU.mult, m2)
        m3 = TT(gt[:, b], gt[:, b], eq[:, b], ALU.add, m1, m2)
        m4 = dve.step(lambda e, b=b: e.reduce_sum(eq[:, b, 0, :], gt[:, b], AX_X), m3)
        m5 = dve.step(lambda e, b=b: e.tensor_scalar(eq[:, b, 0, :], eq[:, b, 0, :], 1.5, None, ALU.is_lt), m4)
        ml = TT(pr[:, b, :], pr[:, b, :], eq[:, b, 0, :], ALU.mult, m5)
    m = normalise(ml)
    for i in range(E):
        bk = bank[1 + i // 2 % 4]
        for b in range(NB):
            mm = pe.step(lambda e, i=i, b=b, bk=bk: e.matmul(
                bk[:, (i % 2) * T + b * P:(i % 2) * T + (b + 1) * P],
                pr[:, b, i:i + 1].broadcast_to([P, P]), ident, start=True, stop=True), m)
        if i % 2:
            mc = dve.step(lambda e, i=i, bk=bk: e.tensor_copy(
                comb[:, i - 1:i + 1, :], bk[:, :].rearrange("p (k t) -> p k t", k=2)), mm)
    meet()
    return comb, mc


def column_chunks(w):
    return w.reshape(KT, P, -1, CW).transpose(2, 1, 0, 3).reshape(-1, P, CHUNK)


def ffn_chunks(w_in, w_out):
    f = w_out.shape[0]
    down = w_out.reshape(f // CW, 2, P, D).transpose(0, 2, 1, 3).reshape(-1, P, CHUNK)
    return np.stack([column_chunks(w_in[:, :f]), column_chunks(w_in[:, f:]), down], axis=1)


def layout(inp):
    g = {k: np.asarray(v) for k, v in inp.items()}
    (main, _), (att, _) = shape_constants()
    tiles = lambda w: w.reshape(-1, P, w.shape[-1]).transpose(1, 0, 2)
    vec = np.concatenate([g[n].reshape(-1, P).T for n, _ in VECTORS], axis=1)
    w_in = g["w_in"][0]
    qkv = g["na_w_qkv_2"][0]
    ada = g["w_ada_2"].reshape(2, KT, P, 6 * D // ADA_W, ADA_W).transpose(0, 3, 2, 1, 4)
    moe_in, moe_out = g["moe_w_gu_2"][0], g["moe_w_down_2"][0]
    return {
        "x": tiles(g["x"][0].T), "vec": vec, "cst": main, "att": att,
        "ffn1": ffn_chunks(g["ffn1_w_in"][0], g["ffn1_w_out"][0]),
        "ffn2": ffn_chunks(g["ffn2_w_in"][0], g["ffn2_w_out"][0]),
        "ffn3": ffn_chunks(g["ffn_w_gu_2"][0], g["ffn_w_down_2"][0]),
        "moe": np.concatenate([ffn_chunks(moe_in[e], moe_out[e]) for e in range(EXPERTS)]),
        "ada": ada.reshape(ADA_UNITS, P, KT, ADA_W),
        "w_in": column_chunks(w_in[:, :MIX_TILES * P]), "w_in_ga": tiles(w_in[:, MIX_TILES * P:]),
        "w_out": column_chunks(g["w_out"][0]),
        "rwkv_w2": g["rwkv_w2"][0], "rwkv_a2": g["rwkv_a2"][0], "rwkv_g2": g["rwkv_g2"][0],
        "gla_w2": g["gla_w2"][0], "pool_w": g["pool_w"][0],
        "na_qk": column_chunks(qkv[:, :2 * D]), "na_v": column_chunks(qkv[:, 2 * D:]),
        "na_o": column_chunks(g["na_w_o_2"][0]),
        "rpb": np.pad(g["na_rpb_2"][0], ((0, 0), (0, 0), (GRID - WIN_W, GRID - WIN_W))),
        "mla_down": tiles(g["mla_w_down_2"][0]), "mla_uq": tiles(g["mla_w_uq_2"][0]),
        "mla_ukv": g["mla_w_ukv_2"][0], "mla_o": column_chunks(g["mla_w_o_2"][0]),
        "router": tiles(g["moe_w_router_2"][0]),
    }


def kernel(**inputs):
    import concourse.bacc as bacc
    from concourse.bass_utils import run_bass_kernel_spmd

    nc = bacc.Bacc("TRN2", target_bir_lowering=False, num_devices=1)
    arrays = {"in_" + k: np.ascontiguousarray(v) for k, v in layout(inputs).items()}
    aps = {k[3:]: nc.dram_tensor(k, v.shape, mybir.dt.from_np(v.dtype), kind="ExternalInput").ap()
           for k, v in arrays.items()}
    out = nc.dram_tensor("out", (P, KT, T), F32, kind="ExternalOutput").ap()
    build_program(nc, aps, out)
    r = run_bass_kernel_spmd(nc, [arrays], core_ids=[0])
    got = r.results[0]["out"]
    return np.ascontiguousarray(got.transpose(2, 1, 0).reshape(1, T, D))
```

```python
from itertools import zip_longest
from contextlib import ExitStack

import numpy as np
import concourse.bass as bass
from concourse import mybir

F32 = mybir.dt.float32
F32R = mybir.dt.float32r
BF16 = mybir.dt.bfloat16
U32 = mybir.dt.uint32
ALU = mybir.AluOpType
ACT = mybir.ActivationFunctionType
AX_X = mybir.AxisListType.X

P = 128
T = 256
D = 1024
KT = D // P
NB = T // P
CW = 256
CHUNK = KT * CW
FFN_UNITS = 2816 // CW
EXPERTS = 8
EXPERT_UNITS = 1792 // CW
SLOTS = P
G = 256
GT = G // P
HD = 64
MH = G // HD
RCHUNK = 64
NCH = T // RCHUNK
MIX_TILES = 26
GLA_LORA = 16
ADA_W = 384
ADA_UNITS = 2 * 6 * D // ADA_W
MODS = 6 * KT
AH = 16
GRID = 64
ROWS = T // GRID
WIN_H, WIN_W = 8, 16
QL, ROPE, QH = 256, 32, 96
EPS = 1e-6
GN_EPS = 64e-5
QK_SCALE = HD ** -0.5
NEG = -1e30

VECTORS = [
    ("norm_ffn1", KT), ("norm_mix", KT), ("norm_ffn2", KT), ("norm_final", KT), ("pool_b", GT),
    ("pool_scale", GT), ("hgrn_lb_logits", GT), ("hgrn_norm", GT), ("rwkv_mu", 8), ("rwkv_w0", GT),
    ("rwkv_a0", GT), ("rwkv_k_k", GT), ("rwkv_k_a", GT), ("rwkv_r_k", GT), ("rwkv_ln_w", GT),
    ("rwkv_ln_b", GT), ("gla_b", GT), ("gla_norm", GT), ("c_2", KT), ("b_ada_2", 2 * MODS),
    ("mla_q_norm_2", GT), ("mla_kv_norm_2", 1), ("final_norm_2", KT),
]
NVEC = sum(n for _, n in VECTORS)
VEC = {}
for _name, _n in VECTORS:
    VEC[_name] = sum(VECTORS[i][1] for i in range(len(VEC)))


def shape_constants():
    s, t = np.arange(P)[:, None], np.arange(P)[None, :]
    main = {"ident": s == t, "ones": np.ones((P, P)), "headsum": s // HD == t // HD}
    same = s // RCHUNK == t // RCHUNK
    main["before"] = same & (s < t)
    main["upto"] = same & (s <= t)
    main["after"] = same & (s > t)
    for m in (1, 2, 4, 8, 16, 32, 64):
        pair = (s // (2 * m) == t // (2 * m)) & (s // m % 2 == 0) & (t // m % 2 == 1)
        main[f"level{m}"] = pair
        if m < RCHUNK:
            main[f"levelT{m}"] = pair.T
    w = np.array([2, 4, 8, 16])[(np.arange(GT)[None, :] * 2 + np.arange(P)[:, None] // 64)]
    count = np.minimum(np.arange(T)[None, None, :] + 1, w[:, :, None])
    main["invcount"] = (np.float32(1) / count.astype(np.float32)).reshape(P, GT * T)
    e = np.arange(EXPERTS)
    main["earlier"] = np.broadcast_to((e[None, :] < e[:, None]).reshape(1, -1), (P, EXPERTS * EXPERTS))
    main["slot"] = s + 1.0
    main["chunkkeep"] = np.broadcast_to((np.arange(T) % RCHUNK != 0)[None, :], (P, T))
    q, k = GRID - 1 - np.arange(P)[:, None] % GRID, np.arange(GRID)[None, :]
    first = np.clip(q - WIN_W // 2, 0, GRID - WIN_W)
    attn = {"window": np.where((k >= first) & (k < first + WIN_W), 0.0, NEG)}
    n = ROPE // 4
    inv = (np.float32(10000.0) ** (-np.arange(n, dtype=np.float32) / np.float32(n))).astype(np.float32)
    pos = np.arange(T)
    ang = np.concatenate([(pos // GRID).astype(np.float32)[:, None] * inv,
                          (pos % GRID).astype(np.float32)[:, None] * inv], axis=-1).astype(np.float32)
    cos, sin = np.ones((P, T)), np.zeros((P, T))
    cos[HD:QH] = np.repeat(np.cos(ang), 2, axis=1).T
    sin[HD:QH] = np.repeat(np.sin(ang), 2, axis=1).T
    turn = np.zeros((P, P))
    for i in range(ROPE // 2):
        a, b = HD + 2 * i, HD + 2 * i + 1
        turn[b, a], turn[a, b] = -1.0, 1.0
    place, placeturn = np.zeros((P, P)), np.zeros((P, P))
    for i in range(ROPE):
        place[i, HD + i] = 1.0
        placeturn[i] = turn[HD + i]
    attn |= {"cos": cos, "sin": sin, "turn": turn, "place": place, "placeturn": placeturn}

    def pack(parts):
        at, where = 0, {}
        for name, a in parts.items():
            where[name] = (at, a.shape[1])
            at += a.shape[1]
        return np.ascontiguousarray(np.concatenate([a.astype(np.float32) for a in parts.values()], 1)), where

    return pack(main), pack(attn)


class Lane:

    def __init__(self, sem):
        self.sem, self.n, self.queue, self.seen = sem, 0, [], {}

    def mark(self):
        return (self.sem, self.n)

    def wait(self, *marks):
        for m in marks:
            if m is None:
                continue
            sem, value = m
            if value > 0 and self.seen.get(sem.name, 0) < value:
                self.seen[sem.name] = value
                self.queue.append(lambda e, s=sem, v=value: e.wait_ge(s, v))

    def step(self, make, *after):
        self.wait(*after)
        self.n += 1
        self.queue.append(lambda e: make(e).then_inc(self.sem, 1))
        return self.mark()

    def plain(self, make):
        self.queue.append(make)

    def loop(self, first, end, body):
        def run(e):
            with e.Fori(first, end) as i:
                body(e, i)
        if end - first > 1:
            self.queue.append(run)
        elif end > first:
            self.queue.append(lambda e: body(e, first))


def build_program(nc, a, out):
    (_, MAIN), (_, ATT) = shape_constants()
    stack = ExitStack()
    with stack:
        def sb(name, shape, dt=F32, ctx=stack):
            return ctx.enter_context(nc.sbuf_tensor("sb_" + name, shape, dt))

        def sem(name):
            return stack.enter_context(nc.semaphore(name))

        bank = [stack.enter_context(nc.psum_tensor(f"bank{i}", [P, 512], F32)) for i in range(8)]
        pe, act, dve, pool, sp = (Lane(sem("done_" + n)) for n in ("pe", "act", "dve", "pool", "sp"))

        raw = [sb(f"raw{s}", [P, CHUNK]) for s in range(3)]
        whi = [sb(f"whi{s}", [P, CHUNK], F32R) for s in range(3)]
        wlo = [sb(f"wlo{s}", [P, CHUNK], F32R) for s in range(3)]
        x = sb("x", [P, KT, T])
        xn = sb("xn", [P, KT, T])
        xhi = sb("xhi", [P, KT, T], F32R)
        xlo = sb("xlo", [P, KT, T], F32R)
        h = sb("h", [P, 2, T])
        hhi = sb("hhi", [P, 2, T], F32R)
        hlo = sb("hlo", [P, 2, T], F32R)
        sil = sb("sil", [P, 2, T])
        ada_raw = sb("ada_raw", [P, KT, ADA_W])
        ada_acc = sb("ada_acc", [P, ADA_W])
        cact = sb("cact", [P, KT])
        mod = sb("mod", [P, 2, MODS])
        cst = sb("cst", [P, sum(n for _, n in MAIN.values())])
        vec = sb("vec", [P, NVEC])
        rstd = sb("rstd", [P, 2, T])
        epss = sb("epss", [P, 2])
        sq = sb("sq", [P, 2, T])
        zero = sb("zero", [P, 512], BF16)

        def C(name, p0=0, p1=P):
            at, n = MAIN[name]
            return cst[p0:p1, at:at + n]

        def V(name, i=0, p0=0, p1=P):
            return vec[p0:p1, VEC[name] + i:VEC[name] + i + 1]

        ident, ones = C("ident"), C("ones")

        def dma(lane, dst, src, name, *after):
            s = sem("in_" + name)
            lane.wait(*after)
            lane.queue.append(lambda e: e.dma_start(dst, src).then_inc(s, 16))
            return (s, 16)

        scratch_free = [[]]

        def meet():
            marks = [l.mark() for l in (pe, act, dve, pool)]
            scratch_free[0] = marks
            for l in (pe, act, dve, pool):
                l.wait(*marks)
            return marks

        got_x = dma(act, x[:, :, :], a["x"], "x")
        got_vec = dma(act, vec[:, :], a["vec"], "vec")
        got_cst = dma(act, cst[:, :], a["cst"], "cst")
        for l in (pe, act, dve, pool):
            l.wait(got_vec, got_cst)
        m_zero = pool.step(lambda e: e.memset(zero[:, :], 0.0))
        m_cact = act.step(lambda e: e.activation(cact[:, :], vec[:, VEC["c_2"]:VEC["c_2"] + KT], ACT.Silu), got_vec)
        dve.wait(m_cact)
        pe.wait(m_zero)
        m_eps = pool.step(lambda e: e.memset(epss[:, 0:1], EPS))
        act.wait(pool.step(lambda e: e.memset(epss[:, 1:2], GN_EPS)), m_eps)

        s_raw = [sem(f"raw_landed{s}") for s in range(3)]
        s_hi = [sem(f"high_ready{s}") for s in range(3)]
        s_lo = [sem(f"low_ready{s}") for s in range(3)]
        s_used = [sem(f"weights_used{s}") for s in range(3)]
        uses = [0, 0, 0]
        turn = [0]
        split_ahead = []
        for s in range(3):
            pe.plain(lambda e, s=s: e.sem_inc(s_used[s], 1))
            act.plain(lambda e, s=s: e.sem_inc(s_hi[s], 1))
            dve.plain(lambda e, s=s: e.sem_inc(s_lo[s], 1))

        def load(e, s, n, src):
            e.wait_ge(s_lo[s], n + 1)
            e.dma_start(raw[s][:, :], src).then_inc(s_raw[s], 16)

        def high(e, s, n):
            e.wait_ge(s_raw[s], 16 * n + 16)
            e.wait_ge(s_used[s], n + 1)
            e.activation(whi[s][:, :], raw[s][:, :], ACT.Copy).then_inc(s_hi[s], 1)

        def low(e, s, n):
            e.wait_ge(s_hi[s], n + 2)
            e.tensor_tensor(wlo[s][:, :], raw[s][:, :], whi[s][:, :], ALU.subtract).then_inc(s_lo[s], 1)

        def fetch(src):
            if split_ahead and src is not None and split_ahead[0][2] is src:
                s, nth, _ = split_ahead.pop(0)
                return s, nth
            assert not split_ahead
            return fetch_now(src)

        def fetch_now(src):
            s = turn[0]
            nth = uses[s]
            turn[0] = (s + 1) % 3
            uses[s] += 1
            sp.plain(lambda e: load(e, s, nth, src))
            act.plain(lambda e: high(e, s, nth))
            dve.plain(lambda e: low(e, s, nth))
            return s, nth

        def ahead(*srcs):
            for src in srcs:
                split_ahead.append((*fetch_now(src), src))

        def product(e, dst, w, x_parts, first, last, skip=False):
            (wh, wl), (xh, xl) = w, x_parts
            e.matmul(dst, wh, xh, start=first, stop=False, skip_group_check=skip)
            e.matmul(dst, wh, xl, start=False, stop=False, skip_group_check=skip)
            return e.matmul(dst, wl, xh, start=False, stop=last, skip_group_check=skip)

        def wtile(s, at):
            return whi[s][:, at:at + P], wlo[s][:, at:at + P]

        def square_sum(src, tiles, dst, *after):
            marks = []
            buf = lambda k: (sil if k % 4 < 2 else sq)[:, k % 2, :]
            for k in range(tiles):
                mine = (after[k],) if len(after) == tiles else after
                m = act.step(lambda e, k=k: e.activation(buf(k), src(k), ACT.Square),
                             *mine, marks[k - 4] if k >= 4 else None)
                marks.append(pe.step(lambda e, k=k: e.matmul(dst, ones, buf(k),
                                                             start=k == 0, stop=k == tiles - 1), m))
            return marks[-1]

        def inv_root(dst, src, scale, eps, *after):
            bias = epss[:, 0:1] if eps == EPS else epss[:, 1:2]
            m = act.step(lambda e: e.activation(dst, src, ACT.Sqrt, bias=bias, scale=scale), *after)
            return dve.step(lambda e: e.reciprocal(dst, dst), m)

        def norm(gain, shift, after, *also):
            act.wait(*also)
            dve.wait(*also)
            m = square_sum(lambda k: x[:, k, :], KT, bank[6][:, 0:T], *after)
            m_r = inv_root(rstd[:, 0, :], bank[6][:, 0:T], 1.0 / D, EPS, m)
            parts, mh = [], []

            def lows(k):
                parts.append(dve.step(lambda e: e.tensor_tensor(
                    xlo[:, k, :], xn[:, k, :], xhi[:, k, :], ALU.subtract), mh[k]))

            for k in range(KT):
                m = dve.step(lambda e, k=k: e.scalar_tensor_tensor(
                    xn[:, k, :], x[:, k, :], gain(k), rstd[:, 0, :], ALU.mult, ALU.mult), m_r)
                if shift is not None:
                    m = act.step(lambda e, k=k: e.activation(xn[:, k, :], xn[:, k, :], ACT.Identity,
                                                             bias=shift(k)), m)
                mh.append(act.step(lambda e, k=k: e.activation(xhi[:, k, :], xn[:, k, :], ACT.Copy), m))
                if k >= 2:
                    lows(k - 2)
            lows(KT - 2)
            lows(KT - 1)
            return parts

        def split_xn(m):
            parts = []
            for k in range(0, KT, 2):
                mh = act.step(lambda e, k=k: e.activation(xhi[:, k:k + 2, :], xn[:, k:k + 2, :], ACT.Copy),
                              *(m[k:k + 2] if isinstance(m, list) else (m,)))
                ml = dve.step(lambda e, k=k: e.tensor_tensor(xlo[:, k:k + 2, :], xn[:, k:k + 2, :],
                                                             xhi[:, k:k + 2, :], ALU.subtract), mh)
                parts += [ml, ml]
            return parts

        s_silu, s_mult, s_hhi, s_hlo = sem("silu_done"), sem("mult_done"), sem("h_high"), sem("h_low")
        s_ada_raw, s_ada, s_chain, s_adr = sem("ada_landed"), sem("ada_partial"), sem("ada_chain"), sem("ada_summed")
        s_ctmp = sem("h_before_weighting")
        for l, s in ((pe, s_adr), (dve, s_ada), (act, s_silu), (dve, s_mult), (dve, s_hlo)):
            l.plain(lambda e, s=s: e.sem_inc(s, 1))
        units_before = [0]
        GATE, UP, MODP = bank[4], bank[5], bank[7]

        def ffn(w, n, ada_first, ada_n, weight, parts, free, following, ada_after=None, loaded=False):
            u0 = units_before[0]
            units_before[0] += n
            (A_, na, _), (B_, nb, _) = split_ahead
            split_ahead.clear()
            C_ = turn[0]
            b0 = {A_: na, B_: nb, C_: uses[C_]}
            for s in range(3):
                uses[s] = b0[s] + n
            turn[0] = A_
            has_ada = lambda j: ada_n > 0 and (not isinstance(j, int) or j < ada_n)

            def sp_in(e, j):
                load(e, A_, b0[A_] + j, w[j, 0])
                load(e, B_, b0[B_] + j, w[j, 1])

            def sp_ada(e, j):
                e.wait_ge(s_ada, ada_first + j + 1)
                e.dma_start(ada_raw[:, :, :], a["ada"][ada_first + j]).then_inc(s_ada_raw, 16)

            def sp_down(e, j):
                load(e, C_, b0[C_] + j, w[j, 2])

            def a_hhi(e, j):
                e.wait_ge(s_mult, u0 + j + 2)
                e.wait_ge(s_used[C_], b0[C_] + j + 1)
                e.activation(hhi[:, :, :], h[:, :, :], ACT.Copy).then_inc(s_hhi, 1)

            def a_silu(e, j):
                e.wait_ge(s_used[A_], b0[A_] + j + 2)
                e.wait_ge(s_mult, u0 + j + 1)
                e.activation(sil[:, :, :], GATE[:, :], ACT.Silu).then_inc(s_silu, 1)

            def v_hlo(e, j):
                e.wait_ge(s_hhi, u0 + j + 1)
                e.tensor_tensor(hlo[:, :, :], h[:, :, :], hhi[:, :, :], ALU.subtract).then_inc(s_hlo, 1)

            def v_mult(e, j):
                e.wait_ge(s_used[B_], b0[B_] + j + 2)
                e.wait_ge(s_hlo, u0 + j + 1)
                e.wait_ge(s_silu, u0 + j + 2)
                if weight is None:
                    e.tensor_tensor(h[:, :, :], sil[:, :, :], UP[:, :], ALU.mult).then_inc(s_mult, 1)
                else:
                    e.tensor_tensor(h[:, :, :], sil[:, :, :], UP[:, :], ALU.mult).then_inc(s_ctmp, 1)
                    e.wait_ge(s_ctmp, j + 1)
                    e.tensor_tensor(h[:, :, :], h[:, :, :], weight(j), ALU.mult).then_inc(s_mult, 1)

            def v_ada(e, j):
                e.wait_ge(s_ada_raw, 16 * (ada_first + j) + 16)
                e.wait_ge(s_adr, ada_first + j + 1)
                c0 = (ada_first + j) * (KT - 1)
                e.tensor_scalar(ada_acc[:, :], ada_raw[:, 0, :], cact[:, 0:1], None, ALU.mult).then_inc(s_chain, 1)
                for k in range(1, KT):
                    e.wait_ge(s_chain, c0 + k)
                    e.scalar_tensor_tensor(ada_acc[:, :], ada_raw[:, k, :], cact[:, k:k + 1], ada_acc[:, :],
                                           ALU.mult, ALU.add).then_inc(s_ada if k == KT - 1 else s_chain, 1)

            def p_ada(e, j):
                e.wait_ge(s_ada, ada_first + j + 2)
                for i in range(ADA_W // P):
                    l = e.matmul(MODP[:, bass.ds((ada_first + j) * (ADA_W // P) + i, 1)],
                                 ada_acc[:, i * P:(i + 1) * P], ones[:, 0:1], start=True, stop=True)
                l.then_inc(s_adr, 1)

            def p_gate(e, j, s, dst, free_sem, parts=None):
                e.wait_ge(s_lo[s], b0[s] + j + 2)
                e.wait_ge(free_sem, u0 + j + 1)
                for m in range(CW // P):
                    for k in range(KT):
                        if parts is not None and m == 0:
                            e.wait_ge(*parts[k])
                        l = product(e, dst[:, m * T:(m + 1) * T], wtile(s, k * CW + m * P),
                                    (xhi[:, k, :], xlo[:, k, :]), k == 0, k == KT - 1)
                l.then_inc(s_used[s], 1)

            def p_down(e, j):
                e.wait_ge(s_lo[C_], b0[C_] + j + 2)
                e.wait_ge(s_hlo, u0 + j + 2)
                for m in range(KT):
                    for k in range(2):
                        l = product(e, bank[m // 2][:, (m % 2) * T:(m % 2 + 1) * T],
                                    wtile(C_, k * D + m * P), (hhi[:, k, :], hlo[:, k, :]),
                                    False, False, skip=True)
                l.then_inc(s_used[C_], 1)

            def sp_body(e, j):
                sp_in(e, j + 1)
                if has_ada(j):
                    sp_ada(e, j)
                sp_down(e, j)

            def act_body(e, j, more=True):
                a_hhi(e, j - 1)
                high(e, C_, b0[C_] + j - 1)
                a_silu(e, j)
                if more:
                    high(e, A_, b0[A_] + j + 1)
                    high(e, B_, b0[B_] + j + 1)

            def dve_body(e, j, more=True):
                v_hlo(e, j - 1)
                low(e, C_, b0[C_] + j - 1)
                if more:
                    low(e, A_, b0[A_] + j + 1)
                v_mult(e, j)
                if more:
                    low(e, B_, b0[B_] + j + 1)
                if has_ada(j):
                    v_ada(e, j)

            def pe_body(e, j):
                p_gate(e, j, A_, GATE, s_silu)
                if has_ada(j - 1):
                    p_ada(e, j - 1)
                p_gate(e, j, B_, UP, s_mult)
                p_down(e, j - 1)

            if not loaded:
                sp.plain(lambda e: sp_in(e, 1))
            sp.wait(ada_after)
            if has_ada(0):
                sp.plain(lambda e: sp_ada(e, 0))
            if not loaded:
                sp.plain(lambda e: sp_down(e, 0))
            sp.loop(1, n - 1, sp_body)
            if has_ada(n - 1):
                sp.plain(lambda e: sp_ada(e, n - 1))
            sp.plain(lambda e: sp_down(e, n - 1))

            act.plain(lambda e: a_silu(e, 0))
            act.plain(lambda e: high(e, A_, b0[A_] + 1))
            act.plain(lambda e: high(e, B_, b0[B_] + 1))
            act.loop(1, n - 1, act_body)
            act.plain(lambda e: act_body(e, n - 1, False))
            act.plain(lambda e: a_hhi(e, n - 1))
            act.plain(lambda e: high(e, C_, b0[C_] + n - 1))

            dve.plain(lambda e: low(e, A_, b0[A_] + 1))
            dve.plain(lambda e: v_mult(e, 0))
            dve.plain(lambda e: low(e, B_, b0[B_] + 1))
            if has_ada(0):
                dve.plain(lambda e: v_ada(e, 0))
            dve.loop(1, n - 1, dve_body)
            dve.plain(lambda e: dve_body(e, n - 1, False))
            dve.plain(lambda e: v_hlo(e, n - 1))
            dve.plain(lambda e: low(e, C_, b0[C_] + n - 1))
            ahead(*following)

            pe.wait(*free)
            for b in range(4):
                pe.plain(lambda e, b=b: e.matmul(bank[b][:, :], zero[:, 0:P], zero[:, :], start=True, stop=False,
                                                 skip_group_check=True))
            pe.plain(lambda e: p_gate(e, 0, A_, GATE, s_silu, parts))
            pe.plain(lambda e: p_gate(e, 0, B_, UP, s_mult))
            pe.loop(1, n - 1, pe_body)
            pe.plain(lambda e: pe_body(e, n - 1))
            pe.plain(lambda e: p_down(e, n - 1))
            if has_ada(n - 1):
                pe.plain(lambda e: p_ada(e, n - 1))
            for b in range(4):
                m = pe.step(lambda e, b=b: e.matmul(bank[b][:, :], zero[:, 0:P], zero[:, :], start=False,
                                                    stop=True, skip_group_check=True))
            return m

        def linear(chunks, evac, parts, following):
            marks, done, slots = [], [], []
            n = len(chunks)

            def run(e, s, form, dst, first):
                for m in range(2):
                    for k in range(KT):
                        if first and m == 0:
                            e.wait_ge(*parts[k])
                        if form == "channels":
                            o = dst[:, m * T:(m + 1) * T]
                            l = product(e, o, wtile(s, k * CW + m * P), (xhi[:, k, :], xlo[:, k, :]),
                                        k == 0, k == KT - 1)
                        else:
                            o = dst[:, m * CW:(m + 1) * CW]
                            wh, wl = (z[s][:, k * CW:(k + 1) * CW] for z in (whi, wlo))
                            xh, xl = (z[:, k, m * P:(m + 1) * P] for z in (xhi, xlo))
                            l = product(e, o, (xh, xl), (wh, wl), k == 0, k == KT - 1)
                l.then_inc(s_used[s], 1)

            for c, (src, form) in enumerate(chunks):
                s, nth = fetch(src)
                slots.append(s)
                pe.wait((s_lo[s], nth + 2), marks[c - 3] if c >= 3 else None)
                pe.plain(lambda e, s=s, form=form, c=c: run(e, s, form, bank[4 + s], c == 0))
                done.append((s_used[s], nth + 2))
                if c >= 2:
                    marks.append(evac(c - 2, bank[4 + slots[c - 2]], done[c - 2]))
            ahead(*following)
            for c in range(max(n - 2, 0), n):
                marks.append(evac(c, bank[4 + slots[c]], done[c]))
            return marks

        def add_half(m):
            r = []
            for b in range(4):
                r += 2 * [dve.step(lambda e, b=b: e.scalar_tensor_tensor(
                    x[:, 2 * b:2 * b + 2, :], bank[b][:, :].rearrange("p (k t) -> p k t", k=2), 0.5,
                    x[:, 2 * b:2 * b + 2, :], ALU.mult, ALU.add), m)]
            return r

        def add_gated(gate, m):
            return [dve.step(lambda e, k=k: e.scalar_tensor_tensor(
                x[:, k, :], bank[k // 2][:, (k % 2) * T:(k % 2 + 1) * T], gate(k), x[:, k, :],
                ALU.mult, ALU.add), m) for k in range(KT)]

        def add_chunks(gate):
            def evac(c, b, m):
                r = None
                for i in range(2):
                    k = 2 * c + i
                    src = b[:, i * T:(i + 1) * T]
                    if gate is None:
                        r = dve.step(lambda e, k=k, src=src: e.tensor_tensor(x[:, k, :], src, x[:, k, :], ALU.add), m)
                    else:
                        r = dve.step(lambda e, k=k, src=src: e.scalar_tensor_tensor(
                            x[:, k, :], src, gate(k), x[:, k, :], ALU.mult, ALU.add), m)
                return r
            return evac

        s_stored = {k: sem(f"stored{k}") for k in (3, 7)}

        def store(k, m):
            sp.wait(m)
            sp.plain(lambda e: e.dma_start(out[:, k - 3:k + 1, :], xn[:, k - 3:k + 1, :]).then_inc(s_stored[k], 16))
            return (s_stored[k], 16)

        def finish(mx):
            mm = square_sum(lambda k: x[:, k, :], KT, bank[4][:, 0:T], *mx)
            mm = inv_root(rstd[:, 0, :], bank[4][:, 0:T], 1.0 / D, EPS, mm)
            stored = []
            for k in range(KT):
                m = dve.step(lambda e, k=k: e.scalar_tensor_tensor(xn[:, k, :], x[:, k, :], V("final_norm_2", k),
                                                                   rstd[:, 0, :], ALU.mult, ALU.mult), mm)
                if k % 4 == 3:
                    stored.append(store(k, m))
            sp.wait(*stored)

        def fork(flag, m_flag, fits, general):
            lanes = (sp, act, dve, pe, pool)
            for l in lanes:
                l.wait(m_flag)
            counters = (uses, turn, split_ahead, units_before)
            kept = [list(z) for z in counters]
            base = [(l.n, dict(l.seen), l.queue) for l in lanes]
            ways = []
            for way in (fits, general):
                for z, was in zip(counters, kept):
                    z[:] = was
                for l, (n, seen, _) in zip(lanes, base):
                    l.n, l.seen, l.queue = n, dict(seen), []
                way()
                ways.append([l.queue for l in lanes])
            for i, (l, (_, _, before)) in enumerate(zip(lanes, base)):
                def run(e, i=i):
                    over = e.value_load(flag[0:1, 0:1], min_val=0, max_val=1)
                    with e.If(over < 1):
                        for item in ways[0][i]:
                            item(e)
                    with e.If(over > 0):
                        for item in ways[1][i]:
                            item(e)
                l.queue = before + [run]

        env = dict(locals())
        first = {n: (a[n][0, 0], a[n][0, 1]) for n in ("ffn1", "ffn2", "ffn3", "moe")}
        chunks = {n: [a[n][c] for c in range(a[n].shape[0])]
                  for n in ("w_in", "w_out", "na_qk", "na_v", "na_o", "mla_o")}
        env |= {"first": first, "chunks": chunks}
        ahead(*first["ffn1"])
        m = norm(lambda k: V("norm_ffn1", k), None, [got_x])
        m = ffn(a["ffn1"], FFN_UNITS, 0, FFN_UNITS, None, m, [], chunks["w_in"][:2])
        mx = add_half(m)
        m = norm(lambda k: V("norm_mix", k), None, mx)
        mx = token_mixer(env, m)
        m = norm(lambda k: V("norm_ffn2", k), None, mx)
        m = ffn(a["ffn2"], FFN_UNITS, FFN_UNITS, FFN_UNITS, None, m, [], chunks["na_qk"][:2], mx[-1])
        mx = add_half(m)
        mm = square_sum(lambda k: x[:, k, :], KT, bank[6][:, 0:T], *mx)
        mm = inv_root(rstd[:, 0, :], bank[6][:, 0:T], 1.0 / D, EPS, mm)
        mx = [dve.step(lambda e, k=k: e.scalar_tensor_tensor(x[:, k, :], x[:, k, :], V("norm_final", k),
                                                             rstd[:, 0, :], ALU.mult, ALU.mult), mm)
              for k in range(KT)]

        def take_mod(layer, pieces):
            b = VEC["b_ada_2"] + layer * MODS
            mt = dve.step(lambda e: e.tensor_tensor(mod[:, layer, :], MODP[:, layer * MODS:(layer + 1) * MODS],
                                                    vec[:, b:b + MODS], ALU.add), (s_adr, pieces + 1))
            for part in (1, 4):
                sl = mod[:, layer, part * KT:(part + 1) * KT]
                mt = dve.step(lambda e, sl=sl: e.tensor_scalar_add(sl, sl, 1.0), mt)
            return mt

        def M(layer, part):
            return lambda k: mod[:, layer, part * KT + k:part * KT + k + 1]

        mt = take_mod(0, 2 * FFN_UNITS)
        m = norm(M(0, 1), M(0, 0), mx, mt)
        mx = neighbourhood(env, M(0, 2), m)
        m = norm(M(0, 4), M(0, 3), mx)
        m = ffn(a["ffn3"], FFN_UNITS, 2 * FFN_UNITS, ADA_UNITS - 2 * FFN_UNITS, None, m, [], chunks["mla_o"][:2])
        mx = add_gated(M(0, 5), m)
        mt = take_mod(1, ADA_UNITS)
        m = norm(M(1, 1), M(1, 0), mx, mt)
        mx = latent(env, M(1, 2), m)
        m = norm(M(1, 4), M(1, 3), mx)
        (A_, na, _), (B_, nb, _) = split_ahead
        C_, w_moe = turn[0], a["moe"]
        for s, n, src in ((C_, uses[C_], w_moe[0, 2]), (A_, na + 1, w_moe[1, 0]), (B_, nb + 1, w_moe[1, 1])):
            sp.plain(lambda e, s=s, n=n, src=src: load(e, s, n, src))
        with ExitStack() as ctx:
            comb, pos, taken, flag, mc, m_flag = router(env, ctx, m[-1])

            def dense():
                mo = ffn(a["moe"], EXPERTS * EXPERT_UNITS, 0, 0,
                         lambda j: comb[:, bass.ds(j // EXPERT_UNITS, 1), :].broadcast_to([P, 2, T])
                         if not isinstance(j, int) else
                         comb[:, j // EXPERT_UNITS:j // EXPERT_UNITS + 1, :].broadcast_to([P, 2, T]), m, [mc], [], loaded=True)
                finish(add_gated(M(1, 5), mo))

            fork(flag, m_flag, lambda: finish(dispatched(env, ctx, comb, pos, taken, mc, M(1, 5))), dense)

        with nc.Block() as block:
            for lane, attach in ((sp, block.sync), (act, block.scalar), (dve, block.vector),
                                 (pe, block.tensor), (pool, block.gpsimd)):
                def run(e, lane=lane):
                    for item in lane.queue:
                        item(e)
                attach(run)


def token_mixer(env, m_in):
    a, sb, bank, pe, act, dve, pool = (env[n] for n in ("a", "sb", "bank", "pe", "act", "dve", "pool"))
    C, V, ident, ones, dma, meet = (env[n] for n in ("C", "V", "ident", "ones", "dma", "meet"))
    linear, square_sum, inv_root, rstd, y = (env[n] for n in ("linear", "square_sum", "inv_root", "rstd", "xn"))
    with ExitStack() as outer:
        p = sb("p", [P, MIX_TILES, T], ctx=outer)
        tok = sb("tok", [P, NB, T], ctx=outer)
        lora = sb("lora", [P, 2, G], ctx=outer)
        g2 = sb("g2", [P, G], ctx=outer)
        gw2 = sb("gw2", [GLA_LORA, G], ctx=outer)
        wga = sb("wga", [P, KT, GLA_LORA], ctx=outer)
        ga = sb("ga", [GLA_LORA, T], ctx=outer)
        wp = sb("wp", [P, GT, P], ctx=outer)
        m_z = pool.step(lambda e: e.memset(lora[:, :, :], 0.0))
        m_zp = pool.step(lambda e: e.memset(wp[:, :, :], 0.0))
        w_lora = [dma(pool, lora[0:64, 0, :], a["rwkv_w2"], "rwkv_w2", m_z),
                  dma(pool, lora[64:128, 1, :], a["rwkv_a2"], "rwkv_a2", m_z),
                  dma(pool, g2[:, :], a["rwkv_g2"], "rwkv_g2"),
                  dma(pool, gw2[:, :], a["gla_w2"], "gla_w2"),
                  dma(pool, wga[:, :, :], a["w_in_ga"], "w_in_ga")]
        w_pool = [dma(pool, wp[i % 2 * 64:i % 2 * 64 + 64, i // 2, i % 2 * 64:i % 2 * 64 + 64],
                      a["pool_w"][i], f"pool_w{i}", m_zp) for i in range(4)]

        unit = outer.enter_context(env["nc"].sbuf_tensor("sb_unit", [P, T], F32))
        m_unit = pool.step(lambda e: e.memset(unit[:, :], 1.0))
        gate = sb("gate", [P, GT, T], ctx=outer)
        lbs = sb("lbs", [P, 6], ctx=outer)
        tmp = sb("tmp", [P, GT, T], ctx=outer)

        gat = ExitStack()
        spare = env["ada_raw"][:, :, :].rearrange("p k n -> p (k n)")
        two = lambda z: z.rearrange("p (k t) -> p k t", k=GT)
        own = {"cumg": sb("cumg", [P, GT, T], ctx=gat)[:, :, :],
               "ex": [sb(f"ex{i}", [P, GT * T], ctx=gat)[:, :] for i in range(2)],
               "qpad": [sb(f"qpad{i}", [P, 2, GT, T], ctx=gat)[:, :, :, :] for i in range(2)],
               "sc": sb("sc", [P, MH, 3, P], ctx=gat)[:, :, :, :], "tok": tok[:, :, :]}
        lent = {"cumg": y[:, 0:2, :], "ex": [y[:, i:i + 2, :].rearrange("p k t -> p (k t)") for i in (2, 4)],
                "sc": spare[:, 0:MH * 3 * P].rearrange("p (h b t) -> p h b t", h=MH, b=3), "tok": y[:, 6:8, :]}
        gate2, tmp2, rstd2 = (two(spare[:, MH * 3 * P + i * GT * T:MH * 3 * P + (i + 1) * GT * T]) for i in range(3))
        for z in (own["sc"], lent["sc"], *own["qpad"]):
            m_zero = pool.step(lambda e, z=z: e.memset(z, 0.0), m_in[-1])
        rstd3 = two(spare[:, 0:GT * T])

        def evac(c, b, m):
            dst = p[:, 2 * c:2 * c + 2, :]
            src = b[:, :].rearrange("p (k t) -> p k t", k=2)
            if c % 2:
                return act.step(lambda e: e.activation(dst, src, ACT.Copy), m)
            return dve.step(lambda e: e.tensor_copy(dst, src), m)

        em = linear([(w, "channels") for w in env["chunks"]["w_in"]], evac, m_in, env["chunks"]["w_out"][:2])
        for k in range(KT):
            mga = pe.step(lambda e, k=k: e.matmul(bank[3][0:GLA_LORA, 0:T], wga[:, k, :], y[:, k, :],
                                                  start=k == 0, stop=k == KT - 1), w_lora[4], m_in[-1])
        mga = act.step(lambda e: e.activation(ga[:, :], bank[3][0:GLA_LORA, 0:T], ACT.Copy), mga)
        meet()
        ready = list(em) + [mga]
        for l in (pe, act, dve, pool):
            l.wait(*ready, *w_lora, *w_pool, m_unit, m_zero)
        lent_q, lent_w = (env["raw"][s][:, :] for s, _, _ in env["split_ahead"])
        half = 2 * GT * T
        lent["qpad"] = [lent_q[:, i * half:(i + 1) * half].rearrange("p (h k t) -> p h k t", h=2, k=GT)
                        for i in range(2)]
        for z in lent["qpad"]:
            m_zero = pool.step(lambda e, z=z: e.memset(z, 0.0))
        pool.wait(m_zero)

        def TT(lane, o, i0, i1, op, *after):
            return lane.step(lambda e: e.tensor_tensor(o, i0, i1, op), *after)

        def TS(lane, o, i0, s1, s2, op0, op1, *after):
            if op1 is None:
                return lane.step(lambda e: e.tensor_scalar(o, i0, s1, None, op0), *after)
            return lane.step(lambda e: e.tensor_scalar(o, i0, s1, s2, op0, op1), *after)

        def STT(o, i0, s, i1, op0, op1, *after):
            return dve.step(lambda e: e.scalar_tensor_tensor(o, i0, s, i1, op0, op1), *after)

        def AC(o, i, f, *after, bias=None, scale=None):
            kw = {}
            if bias is not None:
                kw["bias"] = bias
            if scale is not None:
                kw["scale"] = scale
            return act.step(lambda e: e.activation(o, i, f, **kw), *after)

        def MM(o, l, r, start, stop, *after):
            return pe.step(lambda e: e.matmul(o, l, r, start=start, stop=stop), *after)

        def to_tokens(src, dst, b, *after):
            for i in range(GT):
                for blk in range(NB):
                    o = bank[b][:, blk * T + i * P:blk * T + (i + 1) * P]
                    m = pe.step(lambda e, o=o, i=i, blk=blk: e.transpose(o, src[:, i, blk * P:(blk + 1) * P], ident),
                                *after)
            return dve.step(lambda e: e.tensor_copy(dst, bank[b][:, :].rearrange("p (b c) -> p b c", b=NB)), m)

        def gated_attention(bufs, banks, q, k, g, vt, dst, *after):
            cumg, ex, qpad, sc, tok = (bufs[n] for n in ("cumg", "ex", "qpad", "sc", "tok"))
            b_sc, b_out = banks[0:2], banks[2]
            mb = [dve.step(lambda e, i=i: e.tensor_tensor_scan(
                cumg[:, i, :], unit[:, :], g[:, i, :], 0.0, ALU.mult, ALU.add), *after) for i in range(GT)]
            mb = mb[-1]
            mv = to_tokens(vt, tok, b_out, *after)
            bf = cumg.rearrange("p k t -> p (k t)")
            qf, kf = (z.rearrange("p k t -> p (k t)") for z in (q, k))
            levels = [0, 1, 2, 4, 8, 16, 32, 64, 128]
            ready, read, copied, pending = {}, {}, {}, {}

            def decay(n):
                w, e_, qz = levels[n], ex[n % 2], qpad[n % 2]
                free = read.get(n - 2)
                if not w:
                    ms = [pool.step(lambda e, hh=hh: e.tensor_copy(
                        qz[hh * HD:(hh + 1) * HD, hh], q[hh * HD:(hh + 1) * HD]), *after) for hh in range(2)]
                    ready[n] = (kf, ms[-1], ms[-2], *after)
                    return
                v3 = lambda z: z.rearrange("p (n j) -> p n j", j=2 * w)
                lo, hi = (lambda z: v3(z)[:, :, 0:w]), (lambda z: v3(z)[:, :, w:2 * w])
                mid = v3(bf)[:, :, w - 1:w].broadcast_to([P, GT * T // (2 * w), w])
                m1 = TT(dve, hi(e_), hi(bf), mid, ALU.subtract, mb, free)
                m2 = TT(dve, lo(e_), mid, lo(bf), ALU.subtract, mb, free)
                m3 = AC(e_, e_, ACT.Exp, m1, m2)
                ms = []
                for hh in range(2):
                    hs = slice(hh * HD, (hh + 1) * HD)
                    ms.append(TT(pool, hi(qz[hs, hh].rearrange("p k t -> p (k t)")), hi(e_[hs, :]), hi(qf[hs]),
                                 ALU.mult, m3, free))
                ready[n] = (e_, *ms)
                pending[n] = lambda: TT(dve, lo(e_), lo(e_), lo(kf), ALU.mult, m3)

            def pairs(n):
                w, qz = levels[n], qpad[n % 2]
                lhs, *wait = ready[n]
                for ti in range(GT):
                    bk = bank[b_sc[ti]]
                    for blk in range(NB if w < P else 1):
                        tb = blk if w < P else 1
                        m = MM(bk[:, blk * T:(blk + 1) * T], lhs[:, ti * T + blk * P:ti * T + (blk + 1) * P],
                               qz[:, :, ti, tb * P:(tb + 1) * P], True, True, *wait, copied.get(n - 1))
                read[n] = m

            def collect(n):
                w = levels[n]
                for ti in range(GT):
                    bk = bank[b_sc[ti]]
                    if w < P:
                        mask = (C(f"level{w}") if w else ident).bitcast(U32)
                        mask = mask.rearrange("p (b t) -> p b t", b=1).broadcast_to([P, 2, P])
                        for blk in range(NB):
                            m = dve.step(lambda e, ti=ti, blk=blk, bk=bk: e.copy_predicated(
                                sc[:, 2 * ti:2 * ti + 2, 2 * blk, :], mask,
                                bk[:, blk * T:(blk + 1) * T].rearrange("p (h t) -> p h t", h=2)), read[n], copied.get(n - 1))
                    else:
                        m = dve.step(lambda e, ti=ti, bk=bk: e.tensor_copy(
                            sc[:, 2 * ti:2 * ti + 2, 1, :], bk[:, 0:T].rearrange("p (h t) -> p h t", h=2)), read[n], copied.get(n - 1))
                copied[n] = m

            last = len(levels) - 1
            decay(0)
            for n in range(last + 1):
                if n < last:
                    decay(n + 1)
                pairs(n)
                yield
                if n < last:
                    ready[n + 1] += (pending[n + 1](),)
                collect(n)
            ms = copied[last]
            for hh in range(MH):
                hp, ti = hh % 2 * HD, hh // 2
                lh = lambda blk, hh=hh: tok[:, blk, hh * HD:(hh + 1) * HD]
                MM(bank[b_out][hp:hp + HD, ti * T:(ti + 1) * T], lh(0),
                   sc[:, hh, 0:2, :].rearrange("p b t -> p (b t)"), True, False, ms, mv)
                mo = MM(bank[b_out][hp:hp + HD, ti * T + P:(ti + 1) * T], lh(1), sc[:, hh, 2, :], False, True, ms)
            bufs["done"] = AC(dst, bank[b_out][:, :].rearrange("p (k t) -> p k t", k=2), ACT.Copy, mo)

        def ln_floor(dst, src, tmp, *after):
            big = float(2 ** 64)
            m1 = TS(dve, tmp, src, float(2.0 ** -50), big, ALU.is_lt, ALU.mult, *after)
            m2 = STT(src, tmp, 1.0, src, ALU.max, ALU.mult, m1)
            m3 = AC(dst, src, ACT.Ln, m2)
            return STT(dst, tmp, float(-64 * np.log(2.0) / big), dst, ALU.mult, ALU.add, m3)

        def head_rstd(dst, src, tmp, b, scale, eps, *after):
            m = AC(tmp, src, ACT.Square, *after)
            for i in range(GT):
                m2 = MM(bank[b][:, i * T:(i + 1) * T], C("headsum"), tmp[:, i, :], True, True, m)
            return inv_root(dst, bank[b][:, :].rearrange("p (k t) -> p k t", k=2), scale, eps, m2)

        hq, hf, hi_, hg = (p[:, 2 * i:2 * i + 2, :] for i in (1, 2, 3, 4))
        gq, gk, gv, gg = (p[:, 18 + 2 * i:20 + 2 * i, :] for i in range(4))

        def hgrn():
            lg = env["vec"][:, VEC["hgrn_lb_logits"]:VEC["hgrn_lb_logits"] + GT]
            m0 = TT(dve, lbs[:, 0:2], lg, lg, ALU.subtract)
            m0 = AC(lbs[:, 0:2], lbs[:, 0:2], ACT.Exp, m0)
            m1 = dve.step(lambda e: e.reciprocal(lbs[:, 2:4], lbs[:, 0:2]), m0)
            m1 = TT(dve, lbs[:, 0:2], lbs[:, 0:2], lbs[:, 2:4], ALU.mult, m1)
            m1 = TT(dve, lbs[:, 4:6], lbs[:, 0:2], lbs[:, 0:2], ALU.subtract, m1)
            mlb = TS(dve, lbs[:, 2:4], lbs[:, 4:6], -1.0, 1.0, ALU.mult, ALU.add, m1)
            mf = AC(hf, hf, ACT.Sigmoid)
            mhg = AC(hg, hg, ACT.Sigmoid)
            for i in range(GT):
                mf = TS(dve, hf[:, i, :], hf[:, i, :], lbs[:, 2 + i:3 + i], lbs[:, 4 + i:5 + i], ALU.mult, ALU.add, mf, mlb)
            m1 = TS(dve, gate[:, :, :], hf, 1e-30, None, ALU.max, None, mf)
            mk = TS(dve, hf, hf, -1.0, 1.0, ALU.mult, ALU.add, m1)
            mq = AC(hq, hq, ACT.Silu)
            mq = TS(dve, hq, hq, QK_SCALE, None, ALU.mult, None, mq)
            yield
            mg = ln_floor(gate[:, :, :], gate[:, :, :], tmp[:, :, :], m1)
            yield from gated_attention(own, (0, 1, 4), hq, hf, gate[:, :, :], hi_, hq, mq, mk, mg)
            own["gate_ready"] = mhg

        def hgrn_tail():
            ms = square_sum(lambda k: hq[:, k, :], GT, bank[4][:, 0:T], own["done"])
            yield
            mr = inv_root(rstd3[:, 0, :], bank[4][:, 0:T], 1.0 / G, EPS, ms)
            yield
            for i in range(GT):
                m1 = STT(hq[:, i, :], hq[:, i, :], V("hgrn_norm", i), rstd3[:, 0, :], ALU.mult, ALU.mult, mr)
                TT(dve, hq[:, i, :], hq[:, i, :], hg[:, i, :], ALU.mult, m1, own["gate_ready"])

        def gla():
            for i in range(GT):
                m1 = MM(bank[5][:, i * T:(i + 1) * T], gw2[:, i * P:(i + 1) * P], ga[:, :], True, True)
            for i in range(GT):
                m2 = TS(dve, gate2[:, i, :], bank[5][:, i * T:(i + 1) * T], V("gla_b", i), None, ALU.add, None, m1)
            m3 = STT(tmp2, gate2, -1.0, gate2, ALU.mult, ALU.min, m2)
            mgg = AC(gg, gg, ACT.Silu)
            yield
            m4 = AC(tmp2, tmp2, ACT.Exp, m3)
            m4 = AC(tmp2, tmp2, ACT.Ln, m4, bias=1.0)
            m5 = STT(gate2, gate2, 0.0, tmp2, ALU.min, ALU.subtract, m4)
            mg = TS(dve, gate2, gate2, 1.0 / 16.0, None, ALU.mult, None, m5)
            mq = TS(dve, gq, gq, QK_SCALE, None, ALU.mult, None)
            yield from gated_attention(lent, (2, 3, 5), gq, gk, gate2, gv, gq, mq, mg)
            lent["gate_ready"] = mgg

        def gla_tail():
            yield
            mr = head_rstd(rstd2, gq, tmp2, 5, 1.0 / HD, EPS, lent["done"])
            yield
            for i in range(GT):
                m1 = STT(gq[:, i, :], gq[:, i, :], V("gla_norm", i), rstd2[:, i, :], ALU.mult, ALU.mult, mr)
                lent["end"] = TT(dve, gq[:, i, :], gq[:, i, :], gg[:, i, :], ALU.mult, m1, lent["gate_ready"])

        for _ in zip_longest(hgrn(), gla()):
            pass
        meet()
        gat.close()
        m_gat = pe.mark()
        tails = zip_longest(hgrn_tail(), gla_tail())

        with ExitStack() as c3:
            rw = p[:, 10:18, :]
            cum = sb("rcum", [P, GT, T], ctx=c3)
            av = sb("rwkv_a", [P, GT, T], ctx=c3)
            bb = sb("rwkv_b", [P, GT, T], ctx=c3)
            qr = sb("qr", [P, GT, 2, 2, T], ctx=c3)
            mz_ = pool.step(lambda e: e.memset(qr[:, :, :, :, :], 0.0))
            pad = 16
            wb = [lent_w[:, i * GT * (pad + T):(i + 1) * GT * (pad + T)].rearrange("p (k t) -> p k t", k=GT)
                  for i in range(3)]
            m, m1, m2 = (pool.step(lambda e, i=i: e.memset(wb[i][:, :, 0:pad], 0.0)) for i in range(3))
            m = pool.step(lambda e: e.tensor_copy(wb[0][:, :, pad:], p[:, 0:2, :]), m)
            icn = C("invcount").rearrange("p (k t) -> p k t", k=GT)
            pooled = p[:, 0:2, :]
            cur, takes = 0, []
            for i, w in enumerate((1, 2, 4, 8)):
                nxt = 1 + i % 2 if i < 2 else (1 if i == 2 else 2)
                src, dst = wb[cur], wb[nxt]
                m = TT(pool, dst[:, :, pad:], src[:, :, pad:], src[:, :, pad - w:pad - w + T], ALU.add, m, m1, m2, *takes)
                tile, half = i // 2, i % 2 * 64
                takes.append(TT(pool, pooled[half:half + 64, tile, :], dst[half:half + 64, tile, pad:],
                                icn[half:half + 64, tile, :], ALU.mult, m))
                cur = nxt
            m_win = TT(pool, pooled, pooled, wb[0][:, :, pad:], ALU.subtract, *takes)

            kp, bp, wi = (p[:, i:i + 2, :] for i in (20, 22, 24))
            sh = y[:, :, :]
            m1 = TT(dve, sh[:, :, 1:], rw[:, :, 0:T - 1], rw[:, :, 1:], ALU.subtract)
            m2 = TS(dve, sh[:, :, 0:1], rw[:, :, 0:1], -1.0, None, ALU.mult, None)
            for i in range(8):
                m3 = STT(rw[:, i, :], sh[:, i, :], V("rwkv_mu", i), rw[:, i, :], ALU.mult, ALU.add, m1, m2)
            next(tails)
            r, k, v = (rw[:, 2 * i:2 * i + 2, :] for i in range(3))
            lo_in = rw[:, 6, :]
            m4 = AC(lo_in[0:64, :], lo_in[0:64, :], ACT.Tanh, m3)
            m5 = AC(rw[:, 7, :], rw[:, 7, :], ACT.Sigmoid, m3)
            for i in range(GT):
                m6 = MM(bank[0][:, i * T:(i + 1) * T], lora[:, 0, i * P:(i + 1) * P], lo_in, True, True, m4)
                m7 = MM(bank[1][:, i * T:(i + 1) * T], lora[:, 1, i * P:(i + 1) * P], lo_in, True, True, m4)
                m8 = MM(bank[2][:, i * T:(i + 1) * T], g2[:, i * P:(i + 1) * P], rw[:, 7, :], True, True, m5)
            for i in range(GT):
                m6 = AC(cum[:, i, :], bank[0][:, i * T:(i + 1) * T], ACT.Sigmoid, m6, bias=V("rwkv_w0", i))
                m7 = AC(av[:, i, :], bank[1][:, i * T:(i + 1) * T], ACT.Sigmoid, m7, bias=V("rwkv_a0", i))
            md = TS(dve, gate[:, :, :], cum[:, :, :], -float(np.exp(-0.5)), None, ALU.mult, None, m6)
            for i in range(GT):
                mc = dve.step(lambda e, i=i: e.tensor_tensor_scan(cum[:, i, :], C("chunkkeep"), gate[:, i, :], 0.0,
                                                                  ALU.mult, ALU.add), md)
            next(tails)
            m_g = AC(y[:, 4:6, :], bank[2][:, :].rearrange("p (k t) -> p k t", k=2), ACT.Copy, m8, m3)
            for i in range(GT):
                m1 = TS(dve, bb[:, i, :], k[:, i, :], V("rwkv_k_k", i), None, ALU.mult, None, m3)
            m1 = AC(tmp[:, :, :], bb[:, :, :], ACT.Square, m1)
            for i in range(GT):
                m2 = MM(bank[6][:, i * T:(i + 1) * T], C("headsum"), tmp[:, i, :], True, True, m1)
            m2 = AC(rstd[:, :, :], bank[6][:, :].rearrange("p (k t) -> p k t", k=2), ACT.Sqrt, m2)
            m2 = TS(dve, rstd[:, :, :], rstd[:, :, :], 1e-12, None, ALU.max, None, m2)
            m2 = dve.step(lambda e: e.reciprocal(rstd[:, :, :], rstd[:, :, :]), m2)
            mkk = TT(dve, bb[:, :, :], bb[:, :, :], rstd[:, :, :], ALU.mult, m2)
            m1 = TS(dve, tmp[:, :, :], av[:, :, :], -1.0, None, ALU.add, None, m7, m2)
            for i in range(GT):
                m2 = TS(dve, tmp[:, i, :], tmp[:, i, :], V("rwkv_k_a", i), 1.0, ALU.mult, ALU.add, m1)
            mk = TT(dve, k, k, tmp[:, :, :], ALU.mult, m2)
            assert next(tails, None) is None
            dve.wait(lent["end"])
            m1 = TT(dve, wi[:, :, :], cum[:, :, :], gate[:, :, :], ALU.subtract, mc)
            m1 = AC(wi[:, :, :], wi[:, :, :], ACT.Exp, m1)
            for hh in range(2):
                hs = slice(hh * HD, (hh + 1) * HD)
                mq1 = TT(dve, qr[hs, :, 0, hh, :], bb[hs, :, :], wi[hs, :, :], ALU.mult, m1, mkk, mz_)
            kkd = y[:, 6:8, :]
            mkd = TT(dve, kkd, bb[:, :, :], wi[:, :, :], ALU.mult, m1, mkk)
            mb = TT(dve, bb[:, :, :], bb[:, :, :], av[:, :, :], ALU.mult, mkd)
            m2 = AC(wi[:, :, :], cum[:, :, :], ACT.Exp, mkd)
            for hh in range(2):
                hs = slice(hh * HD, (hh + 1) * HD)
                mq2 = TT(dve, qr[hs, :, 1, hh, :], r[hs], wi[hs, :, :], ALU.mult, m2)
            m3_ = AC(av[:, :, :], cum[:, :, :], ACT.Exp, mb, mc, scale=-1.0)
            mkp = TT(dve, kp[:, :, :], k, av[:, :, :], ALU.mult, m3_, mk)
            mbp = TT(dve, bp[:, :, :], bb[:, :, :], av[:, :, :], ALU.mult, m3_)
            c4 = cum[:, :, :].rearrange("p k (c t) -> p (k c) t", t=RCHUNK)
            g4 = gate[:, :, :].rearrange("p k (c t) -> p (k c) t", t=RCHUNK)
            end = c4[:, :, RCHUNK - 1:RCHUNK].broadcast_to([P, GT * NCH, RCHUNK])
            m1 = TT(dve, g4, end, c4, ALU.subtract, mc, mq1)
            m1 = AC(gate[:, :, :], gate[:, :, :], ACT.Exp, m1)
            kc, bc = y[:, 0:2, :], y[:, 2:4, :]
            mkc = TT(dve, kc, k, gate[:, :, :], ALU.mult, m1, mk)
            mbc = TT(dve, bc, bb[:, :, :], gate[:, :, :], ALU.mult, m1, mb)
            m1 = TT(dve, tmp[:, :, :], r, k, ALU.mult, mk)
            for i in range(GT):
                m2 = TS(dve, tmp[:, i, :], tmp[:, i, :], V("rwkv_r_k", i), None, ALU.mult, None, m1)
            for i in range(GT):
                m3_ = MM(bank[6][:, i * T:(i + 1) * T], C("headsum"), tmp[:, i, :], True, True, m2)
            m_bonus = TT(dve, r, bank[6][:, :].rearrange("p (k t) -> p k t", k=2), v, ALU.mult, m3_, mq2)

            kkt, kct, bct = (p[:, i:i + 2, :] for i in (4, 6, 8))
            mt = [to_tokens(kkd, kkt[:, :, :], 3, mkd),
                  to_tokens(kc, kct[:, :, :], 4, mkc),
                  to_tokens(bc, bct[:, :, :], 5, mbc),
                  to_tokens(v, tok[:, :, :], 6, m3, m_bonus)]
            meet()
            flat = lambda z: z.rearrange("p k t -> p (k t)").rearrange("p (n t) -> p n t", t=P)
            spare = env["ada_raw"][:, :, :].rearrange("p k n -> p (k n)").rearrange("p (i n t) -> p i n t", n=4, t=P)
            own = [sb(f"own{i}", [P, 4, P], ctx=c3)[:, :, :] for i in range(3)]
            sets = [[spare[:, i] for i in range(6)] + own,
                    [flat(z[:, :, :]) for z in (cum, av, bb, env["sil"], env["h"], env["sq"], rstd,
                                                y[:, 0:2, :], y[:, 2:4, :])]]
            oo = sb("oo", [P, GT, T], ctx=c3)
            small = [[rw[:, i, :].rearrange("p (c v) -> p c v", v=HD) for i in (2 + ti, 4 + ti, 6 + ti)]
                     for ti in range(GT)]
            probs = [(hh, blk) for hh in range(2) for blk in range(NB)]
            outs = {}

            def bc(z, n):
                return z.rearrange("p (n t) -> p n t", n=1).broadcast_to([P, n, P])

            def tile_stages(ti):
                akt, art, abt, arbt, ab, inv, invt, xx, yy = sets[ti]
                st, mc_, qq = small[ti]
                qq = qq[:, :, :].rearrange("p c t -> p (c t)")
                ba, bb_, bc_ = bank[3 * ti:3 * ti + 3]
                n4 = lambda b: b[:, :].rearrange("p (n t) -> p n t", n=4)
                hs = lambda hh: slice(hh * HD, (hh + 1) * HD)
                tc = lambda hh: slice(ti * P + hh * HD, ti * P + (hh + 1) * HD)
                free = [None] * 3
                for blk in range(NB):
                    ts = slice(blk * P, (blk + 1) * P)
                    rhs = qr[:, ti, :, :, ts].rearrange("p a h t -> p (a h) t")
                    m1 = MM(ba[:, :], kp[:, ti, ts], rhs, True, True, free[0])
                    m2 = MM(bb_[:, :], bp[:, ti, ts], rhs, True, True, free[1])
                    for hh in range(2):
                        m3 = MM(bc_[:, hh * P:(hh + 1) * P], qr[:, ti, 0, hh, ts], bp[:, ti, ts], True, True, free[2])
                    of = lambda z: z[:, blk:4:NB, :]
                    m_akt = TT(dve, of(akt), n4(ba)[:, 0:2], bc(C("before"), 2), ALU.mult, m1)
                    m_abt = TT(dve, of(abt), n4(bb_)[:, 0:2], bc(C("before"), 2), ALU.mult, m2)
                    m_ab = TT(dve, of(ab), n4(bc_)[:, 0:2], bc(C("after"), 2), ALU.mult, m3)
                    f0 = TT(dve, of(art), n4(ba)[:, 2:4], bc(C("upto"), 2), ALU.mult, m1)
                    f1 = TT(dve, of(arbt), n4(bb_)[:, 2:4], bc(C("upto"), 2), ALU.mult, m2)
                    free = [f0, f1, m_ab]
                    yield
                for n, (hh, blk) in enumerate(probs):
                    mz = MM(bank[6][:, (ti * 4 + n) * HD:(ti * 4 + n + 1) * HD], akt[:, n, :], tok[:, blk, tc(hh)],
                            True, True, m_akt, outs.get("z"))
                m1 = TT(pool, xx, ab, bc(C("levelT1"), 4), ALU.mult, m_ab)
                m1 = TT(dve, inv, bc(ident, 4), xx, ALU.subtract, m1)
                m2 = TT(pool, yy, abt, bc(C("level1"), 4), ALU.mult, m_abt)
                m_it = TT(dve, invt, bc(ident, 4), yy, ALU.subtract, m2)
                m_i = m1
                ml = TT(pool, akt, abt, bc(C("level2"), 4), ALU.mult, m_abt, mz)
                for n, (hh, blk) in enumerate(probs):
                    mr1 = act.step(lambda e, n=n, blk=blk, hh=hh: e.activation(yy[:, n, 0:HD], kkt[:, blk, tc(hh)],
                                                                             ACT.Copy), m_it)
                zs = bank[6][:, ti * T:(ti + 1) * T].rearrange("p (n v) -> p n v", v=HD)
                mr = act.step(lambda e: e.activation(yy[:, :, HD:P], zs, ACT.Copy), mz, m_it)
                outs["z"] = mr
                yield
                for w in (2, 4, 8, 16, 32):
                    for n in range(4):
                        mx = MM(ba[:, n * P:(n + 1) * P], akt[:, n, :], inv[:, n, :], True, True, ml, m_i, *free)
                    if w < 32:
                        ml = TT(pool, akt, abt, bc(C(f"level{2 * w}"), 4), ALU.mult, mx)
                    mx = AC(xx, n4(ba), ACT.Copy, mx, m_it, m_i)
                    yield
                    for n in range(4):
                        mb_ = MM(bc_[:, n * P:(n + 1) * P], xx[:, n, :], invt[:, n, :], True, True, mx, m_it)
                    if w < 32:
                        for n in range(4):
                            ma = MM(bb_[:, n * P:(n + 1) * P], invt[:, n, :], xx[:, n, :], True, True)
                        m_i = TT(dve, inv, inv, n4(bb_), ALU.subtract, ma)
                    m_it = TT(dve, invt, invt, n4(bc_), ALU.subtract, mb_, m_i)
                    yield
                for n in range(4):
                    my = MM(ba[:, n * P:(n + 1) * P], invt[:, n, :], yy[:, n, :], True, True, mr, mr1, m_it)
                my = TS(dve, yy, n4(ba), -1.0, None, ALU.mult, None, my)
                yield
                for n, (hh, blk) in enumerate(probs):
                    ts = slice(blk * P, (blk + 1) * P)
                    mq_ = MM(bb_[hs(hh), ts], yy[:, n, 0:HD], arbt[:, n, :], True, True, my)
                    MM(bc_[hs(hh), ts], yy[:, n, HD:P], arbt[:, n, :], True, False)
                    mo_ = MM(bc_[hs(hh), ts], tok[:, blk, tc(hh)], art[:, n, :], False, True)
                for hh in range(2):
                    mqq = TT(dve, qq[hs(hh)], bb_[hs(hh), 0:T], qr[hs(hh), ti, 1, hh, :], ALU.add, mq_)
                mo_ = AC(oo[:, ti, :], bc_[:, 0:T], ACT.Copy, mo_)
                for c in (0, 2, 1):
                    if c == 1:
                        pe.wait(m2)
                    for hh in range(2):
                        blk, rs = c // 2, slice(c % 2 * 64, c % 2 * 64 + 64)
                        n = hh * NB + blk
                        o1 = ba[hs(hh), c * HD:(c + 1) * HD]
                        o2 = ba[hs(hh), (NCH + c) * HD:(NCH + c + 1) * HD]
                        MM(o1, yy[rs, n, 0:HD], bct[rs, blk, tc(hh)], True, True, my)
                        MM(o2, kct[rs, blk, tc(hh)], tok[rs, blk, tc(hh)], True, False)
                        m2 = MM(o2, bct[rs, blk, tc(hh)], yy[rs, n, HD:P], False, True)
                yield
                for c in range(NCH - 1):
                    for hh in range(2):
                        e0 = c * RCHUNK + RCHUNK - 1
                        m3_ = STT(mc_[hs(hh), c, :], ident[hs(hh), hh * HD:(hh + 1) * HD],
                                  wi[hs(hh), ti, e0:e0 + 1], ba[hs(hh), c * HD:(c + 1) * HD],
                                  ALU.mult, ALU.add, m2)
                ms_ = dve.step(lambda e: e.tensor_copy(
                    st[:, 1:, :], ba[:, NCH * HD:(2 * NCH - 1) * HD].rearrange("p (c v) -> p c v", v=HD)), m2)
                yield
                for c in (1, 2):
                    for hh in range(2):
                        mm_ = MM(ba[hs(hh), c * HD:(c + 1) * HD], mc_[hs(hh), c, :], st[hs(hh), c, :],
                                 True, True, ms_, m3_)
                    ms_ = TT(dve, st[:, c + 1, :], ba[:, c * HD:(c + 1) * HD], st[:, c + 1, :], ALU.add, mm_)
                    yield
                for c in range(1, NCH):
                    for hh in range(2):
                        mm_ = MM(bb_[hs(hh), c * RCHUNK:(c + 1) * RCHUNK], st[hs(hh), c, :],
                                 qq[hs(hh), c * RCHUNK:(c + 1) * RCHUNK], True, True, ms_, mqq)
                outs[ti] = TT(dve, oo[:, ti, RCHUNK:], bb_[:, RCHUNK:T], oo[:, ti, RCHUNK:], ALU.add, mo_, mm_)

            for _ in zip_longest(tile_stages(0), tile_stages(1)):
                pass
            assert len(outs) == 3
            meet()

            for i in range(GT):
                m = MM(bank[1][:, i * T:(i + 1) * T], wp[:, i, :], p[:, i, :], True, True, m_win)
            for i in range(GT):
                m = TS(dve, p[:, i, :], bank[1][:, i * T:(i + 1) * T], V("pool_b", i), V("pool_scale", i),
                       ALU.add, ALU.mult, m)
            for i in range(GT):
                m1 = MM(bank[0][:, i * T:(i + 1) * T], C("headsum"), oo[:, i, :], True, True)
            m1 = STT(oo[:, :, :], bank[0][:, :].rearrange("p (k t) -> p k t", k=2), -1.0 / HD, oo[:, :, :],
                     ALU.mult, ALU.add, m1)
            mr = head_rstd(rstd[:, :, :], oo[:, :, :], tmp[:, :, :], 6, 1.0 / HD, GN_EPS, m1)
            for i in range(GT):
                m1 = STT(oo[:, i, :], oo[:, i, :], V("rwkv_ln_w", i), rstd[:, i, :], ALU.mult, ALU.mult, mr)
                m1 = STT(oo[:, i, :], oo[:, i, :], V("rwkv_ln_b", i), r[:, i, :], ALU.add, ALU.add, m1)
                m_rwkv = TT(dve, r[:, i, :], oo[:, i, :], y[:, 4 + i, :], ALU.mult, m1)
            meet()

        env["sp"].wait(m_gat, m_win)
        for j, t0 in enumerate((0, 2, 10, 18)):
            m = dve.step(lambda e, j=j, t0=t0: e.tensor_copy(y[:, 2 * j:2 * j + 2, :], p[:, t0:t0 + 2, :]))
        m = env["split_xn"](m)
        m = linear([(w, "channels") for w in env["chunks"]["w_out"]], env["add_chunks"](None), m, env["first"]["ffn2"])
        meet()
    return [z for z in m for _ in range(2)]


def backwards(ap):
    step, n = ap.ap[-1]
    return bass.AP(tensor=ap.tensor, offset=ap.offset + step * (n - 1), ap=[*ap.ap[:-1], [-step, n]])


def attend(env, ctx, tag, scores, values, scale, bias, m_ready, order=None):
    sb, bank, pe, act, dve, pool = (env[n] for n in ("sb", "bank", "pe", "act", "dve", "pool"))
    ident, y = env["ident"], env["xn"]
    s = [env["h"], env["sil"], sb(f"s2_{tag}", [P, NB, T], ctx=ctx)]
    pt = [env["rstd"], sb(f"pt_{tag}", [P, NB, T], ctx=ctx)]
    mx = sb(f"mx_{tag}", [P, AH, 4], ctx=ctx)
    m_exp, m_nrm, m_pv, m_tr, m_out = {}, {}, {}, {}, {}
    m_sread, m_tread = {}, {}

    def softmax(i):
        sb_, bk = s[i % 3], bank[i % 2]
        for q in range(NB):
            m = pe.step(lambda e, q=q: e.matmul(bk[:, q * T:(q + 1) * T], *scores(i, q), start=True, stop=True),
                        *m_ready, m_sread.get(i - 2))
        if bias is not None:
            for q in range(NB):
                m1 = dve.step(lambda e, q=q: e.tensor_tensor_reduce(
                    sb_[:, q, :], bk[:, q * T:(q + 1) * T], bias[:, q, i, :], 1.0, -3e38, ALU.add, ALU.max,
                    mx[:, i, q:q + 1]), m, m_tr.get(i - 3))
            src = sb_[:, :, :]
        else:
            src = bk[:, :].rearrange("p (q t) -> p q t", q=NB)
            m1 = dve.step(lambda e: e.reduce_max(mx[:, i, 0:2], src, AX_X), m)
        m1 = dve.step(lambda e: e.tensor_scalar(mx[:, i, 0:2], mx[:, i, 0:2], -scale, None, ALU.mult), m1)
        m_sread[i] = m1
        for q in range(NB):
            m2 = act.step(lambda e, q=q: e.activation(sb_[:, q, :], src[:, q, :], ACT.Exp, bias=mx[:, i, q:q + 1],
                                                      scale=scale, accum_out=mx[:, i, 2 + q:3 + q]),
                          m1, m_tr.get(i - 3))
        if bias is None:
            m_sread[i] = m2
        m3 = dve.step(lambda e: e.reciprocal(mx[:, i, 2:4], mx[:, i, 2:4]), m2)
        for q in range(NB):
            m3 = pool.step(lambda e, q=q: e.tensor_scalar(sb_[:, q, :], sb_[:, q, :], mx[:, i, 2 + q:3 + q], None,
                                                          ALU.mult), m3)
        m_nrm[i] = m3

    def transposed(i):
        bk = bank[2 + i % 2]
        for kb in range(NB):
            for q in range(NB):
                m = pe.step(lambda e, kb=kb, q=q: e.transpose(bk[:, kb * T + q * P:kb * T + (q + 1) * P],
                                                              s[i % 3][:, q, kb * P:(kb + 1) * P], ident),
                            m_nrm[i], m_tread.get(i - 2))
        m_tr[i] = m
        m_tread[i] = dve.step(lambda e: e.tensor_copy(pt[i % 2][:, :, :], bk[:, :].rearrange("p (k q) -> p k q", k=NB)),
                              m, m_pv.get(i - 2))

    def weigh(i):
        hp, bk = i % 2 * HD, bank[4 + i // 2 % 2]
        for kb in range(NB):
            m = pe.step(lambda e, kb=kb: e.matmul(bk[hp:hp + HD, 0:T], values(i, kb), pt[i % 2][:, kb, :],
                                                  start=kb == 0, stop=kb == NB - 1), m_tread[i], m_out.get(i // 2 - 2))
        m_pv[i] = m
        if i % 2:
            dst, src = y[:, i // 2, :], bk[:, 0:T]
            if order is not None:
                dst, src = order(dst), src.rearrange("p (r c) -> p r c", c=GRID)
            m_out[i // 2] = act.step(lambda e: e.activation(dst, src, ACT.Copy), m)

    for i in range(AH + 2):
        if i < AH:
            softmax(i)
        if 0 <= i - 1 < AH:
            transposed(i - 1)
        if 0 <= i - 2 < AH:
            weigh(i - 2)
    return [m_out[i] for i in range(AH // 2)]


def neighbourhood(env, gate, m_in):
    a, sb, bank, act, dve, pool = (env[n] for n in ("a", "sb", "bank", "act", "dve", "pool"))
    dma, meet, linear = (env[n] for n in ("dma", "meet", "linear"))
    assert ROWS <= WIN_H
    (_, _), (_, att) = shape_constants()
    with ExitStack() as ctx:
        marks = env["scratch_free"][0]
        q = sb("na_q", [P, 8, T], ctx=ctx)
        k = sb("na_k", [P, 8, T], ctx=ctx)
        v = sb("na_v", [P, NB, D], ctx=ctx)
        bias = sb("na_bias", [P, NB, AH, ROWS, GRID], ctx=ctx)
        win = sb("na_win", [P, GRID], ctx=ctx)
        rpb = a["rpb"]
        width = 2 * GRID - 1
        got = []
        for qr in range(ROWS):
            for kr in range(ROWS):
                src = bass.AP(tensor=rpb.tensor, offset=rpb.offset + (WIN_H - 1 + kr - qr) * width,
                              ap=[[1, GRID], [(2 * WIN_H - 1) * width, AH], [1, GRID]])
                got.append(dma(pool, bias[qr % 2 * GRID:(qr % 2 + 1) * GRID, qr // 2, :, kr, :], src,
                               f"bias{qr}{kr}", *marks))
        at = att["window"][0]
        got.append(dma(pool, win[:, :], a["att"][:, at:at + GRID], "window", *marks))
        for b in range(NB):
            for j in range(AH):
                m_b = pool.step(lambda e, b=b, j=j: e.tensor_tensor(
                    bias[:, b, j], bias[:, b, j],
                    win[:, :].rearrange("p (r c) -> p r c", r=1).broadcast_to([P, ROWS, GRID]), ALU.add), *got)

        def evac_qk(c, b, m):
            dst = (q if c < 4 else k)[:, 2 * (c % 4):2 * (c % 4) + 2, :]
            src = b[:, :].rearrange("p (k t) -> p k t", k=2)
            if c < 4:
                dst, src = backwards(dst.rearrange("p k (r c) -> p (k r) c", c=GRID)), \
                    src.rearrange("p k (r c) -> p (k r) c", c=GRID)
            return dve.step(lambda e: e.tensor_scalar(dst, src, QK_SCALE if c < 4 else 1.0, None, ALU.mult), m)

        def evac_v(c, b, m):
            dst = v[:, :, c * CW:(c + 1) * CW]
            return act.step(lambda e: e.activation(dst, b[:, :].rearrange("p (b n) -> p b n", b=NB), ACT.Copy), m)

        ch = env["chunks"]
        m1 = linear([(w, "channels") for w in ch["na_qk"]] + [(w, "tokens") for w in ch["na_v"]],
                    lambda c, b, m: evac_qk(c, b, m) if c < 8 else evac_v(c - 8, b, m), m_in, ch["na_o"][:2])
        meet()

        def scores(i, qb):
            hp = i % 2 * HD
            return q[hp:hp + HD, i // 2, qb * P:(qb + 1) * P], k[hp:hp + HD, i // 2, :]

        m = attend(env, ctx, "na", scores, lambda i, kb: v[:, kb, i * HD:(i + 1) * HD], 1.0,
                   bias[:, :, :, :, :].rearrange("p b h r c -> p b h (r c)"), [*m1, m_b],
                   lambda z: backwards(z.rearrange("p (r c) -> p r c", c=GRID)))
        m = env["split_xn"](m)
        m = linear([(w, "channels") for w in ch["na_o"]], env["add_chunks"](gate), m, env["first"]["ffn3"])
        meet()
    return [z for z in m for _ in range(2)]


def latent(env, gate, m_in):
    a, sb, bank, pe, act, dve, pool = (env[n] for n in ("a", "sb", "bank", "pe", "act", "dve", "pool"))
    dma, meet, linear, V, y = (env[n] for n in ("dma", "meet", "linear", "V", "xn"))
    square_sum, inv_root, rstd = (env[n] for n in ("square_sum", "inv_root", "rstd"))
    (_, _), (_, att) = shape_constants()
    with ExitStack() as ctx:
        marks = env["scratch_free"][0]
        tab = sb("tab", [P, sum(n for _, n in att.values())], ctx=ctx)
        wukv = sb("wukv", [P, AH * 2 * HD], ctx=ctx)
        v = sb("mla_v", [P, NB, D], ctx=ctx)
        lat = sb("lat", [P, 3, T], ctx=ctx)
        kr = sb("kr", [P, T], ctx=ctx)
        wuq = env["ada_raw"][:, :, :].rearrange("p k n -> p (k n)").rearrange("p (k n) -> p k n", k=2)

        def A(name, n=None, p0=0, p1=P):
            at, w = att[name]
            return tab[p0:p1, at:at + (n or w)]

        rp = slice(HD, QH)
        with ExitStack() as c1:
            wd = sb("wd", [P, KT, QL + P + ROPE], ctx=c1)
            gd = dma(pool, wd[:, :, :], a["mla_down"], "down", *marks)
            got = [dma(pool, tab[:, :], a["att"], "tab"), dma(pool, wukv[:, :], a["mla_ukv"], "ukv"),
                   dma(pool, wuq, a["mla_uq"], "uq", (env["s_ada"], ADA_UNITS + 1))]
            outs = [(bank[0][:, 0:T], 0, P), (bank[0][:, T:2 * T], P, P), (bank[1][:, 0:T], 2 * P, P),
                    (bank[2][0:ROPE, 0:T], 3 * P, ROPE)]
            for o, at, n in outs:
                for k_ in range(KT):
                    m = pe.step(lambda e, o=o, at=at, n=n, k_=k_: e.matmul(
                        o, wd[:, k_, at:at + n], y[:, k_, :], start=k_ == 0, stop=k_ == KT - 1), gd, m_in[-1])
            m1 = act.step(lambda e: e.activation(lat[:, 0:2, :], bank[0][:, :].rearrange("p (k t) -> p k t", k=2),
                                                 ACT.Copy), m)
            m2 = act.step(lambda e: e.activation(lat[:, 2, :], bank[1][:, 0:T], ACT.Copy), m)
            m3 = dve.step(lambda e: e.tensor_copy(kr[0:ROPE, :], bank[2][0:ROPE, 0:T]), m)
            meet()
        for l in (pe, dve, act, pool):
            l.wait(*got)
        ms = square_sum(lambda k_: lat[:, k_, :], 2, bank[3][:, 0:T], m1)
        mr = inv_root(rstd[:, 0, :], bank[3][:, 0:T], 1.0 / QL, EPS, ms)
        for i in range(2):
            m_cq = dve.step(lambda e, i=i: e.scalar_tensor_tensor(lat[:, i, :], lat[:, i, :], V("mla_q_norm_2", i),
                                                                  rstd[:, 0, :], ALU.mult, ALU.mult), mr)
        ms = square_sum(lambda k_: lat[:, 2, :], 1, bank[3][:, T:2 * T], m2, mr)
        mr = inv_root(rstd[:, 1, :], bank[3][:, T:2 * T], 1.0 / P, EPS, ms)
        m_ckv = dve.step(lambda e: e.scalar_tensor_tensor(lat[:, 2, :], lat[:, 2, :], V("mla_kv_norm_2"),
                                                          rstd[:, 1, :], ALU.mult, ALU.mult), mr)
        q = sb("mla_q", [P, AH, T], ctx=ctx)
        k = sb("mla_k", [P, AH, T], ctx=ctx)
        m_pad = [pool.step(lambda e, z=z: e.memset(z[QH:P, :, :], 0.0)) for z in (q, k)]
        pe.step(lambda e: e.matmul(bank[2][0:QH, 0:T], A("place", QH, 0, ROPE), kr[0:ROPE, :], start=True, stop=True), m3)
        m = pe.step(lambda e: e.matmul(bank[2][0:QH, T:2 * T], A("placeturn", QH, 0, ROPE), kr[0:ROPE, :],
                                       start=True, stop=True))
        m1 = dve.step(lambda e: e.tensor_tensor(kr[rp, :], bank[2][rp, 0:T], A("cos", None, HD, QH), ALU.mult), m)
        m2 = dve.step(lambda e: e.tensor_tensor(k[rp, 0, :], bank[2][rp, T:2 * T], A("sin", None, HD, QH), ALU.mult), m)
        m1 = dve.step(lambda e: e.tensor_tensor(kr[rp, :], kr[rp, :], k[rp, 0, :], ALU.add), m1, m2)
        m_krot = m1
        vcols = wukv[:, :].rearrange("p (h n) -> p h n", n=2 * HD)
        prev = []
        for b in range(NB):
            for hf in range(2):
                bk = bank[4 + hf]
                m = pe.step(lambda e, b=b, hf=hf, bk=bk: e.matmul(
                    bk[:, :], lat[:, 2, b * P:(b + 1) * P], vcols[:, 8 * hf:8 * hf + 8, HD:2 * HD],
                    start=True, stop=True), m_ckv, *prev)
                m_v = act.step(lambda e, b=b, hf=hf, bk=bk: e.activation(v[:, b, hf * 512:(hf + 1) * 512], bk[:, :],
                                                                         ACT.Copy), m)
                if hf:
                    prev = [m_v]
        mk_, mq_, mt_ = {}, {}, {}
        for l in (pe, act, dve):
            l.wait(m_v, m_krot, m_ckv, m_cq)
        pe.wait(*m_pad)
        for i in range(AH // 2):
            kb, qb, tb = bank[0 + i % 2], bank[2 + i % 2], bank[4 + i % 2]
            for j in range(2):
                hh = 2 * i + j
                m = pe.step(lambda e, hh=hh, j=j, kb=kb: e.matmul(
                    kb[0:HD, j * T:(j + 1) * T], vcols[:, hh, 0:HD], lat[:, 2, :], start=True, stop=True), mk_.get(i - 2))
            mk_[i] = act.step(lambda e, i=i, kb=kb: e.activation(
                k[0:HD, 2 * i:2 * i + 2, :], kb[0:HD, :].rearrange("p (h t) -> p h t", h=2), ACT.Copy), m)
            for j in range(2):
                hh = 2 * i + j
                for kt in range(2):
                    m = pe.step(lambda e, hh=hh, j=j, kt=kt, qb=qb: e.matmul(
                        qb[0:QH, j * T:(j + 1) * T], wuq[:, kt, hh * QH:(hh + 1) * QH], lat[:, kt, :],
                        start=kt == 0, stop=kt == 1), m_cq, mq_.get(i - 2))
            qs = q[:, 2 * i:2 * i + 2, :]
            mq_[i] = act.step(lambda e, qs=qs, qb=qb: e.activation(
                qs[0:QH], qb[0:QH, :].rearrange("p (h t) -> p h t", h=2), ACT.Copy), m)
            m = pe.step(lambda e, qs=qs, tb=tb: e.matmul(tb[0:QH, :], A("turn", QH), qs,
                                                         start=True, stop=True), mq_[i], mt_.get(i - 2))
            two = lambda z: z.rearrange("p (n t) -> p n t", n=1).broadcast_to([ROPE, 2, T])
            m_kr = pool.step(lambda e, i=i: e.tensor_copy(k[rp, 2 * i:2 * i + 2, :],
                                                          kr[rp, :].rearrange("p (n t) -> p n t", n=1)
                                                          .broadcast_to([ROPE, 2, T])), m_krot)
            m1 = pool.step(lambda e, qs=qs: e.tensor_tensor(qs[rp], qs[rp], two(A("cos", None, HD, QH)), ALU.mult), m)
            m2 = dve.step(lambda e, tb=tb, i=i: e.tensor_tensor(
                env["h"][rp, :, :], tb[rp, :].rearrange("p (h t) -> p h t", h=2), two(A("sin", None, HD, QH)),
                ALU.mult), m, mt_.get(i - 1))
            mt_[i] = dve.step(lambda e, qs=qs: e.tensor_tensor(qs[rp], qs[rp], env["h"][rp, :, :], ALU.add), m1, m2)
        meet()
        m = attend(env, ctx, "mla", lambda i, qb: (q[:, i, qb * P:(qb + 1) * P], k[:, i, :]),
                   lambda i, kb: v[:, kb, i * HD:(i + 1) * HD], float(QH) ** -0.5, None, [m_kr, m_v])
        m = env["split_xn"](m)
        m = linear([(w, "channels") for w in env["chunks"]["mla_o"]], env["add_chunks"](gate), m, env["first"]["moe"])
        meet()
    return [z for z in m for _ in range(2)]


def router(env, ctx, m_in):
    a, sb, bank, pe, act, dve, pool = (env[n] for n in ("a", "sb", "bank", "pe", "act", "dve", "pool"))
    dma, meet, C, ident, xn = (env[n] for n in ("dma", "meet", "C", "ident", "xn"))
    E = EXPERTS
    marks = env["scratch_free"][0]
    comb = sb("comb", [P, E, T], ctx=ctx)
    wr = sb("wr", [P, KT, E], ctx=ctx)
    pr = sb("pr", [P, NB, E], ctx=ctx)
    st = sb("rst", [P, NB], ctx=ctx)
    gt = sb("rgt", [P, NB, E, E], ctx=ctx)
    eq = sb("req", [P, NB, E, E], ctx=ctx)
    got = dma(pool, wr[:, :, :], a["router"], "router", *marks)
    for b in range(NB):
        for k in range(KT):
            m = pe.step(lambda e, b=b, k=k: e.matmul(bank[0][:, b * E:(b + 1) * E], xn[:, k, b * P:(b + 1) * P],
                                                     wr[:, k, :], start=k == 0, stop=k == KT - 1), got, m_in)
    m = dve.step(lambda e: e.tensor_copy(pr[:, :, :], bank[0][:, 0:NB * E].rearrange("p (b e) -> p b e", b=NB)), m)
    wide = lambda z: z.rearrange("p (b n) -> p b n", n=1).broadcast_to([P, NB, E])

    def TT(o, i0, i1, op, *after):
        return dve.step(lambda e: e.tensor_tensor(o, i0, i1, op), *after)

    m = dve.step(lambda e: e.reduce_max(st[:, :], pr[:, :, :], AX_X), m)
    m = TT(pr[:, :, :], pr[:, :, :], wide(st[:, :]), ALU.subtract, m)
    m = act.step(lambda e: e.activation(pr[:, :, :], pr[:, :, :], ACT.Exp), m)

    def normalise(m):
        m = dve.step(lambda e: e.reduce_sum(st[:, :], pr[:, :, :], AX_X), m)
        m = dve.step(lambda e: e.reciprocal(st[:, :], st[:, :]), m)
        return TT(pr[:, :, :], pr[:, :, :], wide(st[:, :]), ALU.mult, m)

    m = normalise(m)
    for b in range(NB):
        other = pr[:, b, :].rearrange("p (n j) -> p n j", n=1).broadcast_to([P, E, E])
        own = pr[:, b, :].rearrange("p (j n) -> p j n", n=1).broadcast_to([P, E, E])
        m1 = TT(gt[:, b], other, own, ALU.is_gt, m)
        m2 = TT(eq[:, b], other, own, ALU.is_equal, m)
        m2 = TT(eq[:, b], eq[:, b], C("earlier").rearrange("p (e j) -> p e j", e=E), ALU.mult, m2)
        m3 = TT(gt[:, b], gt[:, b], eq[:, b], ALU.add, m1, m2)
        m4 = dve.step(lambda e, b=b: e.reduce_sum(eq[:, b, 0, :], gt[:, b], AX_X), m3)
        m5 = dve.step(lambda e, b=b: e.tensor_scalar(eq[:, b, 0, :], eq[:, b, 0, :], 1.5, None, ALU.is_lt), m4)
        ml = TT(pr[:, b, :], pr[:, b, :], eq[:, b, 0, :], ALU.mult, m5)
    m = normalise(ml)
    for i in range(E):
        bk = bank[1 + i // 2 % 4]
        for b in range(NB):
            mm = pe.step(lambda e, i=i, b=b, bk=bk: e.matmul(
                bk[:, (i % 2) * T + b * P:(i % 2) * T + (b + 1) * P],
                pr[:, b, i:i + 1].broadcast_to([P, P]), ident, start=True, stop=True), m)
        if i % 2:
            mc = dve.step(lambda e, i=i, bk=bk: e.tensor_copy(
                comb[:, i - 1:i + 1, :], bk[:, :].rearrange("p (k t) -> p k t", k=2)), mm)
    pos = env["ada_raw"][:, :, :].rearrange("p k n -> p (k n)")[:, 0:E * T].rearrange("p (e t) -> p e t", e=E)
    taken, flag = sb("taken", [P, E, T], ctx=ctx), sb("flag", [1, 1], mybir.dt.int32, ctx=ctx)
    one = env["ones"][:, 0:1].broadcast_to([P, T])
    m1 = dve.step(lambda e: e.tensor_scalar(taken[:, :, :], comb[:, :, :], 0.0, None, ALU.is_gt), mc)
    for i in range(E):
        m1 = dve.step(lambda e, i=i: e.tensor_tensor_scan(pos[:, i, :], one, taken[:, i, :], 0.0,
                                                          ALU.mult, ALU.add), m1)
    m1 = dve.step(lambda e: e.reduce_max(st[:, 0:1], pos[:, :, T - 1], AX_X), m1)
    m1 = dve.step(lambda e: e.tensor_scalar(st[:, 1:2], st[:, 0:1], float(SLOTS), None, ALU.is_gt), m1)
    m_flag = dve.step(lambda e: e.tensor_copy(flag[:, :], st[0:1, 1:2]), m1)
    meet()
    return comb, pos, taken, flag, mc, m_flag


def dispatched(env, ctx, comb, pos, taken, mc, gate):
    a, sb, bank, pe, act, dve, sp = (env[n] for n in ("a", "sb", "bank", "pe", "act", "dve", "sp"))
    sem, ident, x, xn, C = (env[n] for n in ("sem", "ident", "x", "xn", "C"))
    raw, whi, wlo, s_raw, s_hi, s_lo, s_used = (env[n] for n in ("raw", "whi", "wlo", "s_raw", "s_hi",
                                                                 "s_lo", "s_used"))
    product, w = env["product"], a["moe"]
    sil, h, hhi, hlo = (env[n][:, 0, :] for n in ("sil", "h", "hhi", "hlo"))
    UNITS, PAIR, EU = EXPERTS * EXPERT_UNITS, 2 * EXPERT_UNITS, EXPERT_UNITS
    (A_, na, _), (B_, nb, _) = env["split_ahead"]
    env["split_ahead"].clear()
    C_ = env["turn"][0]
    b0 = {A_: na, B_: nb, C_: env["uses"][C_]}
    xt = sb("xtok", [P, NB, D], ctx=ctx)
    pick = sb("pick", [P, NB, EXPERTS, SLOTS], ctx=ctx)
    xg = [[sb(f"slots_{n}{i}", [P, KT, SLOTS], F32R, ctx=ctx) for n in ("hi", "lo")] for i in range(2)]
    ysl = sb("yslots", [P, D], ctx=ctx)
    flat = lambda z: z.rearrange("p k t -> p (k t)")
    raw2 = {A_: flat(taken[:, :, :]), B_: flat(xn[:, :, :]),
            C_: flat(env["ada_raw"][:, :, :])[:, 0:CHUNK]}
    s_raw2 = {s: sem(f"raw2_landed{s}") for s in range(3)}
    n_silu, n_mult, n_ht, n_hhi, n_hlo = (sem("moe_" + n) for n in ("silu", "mult", "turned", "high", "low"))
    n_gath, n_xhi, n_xlo, n_y, n_scat, n_add = (
        sem("moe_" + n) for n in ("gathered", "slots_high", "slots_low", "outcome", "scattered", "added"))
    act.plain(lambda e: e.sem_inc(n_y, 1))
    dve.plain(lambda e: e.sem_inc(n_add, 1))
    ACC, GATE, UP, HT = bank[0:2], bank[2], bank[3], bank[4]
    SC = (bank[5], bank[6], bank[7], bank[0])

    m_s = dve.step(lambda e: e.scalar_tensor_tensor(comb[:, :, :], pos, C("slot"), comb[:, :, :],
                                                    ALU.is_equal, ALU.mult), mc)
    m_x = []
    for b in range(NB):
        for q in range(2):
            bk = bank[2 * b + q]
            for k in range(4):
                m = pe.step(lambda e, b=b, k=4 * q + k, kk=k, bk=bk: e.transpose(
                    bk[:, kk * P:(kk + 1) * P], xn[:, k, b * P:(b + 1) * P], ident))
            m_x.append(act.step(lambda e, b=b, q=q, bk=bk: e.activation(
                xt[:, b, q * 512:(q + 1) * 512], bk[:, :], ACT.Copy), m))
    for b in range(NB):
        for q in range(2):
            bk = bank[4 + 2 * b + q]
            for k in range(4):
                m = pe.step(lambda e, b=b, k=4 * q + k, kk=k, bk=bk: e.transpose(
                    bk[:, kk * P:(kk + 1) * P], comb[:, k, b * P:(b + 1) * P], ident), m_s)
            m_p = dve.step(lambda e, b=b, q=q, bk=bk: e.tensor_scalar(
                pick[:, b, 4 * q:4 * q + 4, :], bk[:, :].rearrange("p (e t) -> p e t", e=4), 0.0, None,
                ALU.is_gt), m)
    pe.wait(*m_x, m_p)

    def load(e, s, n, second, kind):
        e.wait_ge(s_lo[s], b0[s] + n)
        if second:
            e.dma_start(raw2[s], w[n, kind]).then_inc(s_raw2[s], 16)
        else:
            e.dma_start(raw[s][:, :], w[n, kind]).then_inc(s_raw[s], 16)

    def high(e, s, n, second, nth):
        if second:
            e.wait_ge(s_raw2[s], 16 * nth + 16)
        else:
            e.wait_ge(s_raw[s], 16 * (b0[s] + nth) + 16)
        e.wait_ge(s_used[s], b0[s] + n + 1)
        e.activation(whi[s][:, :], raw2[s] if second else raw[s][:, :], ACT.Copy).then_inc(s_hi[s], 1)

    def low(e, s, n, second):
        e.wait_ge(s_hi[s], b0[s] + n + 2)
        e.tensor_tensor(wlo[s][:, :], raw2[s] if second else raw[s][:, :], whi[s][:, :],
                        ALU.subtract).then_inc(s_lo[s], 1)

    def p_half(e, j, s, dst, which, ks):
        hi, lo = xg[which]
        for k in ks:
            cols = slice(k * CW, (k + 1) * CW)
            l = product(e, dst[:, 0:CW], (hi[:, k, :], lo[:, k, :]), (whi[s][:, cols], wlo[s][:, cols]),
                        k == 0, k == KT - 1)
        if k == KT - 1:
            l.then_inc(s_used[s], 1)

    def p_gate(e, j, which):
        e.wait_ge(s_lo[A_], b0[A_] + j + 2)
        p_half(e, j, A_, GATE, which, range(KT))

    def p_up(e, j, which):
        e.wait_ge(s_lo[B_], b0[B_] + j + 2)
        p_half(e, j, B_, UP, which, range(KT))

    def p_turn(e, j):
        e.wait_ge(n_mult, j + 1)
        for i in range(2):
            l = e.transpose(HT[:, i * P:(i + 1) * P], h[:, i * P:(i + 1) * P], ident)
        l.then_inc(n_ht, 1)

    def p_down(e, j, first, last):
        e.wait_ge(s_lo[C_], b0[C_] + j + 2)
        e.wait_ge(n_hlo, j + 1)
        for k in range(2):
            parts = (hhi[:, k * P:(k + 1) * P], hlo[:, k * P:(k + 1) * P])
            for half in range(2):
                cols = slice(k * D + half * 512, k * D + (half + 1) * 512)
                l = product(e, ACC[half][:, :], parts, (whi[C_][:, cols], wlo[C_][:, cols]),
                            first and k == 0, last and k == 1)
        l.then_inc(s_used[C_], 1)

    def p_gather(e, ex, q):
        for kk in range(4):
            k = 4 * q + kk
            for b in range(NB):
                l = e.matmul(bank[5 + q][:, kk * P:(kk + 1) * P], xt[:, b, k * P:(k + 1) * P],
                             pick[:, b, bass.ds(ex, 1), :].rearrange("p e t -> p (e t)"),
                             start=b == 0, stop=b == NB - 1)
        l.then_inc(n_gath, 1)

    def p_scatter(e, ex):
        e.wait_ge(n_y, ex + 2)
        e.wait_ge(n_add, 4 * ex + 1)
        for b in range(4):
            for i in range(2):
                k = 2 * b + i
                l = e.matmul(SC[b][:, i * T:(i + 1) * T], ysl[:, k * P:(k + 1) * P],
                             comb[:, bass.ds(ex, 1), :].rearrange("p e t -> p (e t)"), start=True, stop=True)
            l.then_inc(n_scat, 1)

    def a_silu(e, j):
        e.wait_ge(s_used[A_], b0[A_] + j + 2)
        e.activation(sil, GATE[:, 0:CW], ACT.Silu).then_inc(n_silu, 1)

    def a_hhi(e, j):
        e.wait_ge(n_ht, j + 1)
        e.activation(hhi, HT[:, 0:2 * P], ACT.Copy).then_inc(n_hhi, 1)

    def a_slots(e, q, g, which):
        e.wait_ge(n_gath, g + 1)
        e.activation(xg[which][0][:, 4 * q:4 * q + 4, :], bank[5 + q][:, :].rearrange("p (k t) -> p k t", k=4),
                     ACT.Copy).then_inc(n_xhi, 1)

    def a_outcome(e, j):
        e.wait_ge(s_used[C_], b0[C_] + j + 2)
        for half in range(2):
            l = e.activation(ysl[:, half * 512:(half + 1) * 512], ACC[half][:, :], ACT.Copy)
        l.then_inc(n_y, 1)

    def v_mult(e, j):
        e.wait_ge(s_used[B_], b0[B_] + j + 2)
        e.wait_ge(n_silu, j + 1)
        e.tensor_tensor(h, sil, UP[:, 0:CW], ALU.mult).then_inc(n_mult, 1)

    def v_hlo(e, j):
        e.wait_ge(n_hhi, j + 1)
        e.tensor_tensor(hlo, HT[:, 0:2 * P], hhi, ALU.subtract).then_inc(n_hlo, 1)

    def v_slots(e, q, g, which):
        e.wait_ge(n_xhi, g + 1)
        e.tensor_tensor(xg[which][1][:, 4 * q:4 * q + 4, :], bank[5 + q][:, :].rearrange("p (k t) -> p k t", k=4),
                        xg[which][0][:, 4 * q:4 * q + 4, :], ALU.subtract).then_inc(n_xlo, 1)

    def v_add(e, ex):
        e.wait_ge(n_add, 4 * ex + 1)
        for b in range(4):
            e.wait_ge(n_scat, 4 * ex + b + 1)
            for i in range(2):
                k = 2 * b + i
                l = e.scalar_tensor_tensor(x[:, k, :], SC[b][:, i * T:(i + 1) * T], gate(k), x[:, k, :],
                                           ALU.mult, ALU.add)
            l.then_inc(n_add, 1)

    def steps(pp, which):
        for i in which:
            j = PAIR * pp + i
            if isinstance(j, int) and j >= UNITS:
                return
            u, ex = i % EU, 2 * pp + i // EU
            yield i, j, i // EU % 2, u, ex, lambda n, j=j: not isinstance(j, int) or j + n < UNITS

    GATHER = (2, 3)
    begins = lambda i, u: u == 0 and i > 0

    def sp_steps(e, pp, which):
        for i, j, half, u, ex, more in steps(pp, which):
            for s, ahead_by, second, kind in ((C_, 2, i % 2, 2), (A_, 4, 1 - i % 2, 0), (B_, 4, 1 - i % 2, 1)):
                if more(ahead_by):
                    load(e, s, j + ahead_by, second, kind)

    def act_steps(e, pp, which):
        for i, j, half, u, ex, more in steps(pp, which):
            if begins(i, u):
                a_outcome(e, j - 1)
            high(e, C_, j, i % 2, EU * pp + i // 2)
            if more(1):
                e.wait_ge(n_mult, j + 1)
                a_silu(e, j + 1)
            a_hhi(e, j)
            if u in GATHER and more(EU):
                a_slots(e, u - 2, 2 * ex + u, 1 - half)
            for s in (A_, B_):
                if more(2):
                    high(e, s, j + 2, 1 - i % 2, EU * pp + (i + 1) // 2 + i % 2)

    def dve_steps(e, pp, which):
        for i, j, half, u, ex, more in steps(pp, which):
            low(e, C_, j, i % 2)
            v_hlo(e, j)
            if u in GATHER and more(EU):
                v_slots(e, u - 2, 2 * ex + u, 1 - half)
            if more(2):
                low(e, A_, j + 2, 1 - i % 2)
            if begins(i, u):
                v_add(e, ex - 1)
            if more(1):
                v_mult(e, j + 1)
            if more(2):
                low(e, B_, j + 2, 1 - i % 2)

    def pe_steps(e, pp, which):
        for i, j, half, u, ex, more in steps(pp, which):
            end = u == EU - 1
            own = 1 - half if end else half
            if u in GATHER and more(EU):
                p_gather(e, ex + 1, u - 2)
            if more(1):
                if end:
                    e.wait_ge(n_xlo, 2 * ex + 4)
                e.wait_ge(n_silu, j + 1)
                p_gate(e, j + 1, own)
            p_turn(e, j)
            if begins(i, u):
                p_scatter(e, ex - 1)
            if more(1):
                p_up(e, j + 1, own)
            if begins(i, u):
                e.wait_ge(n_add, 4 * ex + 1)
            p_down(e, j, u == 0, end)

    sp.wait(m_x[-1], m_s, *env["scratch_free"][0])
    for s, n, second, kind in ((C_, 1, 1, 2), (A_, 2, 1, 0), (B_, 2, 1, 1), (A_, 3, 0, 0), (B_, 3, 0, 1)):
        sp.plain(lambda e, s=s, n=n, second=second, kind=kind: load(e, s, n, second, kind))
    for q in range(2):
        pe.plain(lambda e, q=q: p_gather(e, 0, q))
        act.plain(lambda e, q=q: a_slots(e, q, q, 0))
        dve.plain(lambda e, q=q: v_slots(e, q, q, 0))
    pe.plain(lambda e: e.wait_ge(n_xlo, 2))
    pe.plain(lambda e: p_gate(e, 0, 0))
    pe.plain(lambda e: p_up(e, 0, 0))
    act.plain(lambda e: a_silu(e, 0))
    act.plain(lambda e: high(e, A_, 1, 0, 1))
    dve.plain(lambda e: low(e, A_, 1, 0))
    dve.plain(lambda e: v_mult(e, 0))
    act.plain(lambda e: high(e, B_, 1, 0, 1))
    dve.plain(lambda e: low(e, B_, 1, 0))
    for lane, body in ((sp, sp_steps), (act, act_steps), (dve, dve_steps), (pe, pe_steps)):
        lane.plain(lambda e, body=body: body(e, 0, (0,)))
        lane.loop(0, EXPERTS // 2 - 1, lambda e, pp, body=body: body(e, pp, range(1, PAIR + 1)))
        lane.plain(lambda e, body=body: body(e, EXPERTS // 2 - 1, range(1, PAIR)))
    act.plain(lambda e: a_outcome(e, UNITS - 1))
    pe.plain(lambda e: p_scatter(e, EXPERTS - 1))
    dve.plain(lambda e: v_add(e, EXPERTS - 1))
    return [(n_add, 4 * (EXPERTS - 1) + 2 + k // 2) for k in range(KT)]


def column_chunks(w):
    return w.reshape(KT, P, -1, CW).transpose(2, 1, 0, 3).reshape(-1, P, CHUNK)


def ffn_chunks(w_in, w_out):
    f = w_out.shape[0]
    down = w_out.reshape(f // CW, 2, P, D).transpose(0, 2, 1, 3).reshape(-1, P, CHUNK)
    return np.stack([column_chunks(w_in[:, :f]), column_chunks(w_in[:, f:]), down], axis=1)


def layout(inp):
    g = {k: np.asarray(v) for k, v in inp.items()}
    (main, _), (att, _) = shape_constants()
    tiles = lambda w: w.reshape(-1, P, w.shape[-1]).transpose(1, 0, 2)
    vec = np.concatenate([g[n].reshape(-1, P).T for n, _ in VECTORS], axis=1)
    w_in = g["w_in"][0]
    qkv = g["na_w_qkv_2"][0]
    ada = g["w_ada_2"].reshape(2, KT, P, 6 * D // ADA_W, ADA_W).transpose(0, 3, 2, 1, 4)
    moe_in, moe_out = g["moe_w_gu_2"][0], g["moe_w_down_2"][0]
    return {
        "x": tiles(g["x"][0].T), "vec": vec, "cst": main, "att": att,
        "ffn1": ffn_chunks(g["ffn1_w_in"][0], g["ffn1_w_out"][0]),
        "ffn2": ffn_chunks(g["ffn2_w_in"][0], g["ffn2_w_out"][0]),
        "ffn3": ffn_chunks(g["ffn_w_gu_2"][0], g["ffn_w_down_2"][0]),
        "moe": np.concatenate([ffn_chunks(moe_in[e], moe_out[e]) for e in range(EXPERTS)]),
        "ada": ada.reshape(ADA_UNITS, P, KT, ADA_W),
        "w_in": column_chunks(w_in[:, :MIX_TILES * P]), "w_in_ga": tiles(w_in[:, MIX_TILES * P:]),
        "w_out": column_chunks(g["w_out"][0]),
        "rwkv_w2": g["rwkv_w2"][0], "rwkv_a2": g["rwkv_a2"][0], "rwkv_g2": g["rwkv_g2"][0],
        "gla_w2": g["gla_w2"][0], "pool_w": g["pool_w"][0],
        "na_qk": column_chunks(qkv[:, :2 * D]), "na_v": column_chunks(qkv[:, 2 * D:]),
        "na_o": column_chunks(g["na_w_o_2"][0]),
        "rpb": np.pad(g["na_rpb_2"][0], ((0, 0), (0, 0), (GRID - WIN_W, GRID - WIN_W))),
        "mla_down": tiles(g["mla_w_down_2"][0]), "mla_uq": tiles(g["mla_w_uq_2"][0]),
        "mla_ukv": g["mla_w_ukv_2"][0], "mla_o": column_chunks(g["mla_w_o_2"][0]),
        "router": tiles(g["moe_w_router_2"][0]),
    }


def kernel(**inputs):
    import concourse.bacc as bacc
    from concourse.bass_utils import run_bass_kernel_spmd

    nc = bacc.Bacc("TRN2", target_bir_lowering=False, num_devices=1)
    arrays = {"in_" + k: np.ascontiguousarray(v) for k, v in layout(inputs).items()}
    aps = {k[3:]: nc.dram_tensor(k, v.shape, mybir.dt.from_np(v.dtype), kind="ExternalInput").ap()
           for k, v in arrays.items()}
    out = nc.dram_tensor("out", (P, KT, T), F32, kind="ExternalOutput").ap()
    build_program(nc, aps, out)
    r = run_bass_kernel_spmd(nc, [arrays], core_ids=[0])
    got = r.results[0]["out"]
    return np.ascontiguousarray(got.transpose(2, 1, 0).reshape(1, T, D))
```
